# Optimizing a Trainium2 kernel written in Bass

```python
import jax, jax.numpy as jnp
from jax import lax
import numpy as np

D_MODEL = 1024
BATCH = 1
SEQ = 256
DEPTH = 1

SB_HEADS = 8
SB_HEAD_DIM = 64
SB_WIDTH = SB_HEADS * SB_HEAD_DIM
SB_BLOCK = 128

GLA_HEADS = 4
GLA_DK = 64
GLA_DV = 128
GLA_KW = GLA_HEADS * GLA_DK
GLA_VW = GLA_HEADS * GLA_DV
GLA_RANK = 16
GLA_TAU = 16.0
GLA_CHUNK = 64

D_FF = 2816
CONV_WIDTH = 3

EPS = 1e-6

IN_SIZES = (SB_WIDTH, SB_WIDTH, SB_WIDTH,
            GLA_KW, GLA_KW, GLA_VW, GLA_VW,
            GLA_RANK,
            D_MODEL, D_MODEL)
IN_TOTAL = sum(IN_SIZES)


def rms_norm(x, g):
    xf = x.astype(jnp.float32)
    xf = xf * lax.rsqrt(jnp.mean(xf * xf, axis=-1, keepdims=True) + EPS)
    return xf.astype(x.dtype) * g

def to_heads(t, n_heads):
    b, s, _ = t.shape
    return t.reshape(b, s, n_heads, -1).transpose(0, 2, 1, 3)

def from_heads(t):
    b, h, s, d = t.shape
    return t.transpose(0, 2, 1, 3).reshape(b, s, h * d)

def stick_breaking_attention(q, k, v):
    s_len, dh = q.shape[2], q.shape[3]
    scale = dh ** -0.5
    outs = []
    for i0 in range(0, s_len, SB_BLOCK):
        end = i0 + SB_BLOCK
        qb = q[:, :, i0:end]
        kb = k[:, :, :end]
        vb = v[:, :, :end]
        z = jnp.einsum('bhqd,bhkd->bhqk', qb, kb).astype(jnp.float32) * scale
        t_idx = i0 + jnp.arange(SB_BLOCK)[:, None]
        s_idx = jnp.arange(end)[None, :]
        strict = s_idx < t_idx
        log_keep = jnp.where(strict, jax.nn.log_sigmoid(-z), 0.0)
        tail = lax.cumsum(log_keep, axis=3, reverse=True) - log_keep
        log_w = jax.nn.log_sigmoid(z) + tail
        w = jnp.where(strict, jnp.exp(log_w), 0.0)
        outs.append(jnp.einsum('bhqk,bhkd->bhqd', w.astype(v.dtype), vb))
    return jnp.concatenate(outs, axis=2)

def gla_chunked(q, k, v, log_a):
    b, h, s_len, dk = q.shape
    dv = v.shape[-1]
    c = GLA_CHUNK
    n = s_len // c
    qf = q.astype(jnp.float32).reshape(b, h, n, c, dk)
    kf = k.astype(jnp.float32).reshape(b, h, n, c, dk)
    vf = v.astype(jnp.float32).reshape(b, h, n, c, dv)
    cum = jnp.cumsum(log_a.reshape(b, h, n, c, dk), axis=3)
    cum_last = cum[:, :, :, -1:]
    q_dec = qf * jnp.exp(cum)
    k_inv = kf * jnp.exp(-cum)
    k_to_end = kf * jnp.exp(cum_last - cum)
    att = jnp.einsum('bhnck,bhnsk->bhncs', q_dec, k_inv)
    causal = jnp.tril(jnp.ones((c, c), dtype=bool))
    att = jnp.where(causal, att, 0.0)
    o_intra = jnp.einsum('bhncs,bhnsv->bhncv', att, vf)
    d_state = jnp.einsum('bhnck,bhncv->bhnkv', k_to_end, vf)
    chunk_decay = jnp.exp(cum_last[:, :, :, 0])

    def step(state, inp):
        dec, ds = inp
        return dec[..., None] * state + ds, state

    init = jnp.zeros((b, h, dk, dv), jnp.float32)
    _, states_before = lax.scan(step, init,
                                (jnp.moveaxis(chunk_decay, 2, 0), jnp.moveaxis(d_state, 2, 0)))
    states_before = jnp.moveaxis(states_before, 0, 2)
    o_inter = jnp.einsum('bhnck,bhnkv->bhncv', q_dec, states_before)
    return (o_intra + o_inter).reshape(b, h, s_len, dv)

def mixing_sublayer(xn, w_in, b_gate, w_alpha_up, b_alpha, gla_norm_g,
                    w_branch_sb, w_branch_gla, w_out):
    proj = xn @ w_in
    offsets = np.cumsum(IN_SIZES)[:-1].tolist()
    (sb_q, sb_k, sb_v, g_q, g_k, g_v, g_r, g_a,
     gate_sb, gate_gla) = jnp.split(proj, offsets, axis=-1)

    o_sb = stick_breaking_attention(to_heads(sb_q, SB_HEADS),
                                    to_heads(sb_k, SB_HEADS),
                                    to_heads(sb_v, SB_HEADS))
    o_sb = from_heads(o_sb)

    a_pre = (g_a @ w_alpha_up + b_alpha).astype(jnp.float32)
    log_a = jax.nn.log_sigmoid(a_pre) / GLA_TAU
    o_gla = gla_chunked(to_heads(g_q, GLA_HEADS) * (GLA_DK ** -0.5),
                        to_heads(g_k, GLA_HEADS),
                        to_heads(g_v, GLA_HEADS),
                        to_heads(log_a, GLA_HEADS))
    o_gla = o_gla * lax.rsqrt(jnp.mean(o_gla * o_gla, axis=-1, keepdims=True) + EPS)
    o_gla = from_heads(o_gla).astype(xn.dtype) * gla_norm_g * jax.nn.silu(g_r)

    y = (jax.nn.sigmoid(gate_sb + b_gate[0]) * (o_sb @ w_branch_sb)
         + jax.nn.sigmoid(gate_gla + b_gate[1]) * (o_gla @ w_branch_gla))
    return y @ w_out

def causal_depthwise_conv(u, w, bias):
    k_w = w.shape[0]
    s_len = u.shape[1]
    up = jnp.pad(u, ((0, 0), (k_w - 1, 0), (0, 0)))
    out = bias
    for i in range(k_w):
        out = out + up[:, i:i + s_len] * w[i]
    return out

def conv_ffn(hn, w_ffn_in, conv_w, conv_b, w_ffn_out):
    u = hn @ w_ffn_in
    a, g = jnp.split(u, 2, axis=-1)
    a = causal_depthwise_conv(a, conv_w, conv_b)
    return (jax.nn.gelu(a) * g) @ w_ffn_out

def first_inputs(seed: int = 0) -> dict:
    key = jax.random.key(seed)
    ks = jax.random.split(key, 16)
    f32 = jnp.float32

    def nrm(k, shape, scale):
        return jax.random.normal(k, shape, f32) * scale

    return {
        "x": jax.random.normal(ks[0], (BATCH, SEQ, D_MODEL), f32),
        "norm_mix_g": 1.0 + nrm(ks[1], (DEPTH, D_MODEL), 0.02),
        "w_in": nrm(ks[2], (DEPTH, D_MODEL, IN_TOTAL), D_MODEL ** -0.5),
        "b_gate": nrm(ks[3], (DEPTH, 2, D_MODEL), 0.02),
        "w_alpha_up": nrm(ks[4], (DEPTH, GLA_RANK, GLA_KW), GLA_RANK ** -0.5),
        "b_alpha": nrm(ks[5], (DEPTH, GLA_KW), 0.1),
        "gla_norm_g": 1.0 + nrm(ks[6], (DEPTH, GLA_VW), 0.02),
        "w_branch_sb": nrm(ks[7], (DEPTH, SB_WIDTH, D_MODEL), SB_WIDTH ** -0.5),
        "w_branch_gla": nrm(ks[8], (DEPTH, GLA_VW, D_MODEL), GLA_VW ** -0.5),
        "w_out": nrm(ks[9], (DEPTH, D_MODEL, D_MODEL), D_MODEL ** -0.5),
        "norm_ffn_g": 1.0 + nrm(ks[10], (DEPTH, D_MODEL), 0.02),
        "w_ffn_in": nrm(ks[11], (DEPTH, D_MODEL, 2 * D_FF), D_MODEL ** -0.5),
        "conv_w": nrm(ks[12], (DEPTH, CONV_WIDTH, D_FF), CONV_WIDTH ** -0.5),
        "conv_b": nrm(ks[13], (DEPTH, D_FF), 0.01),
        "w_ffn_out": nrm(ks[14], (DEPTH, D_FF, D_MODEL), D_FF ** -0.5),
        "norm_final_g": 1.0 + nrm(ks[15], (D_MODEL,), 0.02),
    }

def first_block(x, norm_mix_g, w_in, b_gate, w_alpha_up, b_alpha, gla_norm_g,
              w_branch_sb, w_branch_gla, w_out, norm_ffn_g, w_ffn_in, conv_w,
              conv_b, w_ffn_out, norm_final_g):
    h = x
    for i in range(DEPTH):
        xn = rms_norm(h, norm_mix_g[i])
        h = h + mixing_sublayer(xn, w_in[i], b_gate[i], w_alpha_up[i], b_alpha[i],
                                gla_norm_g[i], w_branch_sb[i], w_branch_gla[i], w_out[i])
        hn = rms_norm(h, norm_ffn_g[i])
        h = h + conv_ffn(hn, w_ffn_in[i], conv_w[i], conv_b[i], w_ffn_out[i])
    return rms_norm(h, norm_final_g)


D_POOL = D_MODEL // 2
POOL_WINDOWS = (2, 4, 8, 16)
N_POOL_GROUPS = len(POOL_WINDOWS)
POOL_GROUP_DIM = D_POOL // N_POOL_GROUPS
V_HEAD_DIM = 64
N_HEADS = (D_MODEL // 2) // V_HEAD_DIM
D_ATTN = N_HEADS * V_HEAD_DIM
D_MIX = D_POOL + D_ATTN
QK_NOPE_DIM = 64
QK_ROPE_DIM = 32
QK_DIM = QK_NOPE_DIM + QK_ROPE_DIM
Q_LORA_RANK = D_MODEL // 4
KV_LORA_RANK = D_MODEL // 8
ROPE_THETA = 10000.0
Q_BLOCK = 128
D_IN_PROJ = D_POOL + Q_LORA_RANK + KV_LORA_RANK + QK_ROPE_DIM
N_EXPERTS = 32
TOP_K = 4
D_EXPERT = D_MODEL
SWIGLU_ALPHA = 1.702
SWIGLU_LIMIT = 7.0
MOE_BLOCK = 128
RMS_EPS = 1e-6


def rmsnorm(x, g):
    xf = x.astype(jnp.float32)
    y = xf * lax.rsqrt(jnp.mean(xf * xf, axis=-1, keepdims=True) + RMS_EPS)
    return (y * g.astype(jnp.float32)).astype(x.dtype)

def rope_tables(positions):
    half = QK_ROPE_DIM // 2
    inv = ROPE_THETA ** (-jnp.arange(half, dtype=jnp.float32) / half)
    ang = positions.astype(jnp.float32)[..., None] * inv
    return jnp.cos(ang), jnp.sin(ang)

def apply_rope(x, cos, sin):
    half = QK_ROPE_DIM // 2
    xf = x.astype(jnp.float32)
    x1, x2 = xf[..., :half], xf[..., half:]
    out = jnp.concatenate([x1 * cos - x2 * sin, x2 * cos + x1 * sin], axis=-1)
    return out.astype(x.dtype)

def pool_mixer(u, w_pool, b_pool, pool_scale):
    B, S, _ = u.shape
    uf = u.reshape(B, S, N_POOL_GROUPS, POOL_GROUP_DIM).astype(jnp.float32)
    csum = jnp.pad(jnp.cumsum(uf, axis=1), ((0, 0), (1, 0), (0, 0), (0, 0)))
    t = jnp.arange(S)
    pooled = []
    for g, w in enumerate(POOL_WINDOWS):
        c = csum[:, :, g]
        lo = jnp.pad(c[:, :S + 1 - w], ((0, 0), (w - 1, 0), (0, 0)))
        cnt = jnp.minimum(t + 1, w).astype(jnp.float32)[None, :, None]
        pooled.append((c[:, 1:] - lo) / cnt)
    pooled = jnp.stack(pooled, axis=2)
    diff = (pooled - uf).astype(u.dtype)
    mixed = jnp.einsum('bsgc,gcd->bsgd', diff, w_pool) + b_pool
    return mixed.reshape(B, S, D_POOL) * pool_scale

def mla_attention(q_lat, kv_lat, k_rope_raw, cos, sin, g_q_a, w_q_b, g_kv_a, w_kv_b):
    B, S, _ = q_lat.shape
    q = (rmsnorm(q_lat, g_q_a) @ w_q_b).reshape(B, S, N_HEADS, QK_DIM)
    q_nope = q[..., :QK_NOPE_DIM]
    q_rope = apply_rope(q[..., QK_NOPE_DIM:], cos[:, :, None, :], sin[:, :, None, :])
    kv = (rmsnorm(kv_lat, g_kv_a) @ w_kv_b).reshape(B, S, N_HEADS, QK_NOPE_DIM + V_HEAD_DIM)
    k_nope, v = kv[..., :QK_NOPE_DIM], kv[..., QK_NOPE_DIM:]
    k_rope = apply_rope(k_rope_raw, cos, sin)
    scale = QK_DIM ** -0.5
    nb = S // Q_BLOCK
    qn_b = q_nope.reshape(B, nb, Q_BLOCK, N_HEADS, QK_NOPE_DIM).transpose(1, 0, 2, 3, 4)
    qr_b = q_rope.reshape(B, nb, Q_BLOCK, N_HEADS, QK_ROPE_DIM).transpose(1, 0, 2, 3, 4)
    k_idx = jnp.arange(S)

    def attend(args):
        qn, qr, blk = args
        s = (jnp.einsum('bqhd,bkhd->bhqk', qn, k_nope, preferred_element_type=jnp.float32)
             + jnp.einsum('bqhr,bkr->bhqk', qr, k_rope, preferred_element_type=jnp.float32)) * scale
        q_idx = blk * Q_BLOCK + jnp.arange(Q_BLOCK)
        s = jnp.where(k_idx[None, :] <= q_idx[:, None], s, -jnp.inf)
        p = jax.nn.softmax(s, axis=-1).astype(v.dtype)
        return jnp.einsum('bhqk,bkhd->bqhd', p, v)

    out = lax.map(attend, (qn_b, qr_b, jnp.arange(nb)))
    return out.transpose(1, 0, 2, 3, 4).reshape(B, S, D_ATTN)

def moe(h, w_router, b_router, w_gate_up, b_gate_up, w_down, b_down):
    B, S, D = h.shape
    T = B * S
    ht = h.reshape(T, D)
    logits = (ht @ w_router + b_router).astype(jnp.float32)
    top_vals, top_idx = lax.top_k(logits, TOP_K)
    gates = jax.nn.softmax(top_vals, axis=-1)
    n_assign = T * TOP_K
    e_flat = top_idx.reshape(-1).astype(jnp.int32)
    tok_flat = jnp.repeat(jnp.arange(T, dtype=jnp.int32), TOP_K)
    g_flat = gates.reshape(-1)
    order = jnp.argsort(e_flat)
    e_sorted = e_flat[order]
    counts = jnp.zeros((N_EXPERTS,), jnp.int32).at[e_flat].add(1)
    padded = ((counts + MOE_BLOCK - 1) // MOE_BLOCK) * MOE_BLOCK
    start = jnp.cumsum(counts) - counts
    pad_end = jnp.cumsum(padded)
    pad_start = pad_end - padded
    dest = pad_start[e_sorted] + (jnp.arange(n_assign, dtype=jnp.int32) - start[e_sorted])
    n_blocks = n_assign // MOE_BLOCK + N_EXPERTS
    n_rows = n_blocks * MOE_BLOCK
    row_tok = jnp.full((n_rows,), T, jnp.int32).at[dest].set(tok_flat[order])
    row_gate = jnp.zeros((n_rows,), jnp.float32).at[dest].set(g_flat[order])
    block_expert = jnp.minimum(
        jnp.searchsorted(pad_end, jnp.arange(n_blocks, dtype=jnp.int32) * MOE_BLOCK, side='right'),
        N_EXPERTS - 1)
    h_pad = jnp.concatenate([ht, jnp.zeros((1, D), ht.dtype)], axis=0)
    xb = h_pad[row_tok].reshape(n_blocks, MOE_BLOCK, D)

    def expert_block(args):
        xblk, e = args
        gu = xblk @ w_gate_up[e] + b_gate_up[e]
        gate = jnp.minimum(gu[:, :D_EXPERT], SWIGLU_LIMIT)
        up = jnp.clip(gu[:, D_EXPERT:], -SWIGLU_LIMIT, SWIGLU_LIMIT)
        act = gate * jax.nn.sigmoid(SWIGLU_ALPHA * gate) * (up + 1)
        return act @ w_down[e] + b_down[e]

    yb = lax.map(expert_block, (xb, block_expert)).reshape(n_rows, D)
    y = jnp.zeros((T + 1, D), h.dtype).at[row_tok].add(row_gate[:, None].astype(h.dtype) * yb)
    return y[:T].reshape(B, S, D)

def second_inputs(seed: int = 0) -> dict:
    key = jax.random.key(seed)
    ks = jax.random.split(key, 24)
    L, D, E, F = DEPTH, D_MODEL, N_EXPERTS, D_EXPERT
    nrm = lambda k, shape, fan_in: jax.random.normal(k, shape, jnp.float32) * (fan_in ** -0.5)
    gain = lambda k, shape: 1.0 + 0.05 * jax.random.normal(k, shape, jnp.float32)
    small = lambda k, shape: 0.01 * jax.random.normal(k, shape, jnp.float32)
    x = jax.random.normal(ks[0], (BATCH, SEQ, D), jnp.float32)
    positions = jnp.broadcast_to(jnp.arange(SEQ, dtype=jnp.int32), (BATCH, SEQ))
    return {
        'x': x,
        'positions': positions,
        'g_attn_norm': gain(ks[1], (L, D)),
        'w_in': nrm(ks[2], (L, D, D_IN_PROJ), D),
        'w_pool': nrm(ks[3], (L, N_POOL_GROUPS, POOL_GROUP_DIM, POOL_GROUP_DIM), POOL_GROUP_DIM),
        'b_pool': small(ks[4], (L, N_POOL_GROUPS, POOL_GROUP_DIM)),
        'pool_scale': gain(ks[5], (L, D_POOL)),
        'g_q_a': gain(ks[6], (L, Q_LORA_RANK)),
        'w_q_b': nrm(ks[7], (L, Q_LORA_RANK, N_HEADS * QK_DIM), Q_LORA_RANK),
        'g_kv_a': gain(ks[8], (L, KV_LORA_RANK)),
        'w_kv_b': nrm(ks[9], (L, KV_LORA_RANK, N_HEADS * (QK_NOPE_DIM + V_HEAD_DIM)), KV_LORA_RANK),
        'g_out_pool': gain(ks[10], (L, D_POOL)),
        'g_out_attn': gain(ks[11], (L, D_ATTN)),
        'w_out': nrm(ks[12], (L, D_MIX, D), D_MIX),
        'g_ffn_norm': gain(ks[13], (L, D)),
        'w_router': nrm(ks[14], (L, D, E), D),
        'b_router': small(ks[15], (L, E)),
        'w_gate_up': nrm(ks[16], (L, E, D, 2 * F), D),
        'b_gate_up': small(ks[17], (L, E, 2 * F)),
        'w_down': nrm(ks[18], (L, E, F, D), F),
        'b_down': small(ks[19], (L, E, D)),
        'g_final': gain(ks[20], (D,)),
    }

def second_block(x, positions, g_attn_norm, w_in, w_pool, b_pool, pool_scale, g_q_a, w_q_b,
              g_kv_a, w_kv_b, g_out_pool, g_out_attn, w_out, g_ffn_norm, w_router, b_router,
              w_gate_up, b_gate_up, w_down, b_down, g_final):
    cos, sin = rope_tables(positions)
    o1 = D_POOL
    o2 = o1 + Q_LORA_RANK
    o3 = o2 + KV_LORA_RANK
    for l in range(DEPTH):
        h = rmsnorm(x, g_attn_norm[l])
        proj = h @ w_in[l]
        u, q_lat, kv_lat, k_r = proj[..., :o1], proj[..., o1:o2], proj[..., o2:o3], proj[..., o3:]
        y_pool = pool_mixer(u, w_pool[l], b_pool[l], pool_scale[l])
        y_attn = mla_attention(q_lat, kv_lat, k_r, cos, sin, g_q_a[l], w_q_b[l], g_kv_a[l], w_kv_b[l])
        mix = jnp.concatenate([rmsnorm(y_pool, g_out_pool[l]), rmsnorm(y_attn, g_out_attn[l])], axis=-1)
        x = x + mix @ w_out[l]
        h = rmsnorm(x, g_ffn_norm[l])
        x = x + moe(h, w_router[l], b_router[l], w_gate_up[l], b_gate_up[l], w_down[l], b_down[l])
    return rmsnorm(x, g_final)


def setup_inputs(seed=0):
    out = dict(first_inputs(seed))
    for name, value in second_inputs(seed + 1).items():
        if name != "x":
            out[name + "_2"] = value
    return out


def reference(
    x, norm_mix_g, w_in, b_gate, w_alpha_up, b_alpha, gla_norm_g, w_branch_sb, w_branch_gla,
    w_out, norm_ffn_g, w_ffn_in, conv_w, conv_b, w_ffn_out, norm_final_g, positions_2,
    g_attn_norm_2, w_in_2, w_pool_2, b_pool_2, pool_scale_2, g_q_a_2, w_q_b_2, g_kv_a_2,
    w_kv_b_2, g_out_pool_2, g_out_attn_2, w_out_2, g_ffn_norm_2, w_router_2, b_router_2,
    w_gate_up_2, b_gate_up_2, w_down_2, b_down_2, g_final_2,
):
    x = first_block(
        x, norm_mix_g, w_in, b_gate, w_alpha_up, b_alpha, gla_norm_g, w_branch_sb, w_branch_gla,
        w_out, norm_ffn_g, w_ffn_in, conv_w, conv_b, w_ffn_out, norm_final_g,
    )
    return second_block(
        x, positions_2, g_attn_norm_2, w_in_2, w_pool_2, b_pool_2, pool_scale_2, g_q_a_2,
        w_q_b_2, g_kv_a_2, w_kv_b_2, g_out_pool_2, g_out_attn_2, w_out_2, g_ffn_norm_2,
        w_router_2, b_router_2, w_gate_up_2, b_gate_up_2, w_down_2, b_down_2, g_final_2,
    )


_drawn_inputs = setup_inputs


def setup_inputs(seed=0):
    import zlib

    import numpy as np

    out = dict(_drawn_inputs(seed))
    spreads = {}
    factors = {'b_gate': 2.955, 'conv_b': 3.005, 'b_gate_up_2': 8.0, 'b_down_2': 8.0, 'b_router_2': 3.091}
    for name, (base, spread) in spreads.items():
        noise = np.random.default_rng([zlib.crc32(name.encode()), seed]).standard_normal(out[name].shape)
        drawn = base * np.exp(spread * noise) if base else spread * noise
        out[name] = __import__('jax').numpy.asarray(drawn.astype(out[name].dtype))
    for name, factor in factors.items():
        out[name] = (out[name] * factor).astype(out[name].dtype)
    return out
```

```python
from contextlib import ExitStack

import numpy as np

import concourse.bass as bass
from concourse import mybir
from concourse.alu_op_type import AluOpType as ALU

F32 = mybir.dt.float32
F32R = mybir.dt.float32r
I32 = mybir.dt.int32
U32 = mybir.dt.uint32
ACT = mybir.ActivationFunctionType
X = mybir.AxisListType.X

P = 128
T = 256
NB = T // P
D = 1024
KT = D // P
EPS = 1e-6

SB_H, SB_D = 8, 64
GLA_H, GLA_DK, GLA_DV, CH = 4, 64, 128, 64
KW, VW, RANK = 256, 512, 16
D_FF = 2816
FF_STEPS = D_FF // 256
OFF_Q, OFF_K, OFF_V, OFF_GQK, OFF_GV, OFF_GR, OFF_GA, OFF_GATE = 0, 512, 1024, 1536, 2048, 2560, 3072, 3088

POOL_W = (2, 4, 8, 16)
MH, NOPE, ROPE, QK, VD = 8, 64, 32, 96, 64
HALF = ROPE // 2
QL, KVL = 256, 128
E, TOPK, FE = 32, 4, 1024
SWIGLU_ALPHA, SWIGLU_LIMIT = 1.702, 7.0

SLOTS = 64
OVER = (T * TOPK) // (SLOTS + 1)
JOBS = E + OVER + 1

RING = 6
SPLIT = 4
CW = 2048
JC = 12
POOL_LO = (2, 6, 10)
DVE_LO = tuple(c for c in range(JC) if c not in POOL_LO)

VEC_A = dict(norm_mix=0, norm_ffn=8, attn_norm=16, ffn_norm=24, conv_w=32, conv_b=98)
VEC_B = dict(b_alpha=0, gla_g=2, b_pool=6, pool_scale=10, g_q_a=14, g_kv_a=16, g_out_pool=17, g_out_attn=21,
             b_gate=25)
ROWS_A, ROWS_B = 120, 41

RESULTS = (
    [("vec", "dve")] + [(f"xT{b}{h}", "dve") for b in range(2) for h in range(2)]
    + [("sbq0", "act"), ("sbq1", "act"), ("sbk0", "act"), ("sbk1", "act"), ("sbv0", "dve"), ("sbv1", "dve")]
    + [(f"z{h}", "act") for h in range(4)] + [("gq", "dve"), ("gk", "dve")]
    + [(f"z{h}", "act") for h in range(4, 8)] + [("gv0", "dve"), ("gv1", "dve"), ("ga", "dve")]
    + [("gr0", "act"), ("gr1", "act"), ("al", "dve")]
    + [(f"c{h}", "dve") for h in range(4)] + [(f"gate{n}", "act") for n in range(4)]
    + [(f"c{h}", "dve") for h in range(4, 8)] + [("kend", "act"), ("att0", "act"), ("att1", "act"), ("o0", "dve")]
    + [(f"gate{n}", "act") for n in range(4, 8)]
    + [("ds0", "dve"), ("ds1", "dve"), ("o1", "dve"), ("og0", "act"), ("og1", "act"), ("ogt0", "dve"), ("ogt1", "dve")]
    + [(f"y{n}", "dve") for n in range(8)] + [(f"wo{n}{b}", "dve") for n in range(2) for b in range(2)]
    + [(f"hT{b}{h}", "dve") for b in range(2) for h in range(2)]
)
RESULTS2 = (
    [(f"nT{b}{h}", "dve") for b in range(2) for h in range(2)]
    + [("lat0", "act"), ("lat1", "act"), ("u0", "act"), ("u1", "act")]
    + [("qlT", "dve"), ("kvT", "dve")]
    + [(f"qq{b}{n}", "act") for b in range(2) for n in range(2)]
    + [(f"kv{b}{n}", "act") for b in range(2) for n in range(2)]
    + [(f"qT{n}", "act") for n in range(4)] + [(f"kT{n}", "dve") for n in range(4)]
    + [(f"s{h}", "dve") for h in range(MH)]
    + [("pm0", "act"), ("pm1", "act"), ("pss", "dve")]
    + [(f"pt{h}", "act") for h in range(MH)] + [("av0", "dve"), ("av1", "dve")]
    + [("yt0", "dve"), ("yt1", "dve")]
    + [(f"{s}{n}{b}", "dve") for n in range(2) for b in range(2) for s in ("pa", "pp")]
    + [(f"rT{b}{h}", "act") for b in range(2) for h in range(2)] + [("lg", "dve"), ("rk", "dve"), ("gT", "act")]
)


class Results:

    def __init__(self, order, s, banks):
        self.at = {name: n for n, (name, _) in enumerate(order)}
        self.order, self.s, self.banks = order, s, banks

    def bank(self, name):
        return self.banks[self.at[name] % 8]

    def filled(self, name):
        return self.s.filled, self.at[name] + 1

    def drained(self, name):
        n = self.at[name]
        who = self.order[n][1]
        return drained_sem(self.s, who), sum(w == who for _, w in self.order[: n + 1])

    def room(self, name):
        n = self.at[name]
        return self.drained(self.order[n - 8][0]) if n >= 8 else None


def drained_sem(s, who):
    return s.drained_act if who == "act" else s.drained_dve


class Steps:

    def __init__(self, eng, sem, base=0):
        self.eng, self.sem, self.base, self.n = eng, sem, base, 0

    def settle(self):
        self.eng.wait_ge(self.sem, self.base + self.n)

    def __call__(self, ins):
        ins.then_inc(self.sem, 1)
        self.n += 1
        self.settle()


def spread(ap, n):
    shape = [int(x) for x in ap.shape]
    return ap.unsqueeze(len(shape)).to_broadcast(shape + [n])


def front_chunks(w):
    def cols(m, c0, n, k0=0, kt=4):
        return m[k0 * P:(k0 + kt) * P, c0:c0 + n].rearrange("(k p) n -> p k n", p=P)

    first = []
    for c, user in ((OFF_Q, "sbq1"), (OFF_K, "sbk1"), (OFF_V, "sbv1"), (OFF_GQK, "gk"), (OFF_GV, "gv1"),
                    (OFF_GR, "gr1"), *((OFF_GATE + 512 * n, f"gate{2 * n + 1}") for n in range(4))):
        first += [(cols(w["w_in"], c, 512, 4 * h), (4, 512), user) for h in range(2)]
    for n in range(2):
        first += [(cols(m, 512 * n, 512), (4, 512), f"y{4 * n + 3}") for m in (w["w_branch_sb"], w["w_branch_gla"])]
    for n in range(2):
        first += [(cols(w["w_out"], 512 * n, 512, 4 * h), (4, 512), f"wo{n}1") for h in range(2)]
    second = []
    for c, n, user in ((512, 416, "lat1"), (0, 512, "u1")):
        second += [(cols(w["w_in_2"], c, n, 4 * h), (4, n), user) for h in range(2)]
    second.append((cols(w["w_q_b_2"], 0, 768, 0, 2), (2, 768), "qq11"))
    second.append((w["w_kv_b_2"].rearrange("p (o n) -> p o n", o=1), (1, 1024), "kv11"))
    second.append((w["w_pool_2"].rearrange("g c d -> c g d"), (4, 128), "pm1"))
    for n in range(2):
        second += [(cols(w["w_out_2"], 512 * n, 512, 4 * h), (4, 512), f"pp{n}1") for h in (1, 0)]
    return first, second


def ffn_chunk(g, kind, i):
    if kind == "o":
        return g.n_ffn + (3 * i + 3 if i < FF_STEPS - 1 else 3 * i + 2)
    return g.n_ffn + ((0, 1)[kind == "g"] if i == 0 else 3 * i + (1 if kind == "g" else -1))


class Program:

    def __init__(self, nc, w, s, t, out, banks):
        self.nc, self.w, self.s, self.t, self.out, self.banks = nc, w, s, t, out, banks
        self.r1, self.r2 = Results(RESULTS, s, banks), Results(RESULTS2, Filled2(s), banks)
        self.first, self.second = front_chunks(w)
        self.n_ffn = len(self.first)
        self.n_second = self.n_ffn + 3 * FF_STEPS
        self.n_moe = self.n_second + len(self.second)


def build(nc, w, out):
    with ExitStack() as ctx:
        s = Semaphores(lambda name: ctx.enter_context(nc.semaphore(name)))
        banks = [ctx.enter_context(nc.psum_tensor(f"bank{n}", [P, 512], F32)) for n in range(8)]

        def into(stack):
            def new(name, shape, dtype=F32):
                return stack.enter_context(nc.sbuf_tensor(name, [P, *shape], dtype))
            return new

        t = Buffers()
        t.persistent(into(ctx))
        for phase in (t.mixer, t.ffn, t.attention):
            with ExitStack() as stack:
                phase(into(stack))
        with ExitStack() as stack:
            t.experts(into(stack))
            for phase in (t.scratch, t.before_loop):
                with ExitStack() as inner:
                    phase(into(inner))
        t.h_n = t.x_n
        t.y_T = t.x_n[:].rearrange("p b (k n) -> p (b k) n", n=T)
        flat = t.sb_s[:].rearrange("p h n -> p (h n)")
        t.o_gla = flat[:, 0:1024].rearrange("p (b n) -> p b n", b=NB)
        t.o_n = flat[:, 1024:2048].rearrange("p (b n) -> p b n", b=NB)
        t.o_glaT = flat[:, 2048:3072].rearrange("p (k n) -> p k n", k=4)
        flat = t.prob_T[:].rearrange("p h n -> p (h n)")
        t.sel, t.sel_tmp = (flat[:, n * (OVER + 1) * E:(n + 1) * (OVER + 1) * E].rearrange("p (m e) -> p m e", e=E)
                            for n in range(2))

        g = Program(nc, w, s, t, out, banks)

        block = ctx.enter_context(nc.Block())

        @block.sync
        def _(sp):
            sync_program(g, sp)

        @block.gpsimd
        def _(pool):
            gpsimd_program(g, pool)

        @block.scalar
        def _(act):
            scalar_program(g, act)

        @block.vector
        def _(dve):
            vector_program(g, dve)

        @block.tensor
        def _(pe):
            tensor_program(g, pe)


def slot_use(n):
    return n % RING, 16 * (n // RING + 1)


def chunk(g, n, shape):
    k, m = shape
    return g.t.ring[:, n % RING, 0:k * m].rearrange("p (k m) -> p k m", k=k)


def sync_program(g, sp):
    s, w, t = g.s, g.w, g.t

    def load(n, src, shape):
        sp.dma_start(chunk(g, n, shape), src).then_inc(s.landed[n % RING], 16)

    for n, (src, shape, _) in enumerate(g.first):
        if n >= RING:
            sp.wait_ge(*g.r1.filled(g.first[n - RING][2]))
        load(n, src, shape)

    ffn_in = w["w_ffn_in"].rearrange("(k p) n -> p k n", p=P)
    ffn_out = w["w_ffn_out"].rearrange("(k p) n -> p k n", p=P)

    def load_ffn(i, kind, turns=0, i0=0):
        n = ffn_chunk(g, kind, i0)
        dst = t.ring[:, n % RING, :].rearrange("p (k m) -> p k m", k=2 if kind == "o" else KT)
        if kind == "o":
            src = ffn_out[:, bass.ds(i * 2, 2), :]
        else:
            src = ffn_in[:, :, bass.ds(i * 256 + (D_FF if kind == "g" else 0), 256)]
        sp.dma_start(dst, src).then_inc(s.landed[n % RING], 16)

    for i, kind in ((0, "a"), (0, "g"), (1, "a"), (0, "o"), (1, "g"), (2, "a")):
        n = ffn_chunk(g, kind, i)
        sp.wait_ge(*g.r1.filled(g.first[n - RING][2]))
        load_ffn(i, kind, 0, i)
    sp.wait_ge(s.ff_a, 1)
    load_ffn(1, "o", 0, 1)
    with sp.Fori(0, (FF_STEPS - 3) // 2) as m:
        for q in range(2):
            sp.wait_ge(s.ff_g, m * 2 + (q + 1))
            load_ffn(m * 2 + (q + 2), "g", m, q + 2)
            sp.wait_ge(s.ff_a, m * 2 + (q + 2))
            load_ffn(m * 2 + (q + 3), "a", m, q + 3)
            sp.wait_ge(s.ff_o, m * 2 + (q + 1))
            load_ffn(m * 2 + (q + 2), "o", m, q + 2)
    sp.wait_ge(s.ff_g, FF_STEPS - 2)
    load_ffn(FF_STEPS - 1, "g", 0, FF_STEPS - 1)
    sp.wait_ge(s.ff_o, FF_STEPS - 2)
    load_ffn(FF_STEPS - 1, "o", 0, FF_STEPS - 1)

    former = [("o", 3), ("g", 2), ("a", 1), ("o", 2), ("g", 1), ("o", 1)]
    for n, (src, shape, _) in enumerate(g.second):
        if n < RING:
            kind, back = former[n]
            sp.wait_ge({"a": s.ff_a, "g": s.ff_g, "o": s.ff_o}[kind], FF_STEPS + 1 - back)
        else:
            sp.wait_ge(*g.r2.filled(g.second[n - RING][2]))
        load(g.n_second + n, src, shape)

    gate_up = w["w_gate_up_2"].rearrange("e (h k p) n -> e h p k n", p=P, k=4)
    down = w["w_down_2"].rearrange("e (h k p) n -> e h p k n", p=P, k=4)

    def load_expert(e, c):
        q, h = c // 2, c % 2
        if q < 4:
            col = 512 * (q // 2) + FE * (q % 2)
            src = gate_up[e, h, :, :, col:col + 512]
        else:
            src = down[e, h, :, :, 512 * (q - 4):512 * (q - 4) + 512]
        n = g.n_moe + c
        sp.dma_start(chunk(g, n, (4, 512)), src).then_inc(s.landed[n % RING], 16)

    def wait_split(j, c):
        lo_of, sem = (POOL_LO, s.lo_pool) if c in POOL_LO else (DVE_LO, s.lo_dve)
        sp.wait_ge(sem, j * len(lo_of) + sum(x <= c for x in lo_of))

    for c in range(RING):
        sp.wait_ge(*g.r2.filled(g.second[len(g.second) - RING + c][2]))
        load_expert(0, c)
    sp.wait_ge(s.jobs_ready, 1)
    last = sp.value_load(t.job_count[0:1, 0:1], min_val=E - 1, max_val=E + OVER - 1)

    with sp.Fori(0, last) as j:
        e = sp.value_load(t.job_expert[0:1, bass.ds(j, 1)], min_val=0, max_val=E - 1)
        for c in range(RING, JC):
            wait_split(j, c - RING)
            load_expert(e, c)
        e = sp.value_load(t.job_expert[0:1, bass.ds(j + 1, 1)], min_val=0, max_val=E - 1)
        for c in range(RING):
            wait_split(j, c + RING)
            load_expert(e, c)
    e = sp.value_load(t.job_expert[0:1, bass.ds(last, 1)], min_val=0, max_val=E - 1)
    for c in range(RING, JC):
        wait_split(last, c - RING)
        load_expert(e, c)

    sp.wait_ge(s.out_ready, 2)
    for b in range(NB):
        sp.dma_start(g.out[b * P:(b + 1) * P, :], t.h[:, b, :]).then_inc(s.stored, 16)
    sp.wait_ge(s.stored, 16 * NB)


NORMS = (("mix", NB), ("gla", NB * GLA_H), ("ffn", NB), ("end1", NB), ("attn", NB), ("lat", 2 * NB), ("mla", NB),
         ("pool", NB), ("moe", NB), ("end2", NB))
NORM_AT = {name: n for n, (name, _) in enumerate(NORMS)}
NORM_N = dict(NORMS)


def gpsimd_program(g, pool):
    s, t = g.s, g.t
    step = Steps(pool, s.pool_step)

    def triangle(ap, op, sign, fill, n=P):
        step(pool.affine_select(out=ap, in_=ap, compare_op=op, fill=fill, base=0, pattern=[[sign, n]],
                                channel_multiplier=-sign))

    step(pool.memset(t.ident[:], 0.0))
    triangle(t.ident[:], ALU.not_equal, 1, 1.0)
    step(pool.memset(t.neg_half[:], -0.5))
    for i in range(HALF):
        freq = np.float32(10000.0) ** np.float32(-i / HALF)
        step(pool.memset(t.inv_freq[:, i:i + 1], float(freq)))
    pool.memset(t.ones[:], 1.0).then_inc(s.early_consts, 1)
    step(pool.memset(t.zrow[0:1, :], 0.0))
    step(pool.memset(t.tri[:], 1.0))
    triangle(t.tri[:], ALU.is_ge, -1, 0.0)
    step(pool.memset(t.before[:], 1.0))
    triangle(t.before[:], ALU.is_gt, 1, 0.0)
    step(pool.memset(t.sb_keep[:], 1.0))
    step(pool.memset(t.sb_cap[:], 0.0))
    for c in (0, 2 * P):
        triangle(t.sb_keep[:, c:c + P], ALU.is_gt, 1, 0.0)
        triangle(t.sb_cap[:, c:c + P], ALU.is_gt, 1, -1e30)
    step(pool.memset(t.chunk_start[:], 1.0))
    step(pool.memset(t.att[:], 0.0))
    step(pool.memset(t.state[:], 0.0))
    pool.memset(t.chunk_start[:, 0:T:CH], 0.0).then_inc(s.consts, 1)

    def rsqrt(name):
        k, n = NORM_AT[name], NORM_N[name]
        pool.wait_ge(s.msq_ready, k + 1)
        pool.tensor_tensor(t.rstd[:, k, 0:n], t.msq[:, k, 0:n], t.neg_half[:, 0:n], ALU.pow).then_inc(s.rstd_ready, 1)

    rsqrt("mix")
    pool.wait_ge(*g.r1.drained("att1"))
    for q in range(2):
        rows = slice(CH * q, CH * q + CH)
        pool.affine_select(out=t.att[rows, :, rows], in_=t.att[rows, :, rows], compare_op=ALU.is_ge, fill=0.0, base=0,
                           pattern=[[0, 2 * GLA_H], [1, CH]], channel_multiplier=-1).then_inc(s.att_masked, 1)
    rsqrt("gla")
    rsqrt("ffn")
    rsqrt("end1")
    step(pool.memset(t.at_mask[:], 0.0))
    for c in (0, 2 * P):
        triangle(t.at_mask[:, c:c + P], ALU.is_ge, -1, -1e30)
    for n, win in enumerate(POOL_W):
        step(pool.memset(t.inv_count[:, n, :], 1.0 / win))
    for i in range(POOL_W[-1] - 1):
        n = next(n for n, win in enumerate(POOL_W) if win > i + 1)
        step(pool.memset(t.inv_count[:, n:, i:i + 1], 1.0 / (i + 1)))
    for q in range(2):
        step(pool.iota(t.iota_i[32 * q:32 * q + 32, 0:1], pattern=[[0, 1]], base=0, channel_multiplier=1))
    step(pool.tensor_copy(t.part32[0:64, :], t.iota_i[0:64, 0:1]))
    step(pool.iota(t.iota_i[:, 0:JOBS], pattern=[[1, JOBS]], base=0, channel_multiplier=0))
    step(pool.tensor_copy(t.iota_f[:, 0:JOBS], t.iota_i[:, 0:JOBS]))
    step(pool.iota(t.iota_i[:, 0:2 * SLOTS], pattern=[[0, 2], [1, SLOTS]], base=0, channel_multiplier=0))
    step(pool.tensor_copy(t.iota_s[:], t.iota_i[:, 0:2 * SLOTS]))
    step(pool.memset(t.bias_col[0:64, 0:SLOTS], 1.0))
    step(pool.memset(t.bias_col[0:64, SLOTS:], 0.0))
    pool.memset(t.u_pad[:, :, 0:16], 0.0).then_inc(s.consts2, 1)
    rsqrt("attn")
    rsqrt("lat")
    pool.wait_ge(*g.r2.drained("u1"))
    pool.wait_ge(s.consts2, 1)
    src, dst = t.u_pad, t.win_a
    for n in range(4):
        sh = 1 << n
        step(pool.tensor_tensor(dst[:, n:, sh:], src[:, n:, sh:], src[:, n:, :16 + T - sh], ALU.add))
        step(pool.tensor_tensor(t.diff[:, n, :], dst[:, n, 16:], t.inv_count[:, n, :], ALU.mult))
        if n < 3:
            step(pool.tensor_copy(dst[:, n:, 0:sh], src[:, n:, 0:sh]))
        src, dst = dst, (t.win_b if dst is t.win_a else t.win_a)
    pool.tensor_tensor(t.diff[:], t.diff[:], t.u_pad[:, :, 16:], ALU.subtract).then_inc(s.diff_ready, 1)
    rsqrt("mla")
    rsqrt("pool")
    rsqrt("moe")

    pool.wait_ge(s.jobs_ready, 1)
    last = pool.value_load(t.job_count[0:1, 0:1], min_val=E - 1, max_val=E + OVER - 1)
    with pool.Fori(0, last + 1) as j:
        for c in POOL_LO:
            pool.wait_ge(s.hi_done, j * JC + (c + 1))
            raw = t.ring[:, (g.n_moe + c) % RING, :]
            pool.tensor_tensor(t.w_lo[:, c % SPLIT, :], raw, t.w_hi[:, c % SPLIT, :].bitcast(F32),
                               ALU.subtract).then_inc(s.lo_pool, 1)
    rsqrt("end2")


def scalar_program(g, act):
    s, t, w, r1, r2 = g.s, g.t, g.w, g.r1, g.r2
    step = Steps(act, s.act_step)

    for b in range(NB):
        act.dma_start(t.h[:, b, :], w["x"][b * P:(b + 1) * P, :]).then_inc(s.x_in, 16)

    def rows(table, r0, m):
        n = int(np.prod(m.shape)) // P
        flat = m.rearrange("a (k p) -> (a k) p", p=P)
        act.dma_start(table[r0:r0 + n, :], flat).then_inc(s.vec_in, 16)

    for name, r0 in VEC_A.items():
        rows(t.vec_a, r0, w["vectors"][name])
    for name, r0 in VEC_B.items():
        rows(t.vec_b, r0, w["vectors"][name])
    act.dma_start(t.pos_i[:], w["positions"].rearrange("(b p) -> p b", p=P), allow_slow_non_contiguous=True).then_inc(s.pos_in, 16)
    act.dma_start(t.w_ga[:], w["w_in"][:, OFF_GA:OFF_GA + RANK].rearrange("(k p) n -> p k n", p=P)).then_inc(s.small_in, 16)
    act.dma_start(t.w_alpha[0:RANK, :], w["w_alpha_up"]).then_inc(s.small_in, 16)
    act.dma_start(t.w_router[:], w["w_router_2"].rearrange("(k p) n -> p k n", p=P)).then_inc(s.small_in, 16)
    act.dma_start(t.b_router[:], w["row_b_router_2"].to_broadcast([P, E])).then_inc(s.small_in, 16)
    act.dma_start(t.g_rows[:], w["row_norm_final_g"].to_broadcast([P, D])).then_inc(s.small_in, 16)

    act.wait_ge(s.angles, 1)
    act.activation(t.sin_cos[:], t.ang[:], ACT.Sin).then_inc(s.rope_ready, 1)
    act.preload_act_table_set("natural_log_exp_and_others")

    def take(r, name, dst, src, scale=1.0, fn=ACT.Copy):
        act.wait_ge(*r.filled(name))
        act.activation(dst, src, fn, scale=scale).then_inc(r.drained(name)[0], 1)

    def pair(r, name):
        return r.bank(name)[:].rearrange("p (k n) -> p k n", k=2)

    for n in range(2):
        take(r1, f"sbq{n}", t.sb_q[:, 2 * n:2 * n + 2, :], pair(r1, f"sbq{n}"), scale=SB_D ** -0.5)
    for n in range(2):
        take(r1, f"sbk{n}", t.sb_k[:, 2 * n:2 * n + 2, :], pair(r1, f"sbk{n}"))

    def log_term(dst, src, done):
        step(act.activation(dst, src, ACT.Abs))
        step(act.activation(dst, dst, ACT.Exp, scale=-1.0))
        act.activation(dst, dst, ACT.Ln, bias=1.0).then_inc(done, 1)

    for half in range(2):
        for h in range(4 * half, 4 * half + 4):
            take(r1, f"z{h}", t.z[:, h, :], r1.bank(f"z{h}")[:, 0:384])
        act.wait_ge(*r1.drained(f"z{4 * half + 3}"))
        hs = slice(4 * half, 4 * half + 4)
        log_term(t.sb_l[:, hs, :], t.z[:, hs, :], s.sb_log)
    for n in range(2):
        src = pair(r1, f"gr{n}")
        act.wait_ge(*r1.filled(f"gr{n}"))
        step(act.activation(t.gr[:, 2 * n:2 * n + 2, :], src, ACT.Copy))
        act.activation(t.gr_e[:, 2 * n:2 * n + 2, :], src, ACT.Exp, scale=-1.0).then_inc(s.drained_act, 1)
    act.wait_ge(*r1.drained("al"))
    log_term(t.al_l[:], t.a_pre[:], s.al_log)

    def weights_of_half(half):
        hs = slice(4 * half, 4 * half + 4)
        act.wait_ge(s.sb_arg, half + 1)
        act.activation(t.sb_l[:, hs, :], t.z[:, hs, :], ACT.Exp).then_inc(s.sb_w, 1)

    def gate(n):
        act.wait_ge(*r1.filled(f"gate{n}"))
        for i in range(2):
            ins = act.activation(t.gates[:, 2 * n + i, :], pair(r1, f"gate{n}")[:, i, :], ACT.Exp, scale=-1.0,
                                 bias=t.neg_b_gate[:, 2 * n + i:2 * n + i + 1])
            if i == 0:
                step(ins)
        ins.then_inc(s.drained_act, 1)

    weights_of_half(0)
    act.wait_ge(s.gla_cum, 1)
    act.activation(t.dec_q[:], t.cum[:], ACT.Exp, scale=-1.0 / 16).then_inc(s.gla_exp, 1)
    act.activation(t.dec_k[:], t.cum[:], ACT.Exp, scale=1.0 / 16).then_inc(s.gla_exp, 1)
    act.activation(t.dec_e[:], t.cum_end[:], ACT.Exp, scale=1.0 / 16).then_inc(s.gla_exp, 1)
    for n in range(4):
        gate(n)
    weights_of_half(1)
    take(r1, "kend", t.k_end[:], r1.bank("kend")[:].rearrange("p (b n) -> p b n", b=NB))
    for n in range(2):
        act.wait_ge(*r1.filled(f"att{n}"))
        for q in range(2):
            rows = slice(CH * q, CH * q + CH)
            ins = act.activation(t.att[rows, 4 * n:4 * n + 4, rows],
                                 r1.bank(f"att{n}")[rows].rearrange("p (k n) -> p k n", k=4)[:, :, rows], ACT.Copy)
            if q == 0:
                step(ins)
        ins.then_inc(s.drained_act, 1)
    for n in range(4, 8):
        gate(n)
    for b in range(NB):
        take(r1, f"og{b}", t.o_gla[:, b, :], r1.bank(f"og{b}")[:])

    act.preload_act_table(ACT.Gelu_apprx_tanh)

    def ffn(i, q):
        act.wait_ge(s.ff_a, i + 1)
        act.wait_ge(s.ff_conv, i - 1 if not isinstance(i, int) else max(i - 1, 0))
        act.activation(t.a_pad[:, q, :, 2:], g.banks[4 + q][:].rearrange("p (k n) -> p k n", k=2),
                       ACT.Copy).then_inc(s.ff_pad, 1)
        act.wait_ge(s.ff_conv, i + 1)
        act.activation(t.ff_ge[:, q], t.ff_c[:, q], ACT.Gelu_apprx_tanh).then_inc(s.ff_gelu, 1)

    act.wait_ge(s.ff_zero, 1)
    ffn(0, 0)
    with act.Fori(0, (FF_STEPS - 1) // 2) as m:
        ffn(m * 2 + 1, 1)
        ffn(m * 2 + 2, 0)
    act.preload_act_table_set("natural_log_exp_and_others")

    act.wait_ge(s.msq_ready, NORM_AT["attn"] + 1)
    act.dma_start(t.g_rows[:], w["row_g_ffn_norm_2"].to_broadcast([P, D])).then_inc(s.late_in, 16)
    for b in range(NB):
        take(r2, f"lat{b}", t.lat[:, b, :], r2.bank(f"lat{b}")[:, 0:416])
    act.wait_ge(s.consts2, 1)
    for n in range(2):
        take(r2, f"u{n}", t.u_pad[:, 2 * n:2 * n + 2, 16:], pair(r2, f"u{n}"))
    for b in range(NB):
        for n in range(2):
            take(r2, f"qq{b}{n}", t.q_tok[:, b, 384 * n:384 * n + 384], r2.bank(f"qq{b}{n}")[:, 0:384])
    for b in range(NB):
        for n in range(2):
            src = r2.bank(f"kv{b}{n}")[:].rearrange("p (h x) -> p h x", h=4)
            hs = slice(4 * n, 4 * n + 4)
            act.wait_ge(*r2.filled(f"kv{b}{n}"))
            step(act.activation(t.k_tok[:, b, hs, 0:NOPE], src[:, :, 0:NOPE], ACT.Copy))
            act.activation(t.v_tok[:, b, hs, :], src[:, :, NOPE:], ACT.Copy).then_inc(r2.drained("kv00")[0], 1)
    for n in range(4):
        take(r2, f"qT{n}", t.q_T[0:QK, 2 * n:2 * n + 2, :], pair(r2, f"qT{n}")[0:QK])

    def soft(h):
        for b in range(NB):
            cs = slice(0, P) if b == 0 else slice(P, 3 * P)
            act.wait_ge(s.row_max, h // 4 + 1)
            act.activation(t.score[:, h, cs], t.score[:, h, cs], ACT.Exp, bias=t.row_m[:, h, b:b + 1],
                           accum_out=t.row_l[:, h, b:b + 1]).then_inc(s.prob_ready, 1)

    for h in range(MH):
        soft(h)
        if h == 3:
            for n in range(2):
                act.wait_ge(*r2.filled(f"pm{n}"))
                for i in range(2):
                    f = 2 * n + i
                    ins = act.activation(t.y_pool[:, f, :], pair(r2, f"pm{n}")[:, i, :], ACT.Identity,
                                         bias=vec(t, "b_pool", f))
                    if i == 0:
                        step(ins)
                ins.then_inc(r2.drained(f"pm{n}")[0], 1)
    for h in range(MH):
        take(r2, f"pt{h}", t.prob_T[:, h, :], r2.bank(f"pt{h}")[:, 0:384])
    for b in range(NB):
        for h in range(2):
            take(r2, f"rT{b}{h}", t.h_T[:, 4 * h:4 * h + 4, b * P:(b + 1) * P],
                 r2.bank(f"rT{b}{h}")[:].rearrange("p (k n) -> p k n", k=4))
    for b in range(NB):
        act.wait_ge(s.top_ready, b + 1)
        act.activation(t.top_e[:], t.top_e[:], ACT.Exp, accum_out=t.top_s[:]).then_inc(s.top_exp, 1)
    take(r2, "gT", t.gate_T[0:E, :], r2.bank("gT")[0:E, 0:T])

    act.wait_ge(s.jobs_ready, 1)
    act.dma_start(t.b_down[0:E, :], w["b_down_2"]).then_inc(s.b_down_in, 16)
    for q in range(2):
        act.dma_start(t.bias_raw[32 * q:32 * q + 32, :], w["b_gate_up_2"]).then_inc(s.bias_in, 16)
    act.dma_start(t.g_rows[:], w["row_g_final_2"].to_broadcast([P, D])).then_inc(s.end_in, 16)
    act.activation(t.x_hi[:], t.h_n[:], ACT.Copy).then_inc(s.x_split, 1)
    act.wait_ge(s.bias_in, 32)
    act.activation(t.bias_hl[0:64, :], t.bias_raw[0:64, :], ACT.Copy).then_inc(s.bias_hi, 1)
    act.sem_inc(s.y_copied, 2)
    act.preload_act_table(ACT.Sigmoid)

    def copy_x(half, count):
        act.wait_ge(s.gathered, count)
        act.activation(t.x_T[:, 4 * half:4 * half + 4, :], g.banks[6][:].rearrange("p (k n) -> p k n", k=4),
                       ACT.Copy).then_inc(s.x_copied, 1)

    copy_x(0, 1)
    copy_x(1, 2)
    act.wait_ge(s.jobs_ready, 1)
    last = act.value_load(t.job_count[0:1, 0:1], min_val=E - 1, max_val=E + OVER - 1)
    with act.Fori(0, last + 1) as j:
        def hi(c):
            n = g.n_moe + c
            act.wait_ge(s.landed[n % RING], j * (16 * JC // RING) + 16 * (n // RING + 1))
            if c % 2 == 0:
                act.wait_ge(s.half_done, j * 6 + (c - SPLIT) // 2 + 1 + 2)
            else:
                act.wait_ge(s.group_done, j * 6 + (c - SPLIT) // 2 + 1 + 2)
            act.activation(t.w_hi[:, c % SPLIT, :], t.ring[:, n % RING, :], ACT.Copy).then_inc(s.hi_done, 1)

        def low_rows(q):
            act.wait_ge(s.group_done, j * 6 + q + 1 + 2)
            act.wait_ge(s.summed, j * 4 + q + 1)
            act.activation(t.lo_rows[0:SLOTS, q % 2, :], g.banks[4 + q % 2][SLOTS:, :],
                           ACT.Copy).then_inc(s.lo_rows_ready, 1)

        def sigmoid(half):
            act.wait_ge(s.gate_ready, j * 2 + half + 1)
            act.wait_ge(s.act_ready, j * 2 + half)
            act.activation(t.sig[0:SLOTS, :], t.gate[0:SLOTS, :], ACT.Sigmoid,
                           scale=SWIGLU_ALPHA).then_inc(s.sig_ready, 1)

        def act_hi(half):
            act.wait_ge(s.act_turned, j * 2 + half + 1)
            act.activation(t.act_T[:, 4 * half:4 * half + 4, 0:SLOTS],
                           g.banks[7][:, 256 * half:256 * half + 256].rearrange("p (k n) -> p k n", k=4),
                           ACT.Copy).then_inc(s.act_hi, 1)

        def copy_y(n):
            act.wait_ge(s.group_done, j * 6 + 4 + n + 1 + 2)
            act.wait_ge(s.combined, j * 2 + n + 1)
            act.activation(t.y_slot[:, n, :], g.banks[4 + n][:], ACT.Copy).then_inc(s.y_copied, 1)

        for c in range(4):
            hi(c)
        low_rows(0)
        hi(4)
        hi(5)
        low_rows(1)
        hi(6)
        sigmoid(0)
        hi(7)
        low_rows(2)
        hi(8)
        hi(9)
        low_rows(3)
        hi(10)
        sigmoid(1)
        act.wait_ge(s.weights_turned, j + 1)
        act.wait_ge(s.combined, j * 2 + 2)
        act.activation(t.mix_w[:], g.banks[6][:, 0:T], ACT.Copy).then_inc(s.mix_ready, 1)
        act_hi(0)
        copy_x(0, j * 2 + 3)
        copy_x(1, j * 2 + 4)
        hi(11)
        act_hi(1)
        copy_y(0)
        copy_y(1)


def vec(t, name, n=0, count=1):
    c = (VEC_A[name] if name in VEC_A else ROWS_A + VEC_B[name]) + n
    return t.vec_T[:, c:c + count]


def vector_program(g, dve):
    s, t, w, r1, r2 = g.s, g.t, g.w, g.r1, g.r2
    step = Steps(dve, s.dve_step)

    dve.wait_ge(s.early_consts, 1)
    dve.wait_ge(s.pos_in, 16)
    step(dve.tensor_copy(t.pos_f[:], t.pos_i[:]))
    sin_arg, cos_arg = t.ang[:, 0], t.ang[:, 1]
    for b in range(NB):
        step(dve.tensor_scalar(sin_arg[:, b, :], t.inv_freq[:], t.pos_f[:, b:b + 1], None, ALU.mult))
    step(dve.tensor_scalar(t.turns[:], sin_arg, float(1 / (2 * np.pi)), None, ALU.mult))
    step(dve.tensor_copy(t.turns_i[:], t.turns[:]))
    step(dve.tensor_copy(t.turns[:], t.turns_i[:]))
    two_pi, parts = 2 * np.pi, []
    for bits in (6, 9, 30):
        part = float(np.float32(np.floor(two_pi * 2.0 ** bits) / 2.0 ** bits)) if bits < 30 else float(np.float32(two_pi))
        parts.append(part)
        two_pi -= part
    for part in parts:
        step(dve.scalar_tensor_tensor(out=sin_arg, in0=t.turns[:], scalar=-part, in1=sin_arg, op0=ALU.mult, op1=ALU.add))
    step(dve.tensor_scalar(cos_arg, sin_arg, float(np.pi / 2), None, ALU.add))
    pi = 3.141592
    for arg in (sin_arg, cos_arg):
        for op, turn in ((ALU.is_gt, -2 * np.pi), (ALU.is_lt, 2 * np.pi)):
            bound = pi if op == ALU.is_gt else -pi
            step(dve.tensor_scalar(t.turns[:], arg, bound, float(turn), op, ALU.mult))
            step(dve.tensor_tensor(arg, arg, t.turns[:], ALU.add))
    dve.tensor_scalar(t.ang[:], t.ang[:], -pi, pi, ALU.max, ALU.min).then_inc(s.angles, 1)

    def mean_squares(name, parts):
        k = NORM_AT[name]
        for i, (src, scratch, n) in enumerate(parts):
            step(dve.tensor_tensor_reduce(scratch, src, src, 1.0, 0.0, ALU.mult, ALU.add, t.msq[:, k, i:i + 1]))
        finish_mean(name, [n for _, _, n in parts])

    def finish_mean(name, widths):
        k, m = NORM_AT[name], len(widths)
        for n in sorted(set(widths)):
            cols = [i for i, x in enumerate(widths) if x == n]
            a, b = cols[0], cols[-1] + 1
            ins = dve.tensor_scalar(t.msq[:, k, a:b], t.msq[:, k, a:b], 1.0 / n, EPS, ALU.mult, ALU.add)
            if n != max(widths):
                step(ins)
        ins.then_inc(s.msq_ready, 1)

    def rstd(name, i):
        return t.rstd[:, NORM_AT[name], i:i + 1]

    def have_rstd(name):
        dve.wait_ge(s.rstd_ready, NORM_AT[name] + 1)

    def out_of(r, name):
        dve.wait_ge(*r.filled(name))
        return r.bank(name), r.drained(name)[0]

    def turned(r, prefix, dst, gain):
        for b in range(NB):
            for h in range(2):
                bank, done = out_of(r, f"{prefix}{b}{h}")
                dve.tensor_tensor(dst[:, 4 * h:4 * h + 4, b * P:(b + 1) * P],
                                  bank[:].rearrange("p (k n) -> p k n", k=4),
                                  spread(vec(t, gain, 4 * h, 4), P), ALU.mult).then_inc(done, 1)

    bank, done = None, None
    dve.wait_ge(s.x_in, 16 * NB)
    mean_squares("mix", [(t.h[:, b, :], t.x_n[:, b, :], D) for b in range(NB)])
    bank, done = out_of(r1, "vec")
    step(dve.tensor_copy(t.vec_T[:, 0:ROWS_A], bank[:, 0:ROWS_A]))
    dve.tensor_copy(t.vec_T[:, ROWS_A:], bank[:, P:P + ROWS_B]).then_inc(done, 1)
    dve.wait_ge(*r1.drained("vec"))
    step(dve.tensor_scalar(t.neg_b_gate[:], vec(t, "b_gate", 0, 16), -1.0, None, ALU.mult))
    have_rstd("mix")
    for b in range(NB):
        dve.tensor_scalar(t.x_n[:, b, :], t.h[:, b, :], rstd("mix", b), None, ALU.mult).then_inc(s.x_n_ready, 1)
    turned(r1, "xT", t.x_nT, "norm_mix")
    for b in range(NB):
        bank, done = out_of(r1, f"sbv{b}")
        dve.tensor_copy(t.sb_v[:, b, :], bank[:]).then_inc(done, 1)

    def two(r, name):
        bank, done = out_of(r, name)
        return bank[:].rearrange("p (k n) -> p k n", k=2), done

    bank, done = two(r1, "gq")
    dve.tensor_scalar(t.g_q[:], bank, GLA_DK ** -0.5, None, ALU.mult).then_inc(done, 1)
    bank, done = two(r1, "gk")
    dve.tensor_copy(t.g_k[:], bank).then_inc(done, 1)

    def softplus_of(half):
        hs = slice(4 * half, 4 * half + 4)
        dve.wait_ge(s.sb_log, half + 1)
        step(dve.scalar_tensor_tensor(out=t.sb_s[:, hs, :], in0=t.z[:, hs, :], scalar=0.0, in1=t.sb_l[:, hs, :],
                                      op0=ALU.max, op1=ALU.add))
        for h in range(4 * half, 4 * half + 4):
            dve.tensor_tensor(t.sb_s[:, h, :], t.sb_s[:, h, :], t.sb_keep[:], ALU.mult).then_inc(s.sb_soft, 1)

    def arguments_of(half):
        for h in range(4 * half, 4 * half + 4):
            bank, done = out_of(r1, f"c{h}")
            dve.tensor_tensor(t.z[:, h, :], t.z[:, h, :], bank[:, 0:384], ALU.subtract).then_inc(done, 1)
        dve.wait_ge(*r1.drained(f"c{4 * half + 3}"))
        for h in range(4 * half, 4 * half + 4):
            ins = dve.tensor_tensor(t.z[:, h, :], t.z[:, h, :], t.sb_cap[:], ALU.min)
            if h % 4 < 3:
                step(ins)
        ins.then_inc(s.sb_arg, 1)

    dve.wait_ge(s.consts, 1)
    softplus_of(0)
    for b in range(NB):
        bank, done = out_of(r1, f"gv{b}")
        dve.tensor_copy(t.g_v[:, b, :], bank[:]).then_inc(done, 1)
    bank, done = out_of(r1, "ga")
    dve.tensor_copy(t.ga_T[0:RANK, :], bank[0:RANK, 0:T]).then_inc(done, 1)
    softplus_of(1)
    bank, done = two(r1, "al")
    step(dve.tensor_scalar(t.a_pre[:, 0, :], bank[:, 0, :], vec(t, "b_alpha", 0), None, ALU.add))
    dve.tensor_scalar(t.a_pre[:, 1, :], bank[:, 1, :], vec(t, "b_alpha", 1), None, ALU.add).then_inc(done, 1)
    arguments_of(0)

    dve.wait_ge(s.al_log, 1)
    dve.wait_ge(*r1.drained("al"))
    step(dve.tensor_scalar(t.a_pre[:], t.a_pre[:], -1.0, 0.0, ALU.mult, ALU.max))
    step(dve.tensor_tensor(t.a_pre[:], t.a_pre[:], t.al_l[:], ALU.add))
    for k in range(2):
        step(dve.tensor_tensor_scan(t.cum[:, k, :], t.chunk_start[:], t.a_pre[:, k, :], 0.0, ALU.mult, ALU.add))
    for k in range(2):
        by_chunk = t.cum[:, k, :].rearrange("p (c n) -> p c n", n=CH)
        ends = t.cum[:, k, CH - 1:T:CH]
        ins = dve.tensor_tensor(t.cum_end[:, k, :].rearrange("p (c n) -> p c n", n=CH), by_chunk, spread(ends, CH),
                                ALU.subtract)
        if k == 0:
            step(ins)
    ins.then_inc(s.gla_cum, 1)
    dve.wait_ge(s.gla_exp, 3)
    for k in range(2):
        step(dve.tensor_copy(t.chunk_decay[:, k, :], t.dec_q[:, k, CH - 1:T:CH]))
    dve.tensor_tensor(t.dec_q[:], t.g_q[:], t.dec_q[:], ALU.mult).then_inc(s.gla_dec, 1)
    dve.tensor_tensor(t.dec_k[:], t.g_k[:], t.dec_k[:], ALU.mult).then_inc(s.gla_dec, 1)
    dve.tensor_tensor(t.dec_e[:], t.g_k[:], t.dec_e[:], ALU.mult).then_inc(s.gla_dec, 1)
    arguments_of(1)

    def sigmoids(ap):
        step(dve.tensor_scalar(ap, ap, 1.0, None, ALU.add))
        step(dve.reciprocal(ap, ap))

    dve.wait_ge(*r1.drained("gr1"))
    sigmoids(t.gr_e[:])
    for f in range(4):
        step(dve.scalar_tensor_tensor(out=t.gr[:, f, :], in0=t.gr[:, f, :], scalar=vec(t, "gla_g", f),
                                      in1=t.gr_e[:, f, :], op0=ALU.mult, op1=ALU.mult))

    def sb_out(n):
        bank, done = two(r1, f"o{n}")
        dve.tensor_copy(t.o_sb[:, 2 * n:2 * n + 2, :], bank).then_inc(done, 1)

    sb_out(0)
    for c in range(3):
        if c < 2:
            bank, done = out_of(r1, f"ds{c}")
        else:
            bank = r1.bank("ds0")
        for h in range(GLA_H):
            rows, k = slice(GLA_DK * (h % 2), GLA_DK * (h % 2) + GLA_DK), h // 2
            c0 = (k * 2 + c // 2) * GLA_DV
            part, dst = bank[rows, c0:c0 + GLA_DV], t.state[rows, k, c, h % 2, :]
            if c == 0:
                ins = dve.tensor_copy(dst, part)
            else:
                ins = dve.scalar_tensor_tensor(out=dst, in0=t.state[rows, k, c - 1, h % 2, :],
                                               scalar=t.chunk_decay[rows, k, c:c + 1], in1=part, op0=ALU.mult,
                                               op1=ALU.add)
            if (c, h) in ((1, 3), (2, 3)):
                ins.then_inc(s.drained_dve, 1)
                dve.wait_ge(s.drained_dve, r1.drained(f"ds{c - 1}")[1])
            else:
                step(ins)
    sb_out(1)
    dve.wait_ge(*r1.drained("og1"))
    o_heads = t.o_gla.rearrange("p b (h n) -> p (b h) n", h=GLA_H)
    on_heads = t.o_n.rearrange("p b (h n) -> p (b h) n", h=GLA_H)
    step(dve.tensor_tensor(t.o_n, t.o_gla, t.o_gla, ALU.mult))
    step(dve.tensor_reduce(t.msq[:, NORM_AT["gla"], 0:8], on_heads, X, ALU.add))
    finish_mean("gla", [GLA_DV] * 8)
    dve.wait_ge(*r1.drained("gate7"))
    sigmoids(t.gates[:])
    have_rstd("gla")
    dve.tensor_tensor(on_heads, o_heads, spread(t.rstd[:, NORM_AT["gla"], 0:8], GLA_DV),
                      ALU.mult).then_inc(s.o_n_ready, 1)
    for n in range(2):
        bank, done = two(r1, f"ogt{n}")
        dve.tensor_tensor(t.o_glaT[:, 2 * n:2 * n + 2, :], bank, t.gr[:, 2 * n:2 * n + 2, :], ALU.mult).then_inc(done, 1)
    for f in range(KT):
        bank, done = two(r1, f"y{f}")
        y_a, y_b = t.gr_e[:, 2 * (f % 2), :], t.gr_e[:, 2 * (f % 2) + 1, :]
        if f >= 2:
            dve.wait_ge(s.y_ready, f - 1)
        step(dve.tensor_tensor(y_a, bank[:, 0, :], t.gates[:, f, :], ALU.mult))
        dve.tensor_tensor(y_b, bank[:, 1, :], t.gates[:, KT + f, :], ALU.mult).then_inc(done, 1)
        dve.wait_ge(*r1.drained(f"y{f}"))
        dve.tensor_tensor(t.y_T[:, f, :], y_a, y_b, ALU.add).then_inc(s.y_ready, 1)
    for n in range(2):
        for b in range(NB):
            bank, done = out_of(r1, f"wo{n}{b}")
            cols = slice(512 * n, 512 * n + 512)
            dve.tensor_tensor(t.h[:, b, cols], t.h[:, b, cols], bank[:], ALU.add).then_inc(done, 1)
    dve.wait_ge(*r1.drained("wo11"))
    mean_squares("ffn", [(t.h[:, b, :], t.x_n[:, b, :], D) for b in range(NB)])
    have_rstd("ffn")
    for b in range(NB):
        dve.tensor_scalar(t.x_n[:, b, :], t.h[:, b, :], rstd("ffn", b), None, ALU.mult).then_inc(s.x_n_ready, 1)
    step(dve.memset(t.a_pad[:, 0], 0.0))
    dve.memset(t.a_pad[:, 1], 0.0).then_inc(s.ff_zero, 1)
    turned(r1, "hT", t.h_nT, "norm_ffn")

    conv_b = VEC_A["conv_b"]

    def ffn(i, q):
        per = 6
        local = Steps(dve, s.ff_dve_step, i * per)
        dve.wait_ge(s.ff_pad, i + 1)
        for k in range(2):
            src, dst = t.a_pad[:, q, k, :], t.ff_c[:, q, k, :]
            tap = [t.vec_T[:, bass.ds(i * 2 + (VEC_A["conv_w"] + x * (D_FF // P) + k), 1)] for x in range(3)]
            bias = t.vec_T[:, bass.ds(i * 2 + (conv_b + k), 1)]
            local(dve.tensor_scalar(dst, src[:, 0:T], tap[0], bias, ALU.mult, ALU.add))
            local(dve.scalar_tensor_tensor(out=dst, in0=src[:, 1:T + 1], scalar=tap[1], in1=dst, op0=ALU.mult, op1=ALU.add))
            ins = dve.scalar_tensor_tensor(out=dst, in0=src[:, 2:T + 2], scalar=tap[2], in1=dst, op0=ALU.mult, op1=ALU.add)
            local(ins)
        dve.sem_inc(s.ff_conv, 1)
        dve.wait_ge(s.ff_gelu, i + 1)
        dve.wait_ge(s.ff_g, i + 1)
        dve.wait_ge(s.ff_o, i - 1 if not isinstance(i, int) else max(i - 1, 0))
        dve.tensor_tensor(t.ff_u[:, q], t.ff_ge[:, q], g.banks[6 + q][:].rearrange("p (k n) -> p k n", k=2),
                          ALU.mult).then_inc(s.ff_u, 1)
        assert local.n == per

    ffn(0, 0)
    with dve.Fori(0, (FF_STEPS - 1) // 2) as m:
        ffn(m * 2 + 1, 1)
        ffn(m * 2 + 2, 0)

    dve.wait_ge(s.ff_o, FF_STEPS)
    for b in range(NB):
        for n in range(2):
            cols = slice(512 * n, 512 * n + 512)
            step(dve.tensor_tensor(t.h[:, b, cols], t.h[:, b, cols], g.banks[2 * b + n][:], ALU.add))
    mean_squares("end1", [(t.h[:, b, :], t.x_n[:, b, :], D) for b in range(NB)])
    have_rstd("end1")
    dve.wait_ge(s.small_in, 16 * 5)
    for b in range(NB):
        step(dve.scalar_tensor_tensor(out=t.h[:, b, :], in0=t.h[:, b, :], scalar=rstd("end1", b), in1=t.g_rows[:],
                                      op0=ALU.mult, op1=ALU.mult))

    mean_squares("attn", [(t.h[:, b, :], t.x_n[:, b, :], D) for b in range(NB)])
    have_rstd("attn")
    for b in range(NB):
        dve.tensor_scalar(t.x_n[:, b, :], t.h[:, b, :], rstd("attn", b), None, ALU.mult).then_inc(s.x_n_ready, 1)
    turned(r2, "nT", t.h_nT2, "attn_norm")

    dve.wait_ge(*r2.drained("lat1"))
    mean_squares("lat", [(t.lat[:, b, 0:QL], t.lat_n[:, b, 0:QL], QL) for b in range(NB)]
                 + [(t.lat[:, b, QL:QL + KVL], t.lat_n[:, b, QL:QL + KVL], KVL) for b in range(NB)])

    def rope(dst, src, heads, b):
        def table(n):
            ap = t.sin_cos[:, n, b, :]
            return ap if heads is None else ap.unsqueeze(1).to_broadcast([P, heads, HALF])
        sin, cos = table(0), table(1)
        x1, x2 = (src[..., 0:HALF], src[..., HALF:]) if heads is None else (src[:, :, 0:HALF], src[:, :, HALF:])
        d1, d2 = (dst[..., 0:HALF], dst[..., HALF:]) if heads is None else (dst[:, :, 0:HALF], dst[:, :, HALF:])
        tmp = [t.rope_tmp[:, i, 0:1, :].squeeze(1) if heads is None else t.rope_tmp[:, i] for i in range(4)]
        for i, (a, c) in enumerate(((x1, cos), (x2, sin), (x2, cos), (x1, sin))):
            step(dve.tensor_tensor(tmp[i], a, c, ALU.mult))
        step(dve.tensor_tensor(d1, tmp[0], tmp[1], ALU.subtract))
        step(dve.tensor_tensor(d2, tmp[2], tmp[3], ALU.add))

    dve.wait_ge(s.rope_ready, 1)
    for b in range(NB):
        rope(t.k_rope[:, b, :], t.lat[:, b, QL + KVL:], None, b)
    have_rstd("lat")
    for b in range(NB):
        dve.tensor_scalar(t.lat_n[:, b, 0:QL], t.lat[:, b, 0:QL], rstd("lat", b), None,
                          ALU.mult).then_inc(s.lat_ready, 1)
        dve.tensor_scalar(t.lat_n[:, b, QL:], t.lat[:, b, QL:QL + KVL], rstd("lat", NB + b), None,
                          ALU.mult).then_inc(s.lat_ready, 1)
    bank, done = two(r2, "qlT")
    dve.tensor_tensor(t.ql_T[:], bank, spread(vec(t, "g_q_a", 0, 2), T), ALU.mult).then_inc(done, 1)
    bank, done = out_of(r2, "kvT")
    dve.tensor_scalar(t.kv_T[:], bank[:, 0:T], vec(t, "g_kv_a"), None, ALU.mult).then_inc(done, 1)
    for b in range(NB):
        step(dve.tensor_copy(t.k_tok[:, b, :, NOPE:], t.k_rope[:, b, :].unsqueeze(1).to_broadcast([P, MH, ROPE])))
    dve.wait_ge(*r2.drained("qq11"))
    for b in range(NB):
        q = t.q_tok[:, b, :].rearrange("p (h x) -> p h x", h=MH)[:, :, NOPE:]
        rope(q, q, MH, b)
    dve.sem_inc(s.q_roped, 1)
    for n in range(4):
        bank, done = two(r2, f"kT{n}")
        dve.tensor_copy(t.k_T[0:QK, 2 * n:2 * n + 2, :], bank[0:QK]).then_inc(done, 1)
    dve.wait_ge(s.consts2, 1)
    for h in range(MH):
        bank, done = out_of(r2, f"s{h}")
        dve.scalar_tensor_tensor(out=t.score[:, h, :], in0=bank[:, 0:384], scalar=QK ** -0.5, in1=t.at_mask[:],
                                 op0=ALU.mult, op1=ALU.add).then_inc(done, 1)
        if h % 4 == 3:
            dve.wait_ge(*r2.drained(f"s{h}"))
            hs = slice(h - 3, h + 1)
            step(dve.tensor_reduce(t.row_m[:, hs, 0], t.score[:, hs, 0:P], X, ALU.max))
            step(dve.tensor_reduce(t.row_m[:, hs, 1], t.score[:, hs, P:], X, ALU.max))
            dve.tensor_scalar(t.row_m[:, hs, :], t.row_m[:, hs, :], -1.0, None, ALU.mult).then_inc(s.row_max, 1)
    dve.wait_ge(*r2.drained("pm1"))
    step(dve.tensor_tensor(t.y_pool[:], t.y_pool[:], spread(vec(t, "pool_scale", 0, 4), T), ALU.mult))
    dve.tensor_tensor(t.y_sq[:], t.y_pool[:], t.y_pool[:], ALU.mult).then_inc(s.pool_sq, 1)
    dve.wait_ge(s.pool_sq, 1)
    dve.tensor_tensor(t.y_pool[:], t.y_pool[:], spread(vec(t, "g_out_pool", 0, 4), T), ALU.mult).then_inc(s.pool_y, 1)
    dve.wait_ge(s.prob_ready, NB * MH)
    step(dve.reciprocal(t.row_l[:], t.row_l[:]))
    bank, done = out_of(r2, "pss")
    dve.tensor_copy(t.pool_sum[:], bank[:, 0:NB]).then_inc(done, 1)
    dve.wait_ge(*r2.drained("pss"))
    for b in range(NB):
        bank, done = out_of(r2, f"av{b}")
        dve.tensor_tensor(t.y_att[:, b, :].rearrange("p (h n) -> p h n", h=MH),
                          bank[:].rearrange("p (h n) -> p h n", h=MH), spread(t.row_l[:, :, b], VD),
                          ALU.mult).then_inc(done, 1)
    dve.wait_ge(*r2.drained("av1"))
    mean_squares("mla", [(t.y_att[:, b, :], t.y_attn[:, b, :], 512) for b in range(NB)])
    k = NORM_AT["pool"]
    dve.tensor_scalar(t.msq[:, k, 0:NB], t.pool_sum[:], 1.0 / 512, EPS, ALU.mult, ALU.add).then_inc(s.msq_ready, 1)
    have_rstd("mla")
    for b in range(NB):
        dve.tensor_scalar(t.y_attn[:, b, :], t.y_att[:, b, :], rstd("mla", b), None, ALU.mult).then_inc(s.y_attn_ready, 1)
    for b in range(NB):
        bank, done = out_of(r2, f"yt{b}")
        dve.tensor_tensor(t.ya_T[:, :, b * P:(b + 1) * P], bank[:].rearrange("p (k n) -> p k n", k=4),
                          spread(vec(t, "g_out_attn", 0, 4), P), ALU.mult).then_inc(done, 1)
    have_rstd("pool")
    for n in range(2):
        for b in range(NB):
            cols = slice(512 * n, 512 * n + 512)
            bank, done = out_of(r2, f"pa{n}{b}")
            dve.tensor_tensor(t.h[:, b, cols], t.h[:, b, cols], bank[:], ALU.add).then_inc(done, 1)
            dve.wait_ge(*r2.drained(f"pa{n}{b}"))
            bank, done = out_of(r2, f"pp{n}{b}")
            dve.scalar_tensor_tensor(out=t.h[:, b, cols], in0=bank[:], scalar=rstd("pool", b), in1=t.h[:, b, cols],
                                     op0=ALU.mult, op1=ALU.add).then_inc(done, 1)
    dve.wait_ge(*r2.drained("pp11"))
    mean_squares("moe", [(t.h[:, b, :], t.h_n[:, b, :], D) for b in range(NB)])
    have_rstd("moe")
    dve.wait_ge(s.late_in, 16)
    for b in range(NB):
        dve.scalar_tensor_tensor(out=t.h_n[:, b, :], in0=t.h[:, b, :], scalar=rstd("moe", b), in1=t.g_rows[:],
                                 op0=ALU.mult, op1=ALU.mult).then_inc(s.h_ready, 1)

    bank, done = out_of(r2, "lg")
    dve.tensor_tensor(t.logits[:], bank[:, 0:NB * E].rearrange("p (b e) -> p b e", b=NB),
                      t.b_router[:].unsqueeze(1).to_broadcast([P, NB, E]), ALU.add).then_inc(done, 1)
    dve.wait_ge(*r2.drained("lg"))
    iota_e = t.iota_f[:, 0:E]
    for b in range(NB):
        step(dve.max(t.top[:], t.logits[:, b, :]))
        step(dve.max_index(t.top_i[:], t.top[:], t.logits[:, b, :]))
        step(dve.tensor_copy(t.top_f[:], t.top_i[:, 0:TOPK]))
        step(dve.tensor_scalar(t.top_e[:], t.top[:, 0:TOPK], t.top[:, 0:1], None, ALU.subtract))
        dve.sem_inc(s.top_ready, 1)
        dve.wait_ge(s.top_exp, b + 1)
        step(dve.reciprocal(t.top_s[:], t.top_s[:]))
        step(dve.tensor_scalar(t.top_e[:], t.top_e[:], t.top_s[:], None, ALU.mult))
        for k in range(TOPK):
            step(dve.tensor_scalar(t.one_hot[:, k, :], iota_e, t.top_f[:, k:k + 1], None, ALU.is_equal))
        step(dve.tensor_reduce(t.mask[:, b, :], t.one_hot[:].rearrange("p k e -> p e k"), X, ALU.add))
        for k in range(TOPK):
            step(dve.tensor_scalar(t.one_hot[:, k, :], iota_e, t.top_f[:, k:k + 1], t.top_e[:, k:k + 1],
                                   ALU.is_equal, ALU.mult))
        step(dve.tensor_reduce(t.gate_e[:, b, :], t.one_hot[:].rearrange("p k e -> p e k"), X, ALU.add))
    dve.sem_inc(s.mask_ready, 1)
    bank, done = out_of(r2, "rk")
    rank = bank[:, 0:NB * E].rearrange("p (b e) -> p b e", b=NB)
    step(dve.tensor_scalar(t.count[:], bank[:, NB * E:NB * E + E], 1.0, None, ALU.mult))
    dve.scalar_tensor_tensor(out=t.pos_e[:], in0=rank, scalar=1000.0, in1=t.mask[:], op0=ALU.add,
                             op1=ALU.mult).then_inc(done, 1)
    dve.wait_ge(*r2.drained("rk"))
    step(dve.tensor_scalar(t.pos_e[:], t.pos_e[:], -1000.0, None, ALU.add))
    step(dve.tensor_scalar(t.over[:], t.count[:], float(SLOTS), None, ALU.is_gt))
    for n in (2, 3):
        step(dve.scalar_tensor_tensor(out=t.over[:], in0=t.count[:], scalar=float(n * SLOTS), in1=t.over[:],
                                      op0=ALU.is_gt, op1=ALU.add))
    step(dve.memset(t.first_over[:], 1.0))
    step(dve.tensor_tensor_scan(t.end_over[:], t.first_over[:], t.over[:], 0.0, ALU.mult, ALU.add))
    step(dve.tensor_tensor(t.first_over[:], t.end_over[:], t.over[:], ALU.subtract))
    m_shape = [P, OVER + 1, E]
    m_iota = spread(t.iota_f[:, 0:OVER + 1], E)

    def per_job(ap):
        return ap.unsqueeze(1).to_broadcast(m_shape)

    step(dve.tensor_tensor(t.sel, m_iota, per_job(t.first_over[:]), ALU.is_ge))
    step(dve.tensor_tensor(t.sel_tmp, m_iota, per_job(t.end_over[:]), ALU.is_lt))
    step(dve.tensor_tensor(t.sel, t.sel, t.sel_tmp, ALU.mult))

    def choose(dst, values):
        step(dve.tensor_tensor(t.sel_tmp, t.sel, per_job(values), ALU.mult))
        step(dve.tensor_reduce(dst, t.sel_tmp, X, ALU.add))

    step(dve.tensor_copy(t.job_e[:, 0:E], iota_e))
    choose(t.job_e[:, E:], iota_e)
    for b in range(NB):
        step(dve.tensor_copy(t.job_pos[:, b, 0:E], t.pos_e[:, b, :]))
        step(dve.tensor_copy(t.job_gate[:, b, 0:E], t.gate_e[:, b, :]))
        choose(t.job_gate[:, b, E:], t.gate_e[:, b, :])
        step(dve.scalar_tensor_tensor(out=t.pos_e[:, b, :], in0=t.first_over[:], scalar=float(SLOTS),
                                      in1=t.pos_e[:, b, :], op0=ALU.mult, op1=ALU.add))
        choose(t.job_pos[:, b, E:], t.pos_e[:, b, :])
        step(dve.scalar_tensor_tensor(out=t.job_pos[:, b, E:], in0=t.iota_f[:, 1:OVER + 2], scalar=-float(SLOTS),
                                      in1=t.job_pos[:, b, E:], op0=ALU.mult, op1=ALU.add))
    step(dve.tensor_scalar(t.job_sel[0:64, :], t.job_e[0:64, :], t.part32[0:64, :], None, ALU.is_equal))
    step(dve.tensor_copy(t.job_expert[0:1, :], t.job_e[0:1, :]))
    step(dve.tensor_scalar(t.count[0:1, 0:1], t.end_over[0:1, E - 1:E], float(E - 1), None, ALU.add))
    dve.tensor_copy(t.job_count[0:1, 0:1], t.count[0:1, 0:1]).then_inc(s.jobs_ready, 1)

    dve.wait_ge(s.jobs_ready, 1)
    dve.wait_ge(s.x_split, 1)
    dve.wait_ge(s.h_ready, NB)
    dve.tensor_tensor(t.x_lo[:], t.h_n[:], t.x_hi[:].bitcast(F32), ALU.subtract).then_inc(s.x_split, 1)
    dve.wait_ge(s.bias_hi, 1)
    dve.tensor_tensor(t.bias_hl[32:64, :], t.bias_raw[32:64, :], t.bias_hl[32:64, :].bitcast(F32),
                      ALU.subtract).then_inc(s.bias_ready, 1)

    def pick(j):
        for b in range(NB):
            dve.tensor_scalar(t.picks[:, b, :], t.iota_s[:, 0:SLOTS], t.job_pos[:, b, bass.ds(j, 1)], None,
                              ALU.is_equal).then_inc(s.picked, 1)

    def pick_bias(j):
        dve.tensor_scalar(t.bias_sel[0:64, :], t.bias_col[0:64, :], t.job_sel[0:64, bass.ds(j, 1)], None,
                          ALU.mult).then_inc(s.bias_picked, 1)

    pick(0)
    pick_bias(0)
    dve.sem_inc(s.summed, 2)
    last = dve.value_load(t.job_count[0:1, 0:1], min_val=E - 1, max_val=E + OVER - 1)
    with dve.Fori(0, last + 1) as j:
        own = Steps(dve, s.job_dve_step, j * JOB_DVE_STEPS)

        def lo(c):
            dve.wait_ge(s.hi_done, j * JC + (c + 1))
            dve.tensor_tensor(t.w_lo[:, c % SPLIT, :], t.ring[:, (g.n_moe + c) % RING, :],
                              t.w_hi[:, c % SPLIT, :].bitcast(F32), ALU.subtract).then_inc(s.lo_dve, 1)

        def add_rows(q, dst):
            dve.wait_ge(s.lo_rows_ready, j * 4 + q + 1)
            dve.tensor_tensor(dst, g.banks[4 + q % 2][0:SLOTS, :], t.lo_rows[0:SLOTS, q % 2, :],
                              ALU.add).then_inc(s.summed, 1)
            dve.wait_ge(s.summed, j * 4 + q + 1 + 2)

        def swiglu_gate(half):
            add_rows(2 * half, t.gate[0:SLOTS, :])
            dve.tensor_scalar(t.gate[0:SLOTS, :], t.gate[0:SLOTS, :], SWIGLU_LIMIT, None,
                              ALU.min).then_inc(s.gate_ready, 1)

        def swiglu_up(half):
            up, res = t.up[0:SLOTS, :], t.act[0:SLOTS, half, :]
            add_rows(2 * half + 1, up)
            dve.wait_ge(s.gate_ready, j * 2 + half + 1)
            own(dve.tensor_scalar(up, up, SWIGLU_LIMIT, -SWIGLU_LIMIT, ALU.min, ALU.max))
            own(dve.scalar_tensor_tensor(out=up, in0=up, scalar=1.0, in1=t.gate[0:SLOTS, :], op0=ALU.add, op1=ALU.mult))
            dve.wait_ge(s.sig_ready, j * 2 + half + 1)
            dve.tensor_tensor(res, up, t.sig[0:SLOTS, :], ALU.mult).then_inc(s.act_ready, 1)

        def act_lo(half):
            dve.wait_ge(s.act_hi, j * 2 + half + 1)
            fs = slice(4 * half, 4 * half + 4)
            dve.tensor_tensor(t.act_T[:, fs, SLOTS:],
                              g.banks[7][:, 256 * half:256 * half + 256].rearrange("p (k n) -> p k n", k=4),
                              t.act_T[:, fs, 0:SLOTS].bitcast(F32), ALU.subtract).then_inc(s.act_lo, 1)

        dve.wait_ge(s.act_ready, j * 2)
        lo(0)
        lo(1)
        dve.wait_ge(s.weights_turned, j)
        for b in range(NB):
            dve.tensor_scalar(t.mix_in[:, b, :], t.iota_s[:], t.job_pos[:, b, bass.ds(j, 1)],
                              t.job_gate[:, b, bass.ds(j, 1)], ALU.is_equal, ALU.mult).then_inc(s.mix_in_ready, 1)
        dve.wait_ge(s.gathered, j * 2 + 2)
        pick(j + 1)
        lo(3)
        swiglu_gate(0)
        lo(4)
        lo(5)
        swiglu_up(0)
        lo(7)
        dve.wait_ge(s.act_ready, j * 2 + 1)
        swiglu_gate(1)
        lo(8)
        lo(9)
        swiglu_up(1)
        pick_bias(j + 1)
        act_lo(0)
        lo(11)
        act_lo(1)
        assert own.n == JOB_DVE_STEPS

    dve.wait_ge(s.closed, 1)
    for b in range(NB):
        for n in range(2):
            cols = slice(512 * n, 512 * n + 512)
            step(dve.tensor_tensor(t.h[:, b, cols], t.h[:, b, cols], g.banks[2 * b + n][:], ALU.add))
    mean_squares("end2", [(t.h[:, b, :], t.h_n[:, b, :], D) for b in range(NB)])
    have_rstd("end2")
    dve.wait_ge(s.end_in, 16)
    for b in range(NB):
        dve.scalar_tensor_tensor(out=t.h[:, b, :], in0=t.h[:, b, :], scalar=rstd("end2", b), in1=t.g_rows[:],
                                 op0=ALU.mult, op1=ALU.mult).then_inc(s.out_ready, 1)


JOB_DVE_STEPS = 4


def tensor_program(g, pe):
    s, t, r1, r2, banks = g.s, g.t, g.r1, g.r2, g.banks

    def open_bank(r, name):
        room = r.room(name)
        if room is not None:
            pe.wait_ge(*room)
        return r.bank(name)

    def landed(n):
        slot, value = slot_use(n)
        pe.wait_ge(s.landed[slot], value)

    def halves(n, m):
        return [chunk(g, n + k // 4, (4, m))[:, k % 4, :] for k in range(KT)]

    def turn(r, prefix, src):
        for b in range(NB):
            for h in range(2):
                bank = open_bank(r, f"{prefix}{b}{h}")
                for k in range(4):
                    f = 4 * h + k
                    ins = pe.transpose(bank[:, k * P:(k + 1) * P], src[:, b, f * P:(f + 1) * P], t.ident[:])
                ins.then_inc(r.s.filled, 1)

    def project_T(r, names, weights, src, f0=0):
        for i, name in enumerate(names):
            bank = open_bank(r, name)
            for j in range(2):
                f = f0 + 2 * i + j
                for k, wk in enumerate(weights):
                    ins = pe.matmul(bank[:, j * T:(j + 1) * T], wk[:, f * P:(f + 1) * P], src[:, k, :],
                                    start=(k == 0), stop=(k == len(weights) - 1))
            ins.then_inc(r.s.filled, 1)

    def project(r, name, b, weights, src, c0, n):
        bank = open_bank(r, name)
        for k, wk in enumerate(weights):
            ins = pe.matmul(bank[:, 0:n], src[:, k, b * P:(b + 1) * P], wk[:, c0:c0 + n], start=(k == 0),
                            stop=(k == len(weights) - 1))
        ins.then_inc(r.s.filled, 1)

    pe.wait_ge(s.early_consts, 1)
    pe.wait_ge(s.vec_in, 16 * (len(VEC_A) + len(VEC_B)))
    bank = open_bank(r1, "vec")
    pe.transpose(bank[:, 0:ROWS_A], t.vec_a[0:ROWS_A, :], t.ident[0:ROWS_A, 0:ROWS_A])
    pe.transpose(bank[:, P:P + ROWS_B], t.vec_b[0:ROWS_B, :], t.ident[0:ROWS_B, 0:ROWS_B]).then_inc(s.filled, 1)
    pe.wait_ge(s.x_n_ready, NB)
    turn(r1, "xT", t.x_n)
    pe.wait_ge(*r1.drained("xT11"))

    def w_in(n):
        landed(n)
        landed(n + 1)
        return halves(n, 512)

    project_T(r1, ["sbq0", "sbq1"], w_in(0), t.x_nT)
    project_T(r1, ["sbk0", "sbk1"], w_in(2), t.x_nT)
    wv = w_in(4)
    for b in range(NB):
        project(r1, f"sbv{b}", b, wv, t.x_nT, 0, 512)

    def head_scores(h):
        bank = open_bank(r1, f"z{h}")
        rows = slice(SB_D * (h % 2), SB_D * (h % 2) + SB_D)
        k, q = t.sb_k[rows, h // 2, :], t.sb_q[rows, h // 2, :]
        pe.matmul(bank[:, 0:T], k[:, 0:P], q, start=True, stop=True)
        pe.matmul(bank[:, T:T + P], k[:, P:], q[:, P:], start=True, stop=True).then_inc(s.filled, 1)

    pe.wait_ge(*r1.drained("sbk1"))
    for h in range(4):
        head_scores(h)
    project_T(r1, ["gq", "gk"], w_in(6), t.x_nT)
    for h in range(4, 8):
        head_scores(h)
    wv = w_in(8)
    for b in range(NB):
        project(r1, f"gv{b}", b, wv, t.x_nT, 0, 512)
    pe.wait_ge(s.small_in, 16 * 5)
    bank = open_bank(r1, "ga")
    for k in range(KT):
        ins = pe.matmul(bank[0:RANK, 0:T], t.w_ga[:, k, :], t.x_nT[:, k, :], start=(k == 0), stop=(k == KT - 1))
    ins.then_inc(s.filled, 1)
    project_T(r1, ["gr0", "gr1"], w_in(10), t.x_nT)
    pe.wait_ge(*r1.drained("ga"))
    project_T(r1, ["al"], [t.w_alpha[0:RANK, :]], t.ga_T[0:RANK, :].unsqueeze(1))

    def key_sums(h):
        pe.wait_ge(s.sb_soft, h + 1)
        bank = open_bank(r1, f"c{h}")
        sp = t.sb_s[:, h, :]
        pe.matmul(bank[:, 0:T], t.tri[:], sp[:, 0:T], start=True, stop=False)
        pe.matmul(bank[:, P:T], t.ones[:], sp[:, T:], start=False, stop=True)
        pe.matmul(bank[:, T:T + P], t.tri[:], sp[:, T:], start=True, stop=True).then_inc(s.filled, 1)

    def sb_outputs(n):
        pe.wait_ge(s.sb_w, n + 1)
        bank = open_bank(r1, f"o{n}")
        for h in range(4 * n, 4 * n + 4):
            rows, c0 = slice(SB_D * (h % 2), SB_D * (h % 2) + SB_D), T * (h // 2 % 2)
            v, wt = t.sb_v[:, :, SB_D * h:SB_D * (h + 1)], t.sb_l[:, h, :]
            pe.matmul(bank[rows, c0:c0 + T], v[:, 0, :], wt[:, 0:T], start=True, stop=False)
            ins = pe.matmul(bank[rows, c0 + P:c0 + T], v[:, 1, :], wt[:, T:], start=False, stop=True)
        ins.then_inc(s.filled, 1)

    for h in range(4):
        key_sums(h)
    for q in range(2):
        project_T(r1, [f"gate{2 * q}", f"gate{2 * q + 1}"], w_in(12 + 2 * q), t.x_nT)
    for h in range(4, 8):
        key_sums(h)
    pe.wait_ge(s.gla_dec, 3)
    bank = open_bank(r1, "kend")
    for b in range(NB):
        for k in range(2):
            ins = pe.transpose(bank[:, (2 * b + k) * P:(2 * b + k + 1) * P], t.dec_e[:, k, b * P:(b + 1) * P], t.ident[:])
    ins.then_inc(s.filled, 1)

    def gla_rows(h):
        return slice(GLA_DK * (h % 2), GLA_DK * (h % 2) + GLA_DK)

    def chunk_rows(c):
        return slice(CH * (c % 2), CH * (c % 2) + CH)

    for n in range(2):
        bank = open_bank(r1, f"att{n}")
        for m, (h, b) in enumerate((h, b) for h in (n, n + 2) for b in range(NB)):
            toks = slice(b * P, (b + 1) * P)
            ins = pe.matmul(bank[:, m * P:(m + 1) * P], t.dec_k[gla_rows(h), h // 2, toks],
                            t.dec_q[gla_rows(h), h // 2, toks], start=True, stop=True)
        ins.then_inc(s.filled, 1)
    sb_outputs(0)
    for q in range(2, 4):
        project_T(r1, [f"gate{2 * q}", f"gate{2 * q + 1}"], w_in(12 + 2 * q), t.x_nT)
    pe.wait_ge(*r1.drained("kend"))
    for n, cs in enumerate(((0, 2), (1,))):
        bank = open_bank(r1, f"ds{n}")
        for h in range(GLA_H):
            for c in cs:
                c0 = (h // 2 * 2 + c // 2) * GLA_DV
                ins = pe.matmul(bank[gla_rows(h), c0:c0 + GLA_DV],
                                t.k_end[chunk_rows(c), c // 2, GLA_DK * h:GLA_DK * (h + 1)],
                                t.g_v[chunk_rows(c), c // 2, GLA_DV * h:GLA_DV * (h + 1)], start=True, stop=True)
        ins.then_inc(s.filled, 1)
    sb_outputs(1)
    pe.wait_ge(s.att_masked, 2)
    pe.wait_ge(*r1.drained("ds1"))
    for b in range(NB):
        bank = open_bank(r1, f"og{b}")
        for k in range(2):
            for h in (2 * k, 2 * k + 1):
                ins = pe.matmul(bank[:, GLA_DV * h:GLA_DV * (h + 1)], t.att[:, 4 * (h % 2) + 2 * k + b, :],
                                t.g_v[:, b, GLA_DV * h:GLA_DV * (h + 1)], start=(h == 0), stop=False,
                                skip_group_check=True)
            for c in (2 * b, 2 * b + 1):
                if c > 0:
                    ins = pe.matmul(bank[chunk_rows(c), 2 * GLA_DV * k:2 * GLA_DV * (k + 1)],
                                    t.dec_q[:, k, CH * c:CH * c + CH],
                                    t.state[:, k, c - 1].rearrange("p h n -> p (h n)"), start=False, stop=(c % 2 == 1),
                                    skip_group_check=True)
        ins.then_inc(s.filled, 1)
    pe.wait_ge(s.o_n_ready, 1)
    for n in range(2):
        bank = open_bank(r1, f"ogt{n}")
        for h in (2 * n, 2 * n + 1):
            for b in range(NB):
                c0 = (h % 2) * T + b * P
                ins = pe.transpose(bank[:, c0:c0 + P], t.o_n[:, b, GLA_DV * h:GLA_DV * (h + 1)], t.ident[:])
        ins.then_inc(s.filled, 1)
    pe.wait_ge(*r1.drained("ogt1"))
    for f in range(KT):
        n = 20 + 2 * (f // 4)
        landed(n)
        landed(n + 1)
        bank = open_bank(r1, f"y{f}")
        cols = slice(P * (f % 4), P * (f % 4) + P)
        for q, src in enumerate((t.o_sb, t.o_glaT)):
            for k in range(4):
                ins = pe.matmul(bank[:, q * T:(q + 1) * T], chunk(g, n + q, (4, 512))[:, k, cols], src[:, k, :],
                                start=(k == 0), stop=(k == 3))
        ins.then_inc(s.filled, 1)
    pe.wait_ge(s.y_ready, KT)
    for n in range(2):
        wo = w_in(24 + 2 * n)
        for b in range(NB):
            project(r1, f"wo{n}{b}", b, wo, t.y_T, 0, 512)
    pe.wait_ge(s.x_n_ready, 2 * NB)
    turn(r1, "hT", t.x_n)

    pe.wait_ge(*r1.drained("hT11"))
    for n in range(4):
        pe.matmul(banks[n][:], t.zrow[0:1, 0:P], t.zrow[0:1, P:], start=True, stop=False)

    def ffn_landed(n, turns):
        slot, value = slot_use(n)
        pe.wait_ge(s.landed[slot], turns * 16 + value)

    def ffn_in(n, turns, bank, done):
        ffn_landed(n, turns)
        wt = t.ring[:, n % RING, :].rearrange("p (k m) -> p k m", k=KT)
        for f in range(2):
            for k in range(KT):
                ins = pe.matmul(bank[:, f * T:(f + 1) * T], wt[:, k, f * P:(f + 1) * P], t.h_nT[:, k, :],
                                start=(k == 0), stop=(k == KT - 1))
        ins.then_inc(done, 1)

    def ffn_out(n, turns, i, q, end=False):
        ffn_landed(n, turns)
        pe.wait_ge(s.ff_u, i + 1)
        wt = t.ring[:, n % RING, :].rearrange("p (k m) -> p k m", k=2)
        for b in range(NB):
            for c in range(2):
                for k in range(2):
                    ins = pe.matmul(banks[2 * b + c][:], t.ff_u[:, q, k, b * P:(b + 1) * P],
                                    wt[:, k, 512 * c:512 * c + 512], start=False, stop=end and k == 1,
                                    skip_group_check=not (end and k == 1))
        ins.then_inc(s.ff_o, 1)

    n0 = g.n_ffn
    ffn_in(n0, 0, banks[4], s.ff_a)
    ffn_in(n0 + 1, 0, banks[6], s.ff_g)
    with pe.Fori(0, (FF_STEPS - 1) // 2) as m:
        for q in range(2):
            i, n = m * 2 + (q + 1), n0 + 2 + 3 * q
            if q == 0:
                pe.wait_ge(s.ff_pad, m * 2)
            else:
                pe.wait_ge(s.ff_pad, m * 2 + 1)
            ffn_in(n, m, banks[5 - q], s.ff_a)
            ffn_out(n + 1, m, m * 2 + q, q)
            ffn_in(n + 2, m, banks[7 - q], s.ff_g)
    ffn_out(n0 + 3 * FF_STEPS - 1, 0, FF_STEPS - 1, 0, end=True)

    pe.wait_ge(s.x_n_ready, 3 * NB)
    turn(r2, "nT", t.x_n)
    pe.wait_ge(*r2.drained("nT11"))
    n = g.n_second
    landed(n)
    landed(n + 1)
    wl = halves(n, 416)
    for b in range(NB):
        project(r2, f"lat{b}", b, wl, t.h_nT2, 0, 416)
    landed(n + 2)
    landed(n + 3)
    project_T(r2, ["u0", "u1"], halves(n + 2, 512), t.h_nT2)
    pe.wait_ge(s.lat_ready, 2 * NB)
    bank = open_bank(r2, "qlT")
    for k in range(2):
        for b in range(NB):
            ins = pe.transpose(bank[:, k * T + b * P:k * T + (b + 1) * P], t.lat_n[:, b, k * P:(k + 1) * P], t.ident[:])
    ins.then_inc(s.filled2, 1)
    bank = open_bank(r2, "kvT")
    for b in range(NB):
        ins = pe.transpose(bank[:, b * P:(b + 1) * P], t.lat_n[:, b, QL:QL + KVL], t.ident[:])
    ins.then_inc(s.filled2, 1)
    landed(n + 4)
    pe.wait_ge(*r2.drained("qlT"))
    wq = chunk(g, n + 4, (2, 768))
    for b in range(NB):
        for c in range(2):
            project(r2, f"qq{b}{c}", b, [wq[:, k, :] for k in range(2)], t.ql_T, 384 * c, 384)
    landed(n + 5)
    pe.wait_ge(*r2.drained("kvT"))
    wkv = chunk(g, n + 5, (1, 1024))
    for b in range(NB):
        for c in range(2):
            project(r2, f"kv{b}{c}", b, [wkv[:, 0, :]], t.kv_T[:].unsqueeze(1), 512 * c, 512)
    pe.wait_ge(s.q_roped, 1)
    pe.wait_ge(*r2.drained("kv11"))
    for prefix, src in (("qT", [t.q_tok[:, b, :].rearrange("p (h x) -> p h x", h=MH) for b in range(NB)]),
                        ("kT", [t.k_tok[:, b] for b in range(NB)])):
        for m in range(4):
            bank = open_bank(r2, f"{prefix}{m}")
            for h in (2 * m, 2 * m + 1):
                for b in range(NB):
                    c0 = (h % 2) * T + b * P
                    ins = pe.transpose(bank[0:QK, c0:c0 + P], src[b][:, h, :], t.ident[:])
            ins.then_inc(s.filled2, 1)
    pe.wait_ge(*r2.drained("qT3"))
    pe.wait_ge(*r2.drained("kT3"))
    for h in range(MH):
        bank = open_bank(r2, f"s{h}")
        pe.matmul(bank[:, 0:P], t.q_T[0:QK, h, 0:P], t.k_T[0:QK, h, 0:P], start=True, stop=True)
        pe.matmul(bank[:, P:3 * P], t.q_T[0:QK, h, P:], t.k_T[0:QK, h, :], start=True, stop=True).then_inc(s.filled2, 1)
    landed(n + 6)
    pe.wait_ge(s.diff_ready, 1)
    w_pool = chunk(g, n + 6, (4, P))
    for m in range(2):
        bank = open_bank(r2, f"pm{m}")
        for i in range(2):
            ins = pe.matmul(bank[:, i * T:(i + 1) * T], w_pool[:, 2 * m + i, :], t.diff[:, 2 * m + i, :],
                            start=True, stop=True)
        ins.then_inc(s.filled2, 1)
    pe.wait_ge(s.pool_sq, 1)
    bank = open_bank(r2, "pss")
    for b in range(NB):
        for k in range(4):
            ins = pe.matmul(bank[:, b:b + 1], t.y_sq[:, k, b * P:(b + 1) * P], t.ones[:, 0:1], start=(k == 0), stop=(k == 3))
    ins.then_inc(s.filled2, 1)
    for h in range(MH):
        pe.wait_ge(s.prob_ready, NB * (h + 1))
        bank = open_bank(r2, f"pt{h}")
        for k in range(3):
            ins = pe.transpose(bank[:, k * P:(k + 1) * P], t.score[:, h, k * P:(k + 1) * P], t.ident[:])
        ins.then_inc(s.filled2, 1)
    pe.wait_ge(*r2.drained("pt7"))
    for b in range(NB):
        bank = open_bank(r2, f"av{b}")
        for h in range(MH):
            dst = bank[:, VD * h:VD * (h + 1)]
            for k in range(b + 1):
                c0 = (b + k) * P
                ins = pe.matmul(dst, t.prob_T[:, h, c0:c0 + P], t.v_tok[:, k, h, :], start=(k == 0), stop=(k == b))
        ins.then_inc(s.filled2, 1)
    for b in range(NB):
        pe.wait_ge(s.y_attn_ready, b + 1)
        bank = open_bank(r2, f"yt{b}")
        for k in range(4):
            ins = pe.transpose(bank[:, k * P:(k + 1) * P], t.y_attn[:, b, k * P:(k + 1) * P], t.ident[:])
        ins.then_inc(s.filled2, 1)
    pe.wait_ge(*r2.drained("yt1"))
    pe.wait_ge(s.pool_y, 1)
    for c in range(2):
        landed(n + 7 + 2 * c)
        landed(n + 8 + 2 * c)
        for b in range(NB):
            for q, (prefix, src) in enumerate((("pa", t.ya_T), ("pp", t.y_pool))):
                wt = chunk(g, n + 7 + 2 * c + q, (4, 512))
                project(r2, f"{prefix}{c}{b}", b, [wt[:, k, :] for k in range(4)], src, 0, 512)
    pe.wait_ge(s.h_ready, NB)
    turn(r2, "rT", t.x_n)
    pe.wait_ge(*r2.drained("rT11"))
    pe.wait_ge(s.small_in, 16 * 5)
    bank = open_bank(r2, "lg")
    for b in range(NB):
        for k in range(KT):
            ins = pe.matmul(bank[:, b * E:(b + 1) * E], t.h_T[:, k, b * P:(b + 1) * P], t.w_router[:, k, :],
                            start=(k == 0), stop=(k == KT - 1))
    ins.then_inc(s.filled2, 1)
    pe.wait_ge(s.mask_ready, 1)
    bank = open_bank(r2, "rk")
    pe.matmul(bank[:, 0:E], t.before[:], t.mask[:, 0, :], start=True, stop=True)
    pe.matmul(bank[:, E:2 * E], t.ones[:], t.mask[:, 0, :], start=True, stop=False)
    pe.matmul(bank[:, E:2 * E], t.before[:], t.mask[:, 1, :], start=False, stop=True)
    for b in range(NB):
        ins = pe.matmul(bank[:, 2 * E:3 * E], t.ones[:], t.mask[:, b, :], start=(b == 0), stop=(b == 1))
    ins.then_inc(s.filled2, 1)
    bank = open_bank(r2, "gT")
    for b in range(NB):
        ins = pe.transpose(bank[0:E, b * P:(b + 1) * P], t.gate_e[:, b, :], t.ident[:])
    ins.then_inc(s.filled2, 1)

    pe.wait_ge(*r2.drained("gT"))
    pe.wait_ge(*r2.drained("rk"))
    pe.wait_ge(s.b_down_in, 16)
    for b in range(NB):
        for c in range(2):
            pe.matmul(banks[2 * b + c][:], t.gate_T[0:E, b * P:(b + 1) * P], t.b_down[0:E, 512 * c:512 * c + 512],
                      start=True, stop=False, skip_group_check=True)

    def gather(half, picked, free):
        pe.wait_ge(s.picked, picked)
        pe.wait_ge(*free)
        for i in range(4):
            f = 4 * half + i
            for part, src in enumerate((t.x_hi, t.x_lo)):
                c0 = i * P + part * SLOTS
                for b in range(NB):
                    ins = pe.matmul(banks[6][:, c0:c0 + SLOTS], src[:, b, f * P:(f + 1) * P], t.picks[:, b, :],
                                    start=(b == 0), stop=(b == 1))
        ins.then_inc(s.gathered, 1)

    pe.wait_ge(s.x_split, 2)
    gather(0, NB, (s.x_split, 2))
    gather(1, NB, (s.x_copied, 1))
    pe.wait_ge(s.bias_ready, 1)
    for sem in (s.half_done, s.group_done, s.combined):
        pe.sem_inc(sem, 2)
    last = pe.value_load(t.job_count[0:1, 0:1], min_val=E - 1, max_val=E + OVER - 1)
    with pe.Fori(0, last + 1) as j:
        def split_ready(c):
            pe.wait_ge(s.hi_done, j * JC + (c + 1))
            if c in POOL_LO:
                pe.wait_ge(s.lo_pool, j * len(POOL_LO) + sum(x <= c for x in POOL_LO))
            else:
                pe.wait_ge(s.lo_dve, j * len(DVE_LO) + sum(x <= c for x in DVE_LO))

        def group(q, stationary, bias=None):
            bank = banks[4 + q % 2]
            if bias is not None:
                pe.matmul(bank[:], t.bias_sel[0:64, :], t.bias_hl[0:64, bias:bias + 512], start=True, stop=False)
            for k in range(KT):
                c = 2 * q + k // 4
                if k % 4 == 0:
                    split_ready(c)
                for part, wt in enumerate((t.w_hi, t.w_lo)):
                    ins = pe.matmul(bank[:], stationary[:, k, :], wt[:, c % SPLIT, 512 * (k % 4):512 * (k % 4) + 512],
                                    start=(bias is None and k == 0 and part == 0), stop=(k == KT - 1 and part == 1))
                if k == 3:
                    ins.then_inc(s.half_done, 1)
            ins.then_inc(s.group_done, 1)

        def turn_act(half):
            pe.wait_ge(s.act_ready, j * 2 + half + 1)
            pe.wait_ge(s.act_lo, j * 2 + half)
            for k in range(4):
                c0 = 256 * half + k * SLOTS
                ins = pe.matmul(banks[7][:, c0:c0 + SLOTS], t.act[0:SLOTS, half, k * P:(k + 1) * P],
                                t.ident[0:SLOTS, 0:SLOTS], start=True, stop=True)
            ins.then_inc(s.act_turned, 1)

        pe.wait_ge(s.x_copied, j * 2 + 2)
        pe.wait_ge(s.bias_picked, j + 1)
        for q in range(4):
            if q < 2:
                pe.wait_ge(s.y_copied, j * 2 + q + 1)
            else:
                pe.wait_ge(s.summed, j * 4 + q - 2 + 1 + 2)
            group(q, t.x_T, bias=512 * (q // 2) + FE * (q % 2))
        pe.wait_ge(s.mix_in_ready, j * 2 + 2)
        for b in range(NB):
            ins = pe.transpose(banks[6][:, b * P:(b + 1) * P], t.mix_in[:, b, :], t.ident[:])
        ins.then_inc(s.weights_turned, 1)
        turn_act(0)
        gather(0, j * NB + 2 * NB, (s.mix_ready, j + 1))
        gather(1, j * NB + 2 * NB, (s.x_copied, j * 2 + 3))
        turn_act(1)
        pe.wait_ge(s.act_lo, j * 2 + 2)
        for q in (4, 5):
            pe.wait_ge(s.summed, j * 4 + q - 2 + 1 + 2)
            group(q, t.act_T)
        for c in range(2):
            pe.wait_ge(s.y_copied, j * 2 + c + 1 + 2)
            for b in range(NB):
                ins = pe.matmul(banks[2 * b + c][:], t.mix_w[:, b * P:(b + 1) * P], t.y_slot[:, c, :], start=False,
                                stop=False, skip_group_check=True)
            ins.then_inc(s.combined, 1)
    for n in range(4):
        ins = pe.matmul(banks[n][:], t.zrow[0:1, 0:P], t.zrow[0:1, P:], start=False, stop=True, skip_group_check=True)
    ins.then_inc(s.closed, 1)


class Semaphores:
    def __init__(self, new):
        self.filled = new("filled")
        self.drained_act = new("drained_act")
        self.drained_dve = new("drained_dve")
        self.filled2 = new("filled2")
        self.drained_act2 = new("drained_act2")
        self.drained_dve2 = new("drained_dve2")
        self.early_consts = new("early_consts")
        self.consts = new("consts")
        self.consts2 = new("consts2")
        self.pool_step = new("pool_step")
        self.act_step = new("act_step")
        self.dve_step = new("dve_step")
        self.x_in = new("x_in")
        self.vec_in = new("vec_in")
        self.pos_in = new("pos_in")
        self.small_in = new("small_in")
        self.late_in = new("late_in")
        self.end_in = new("end_in")
        self.bias_in = new("bias_in")
        self.b_down_in = new("b_down_in")
        self.angles = new("angles")
        self.rope_ready = new("rope_ready")
        self.msq_ready = new("msq_ready")
        self.rstd_ready = new("rstd_ready")
        self.x_n_ready = new("x_n_ready")
        self.sb_log = new("sb_log")
        self.sb_soft = new("sb_soft")
        self.sb_arg = new("sb_arg")
        self.sb_w = new("sb_w")
        self.al_log = new("al_log")
        self.gla_cum = new("gla_cum")
        self.gla_exp = new("gla_exp")
        self.gla_dec = new("gla_dec")
        self.att_masked = new("att_masked")
        self.o_n_ready = new("o_n_ready")
        self.y_ready = new("y_ready")
        self.ff_zero = new("ff_zero")
        self.ff_a = new("ff_a")
        self.ff_g = new("ff_g")
        self.ff_o = new("ff_o")
        self.ff_pad = new("ff_pad")
        self.ff_conv = new("ff_conv")
        self.ff_gelu = new("ff_gelu")
        self.ff_u = new("ff_u")
        self.ff_dve_step = new("ff_dve_step")
        self.lat_ready = new("lat_ready")
        self.diff_ready = new("diff_ready")
        self.q_roped = new("q_roped")
        self.row_max = new("row_max")
        self.prob_ready = new("prob_ready")
        self.pool_sq = new("pool_sq")
        self.pool_y = new("pool_y")
        self.y_attn_ready = new("y_attn_ready")
        self.h_ready = new("h_ready")
        self.top_ready = new("top_ready")
        self.top_exp = new("top_exp")
        self.mask_ready = new("mask_ready")
        self.jobs_ready = new("jobs_ready")
        self.x_split = new("x_split")
        self.bias_hi = new("bias_hi")
        self.bias_ready = new("bias_ready")
        self.picked = new("picked")
        self.bias_picked = new("bias_picked")
        self.gathered = new("gathered")
        self.x_copied = new("x_copied")
        self.hi_done = new("hi_done")
        self.lo_dve = new("lo_dve")
        self.lo_pool = new("lo_pool")
        self.half_done = new("half_done")
        self.group_done = new("group_done")
        self.lo_rows_ready = new("lo_rows_ready")
        self.summed = new("summed")
        self.gate_ready = new("gate_ready")
        self.sig_ready = new("sig_ready")
        self.act_ready = new("act_ready")
        self.act_turned = new("act_turned")
        self.act_hi = new("act_hi")
        self.act_lo = new("act_lo")
        self.mix_in_ready = new("mix_in_ready")
        self.weights_turned = new("weights_turned")
        self.mix_ready = new("mix_ready")
        self.y_copied = new("y_copied")
        self.combined = new("combined")
        self.job_dve_step = new("job_dve_step")
        self.closed = new("closed")
        self.out_ready = new("out_ready")
        self.stored = new("stored")
        self.landed = [new(f"landed{n}") for n in range(RING)]


class Filled2:

    def __init__(self, s):
        self.filled, self.drained_act, self.drained_dve = s.filled2, s.drained_act2, s.drained_dve2


class Buffers:

    def persistent(self, new):
        self.h = new("h", [NB, D])
        self.x_n = new("x_n", [NB, D])
        self.ring = new("ring", [RING, CW])
        self.ident = new("ident", [P])
        self.ones = new("ones", [P])
        self.before = new("before", [P])
        self.neg_half = new("neg_half", [8])
        self.inv_freq = new("inv_freq", [HALF])
        self.vec_T = new("vec_T", [ROWS_A + ROWS_B])
        self.zrow = new("zrow", [P + 512], mybir.dt.bfloat16)
        self.g_rows = new("g_rows", [D])
        self.w_router = new("w_router", [KT, E])
        self.b_router = new("b_router", [E])
        self.sin_cos = new("sin_cos", [2, NB, HALF])
        self.msq = new("msq", [len(NORMS), 8])
        self.rstd = new("rstd", [len(NORMS), 8])
        self.job_expert = new("job_expert", [JOBS], I32)
        self.job_count = new("job_count", [1], I32)
        self.job_pos = new("job_pos", [NB, JOBS])
        self.job_gate = new("job_gate", [NB, JOBS])
        self.job_sel = new("job_sel", [JOBS])
        self.iota_s = new("iota_s", [2 * SLOTS])
        self.bias_col = new("bias_col", [2 * SLOTS])
        self.gate_T = new("gate_T", [T])

    def mixer(self, new):
        self.vec_a = new("vec_a", [P])
        self.vec_b = new("vec_b", [P])
        self.tri = new("tri", [P])
        self.pos_i = new("pos_i", [NB], I32)
        self.pos_f = new("pos_f", [NB])
        self.turns = new("turns", [NB, HALF])
        self.turns_i = new("turns_i", [NB, HALF], I32)
        self.ang = new("ang", [2, NB, HALF])
        self.w_ga = new("w_ga", [KT, RANK])
        self.w_alpha = new("w_alpha", [KW])
        self.neg_b_gate = new("neg_b_gate", [16])
        self.x_nT = new("x_nT", [KT, T])
        self.sb_q = new("sb_q", [4, T])
        self.sb_k = new("sb_k", [4, T])
        self.sb_v = new("sb_v", [NB, 512])
        self.z = new("z", [SB_H, 384])
        self.sb_l = new("sb_l", [SB_H, 384])
        self.sb_s = new("sb_s", [SB_H, 384])
        self.sb_keep = new("sb_keep", [384])
        self.sb_cap = new("sb_cap", [384])
        self.g_q = new("g_q", [2, T])
        self.g_k = new("g_k", [2, T])
        self.g_v = new("g_v", [NB, VW])
        self.gr = new("gr", [4, T])
        self.gr_e = new("gr_e", [4, T])
        self.ga_T = new("ga_T", [T])
        self.a_pre = new("a_pre", [2, T])
        self.al_l = new("al_l", [2, T])
        self.chunk_start = new("chunk_start", [T])
        self.cum = new("cum", [2, T])
        self.cum_end = new("cum_end", [2, T])
        self.dec_q = new("dec_q", [2, T])
        self.dec_k = new("dec_k", [2, T])
        self.dec_e = new("dec_e", [2, T])
        self.chunk_decay = new("chunk_decay", [2, 4])
        self.k_end = new("k_end", [NB, KW])
        self.att = new("att", [8, P])
        self.state = new("state", [2, 3, 2, GLA_DV])
        self.gates = new("gates", [16, T])
        self.o_sb = new("o_sb", [4, T])

    def ffn(self, new):
        self.h_nT = new("h_nT", [KT, T])
        self.a_pad = new("a_pad", [2, 2, 2 + T])
        self.ff_c = new("ff_c", [2, 2, T])
        self.ff_ge = new("ff_ge", [2, 2, T])
        self.ff_u = new("ff_u", [2, 2, T])

    def attention(self, new):
        self.h_nT2 = new("h_nT2", [KT, T])
        self.lat = new("lat", [NB, 416])
        self.lat_n = new("lat_n", [NB, 384])
        self.k_rope = new("k_rope", [NB, ROPE])
        self.rope_tmp = new("rope_tmp", [4, MH, HALF])
        self.u_pad = new("u_pad", [4, 16 + T])
        self.win_a = new("win_a", [4, 16 + T])
        self.win_b = new("win_b", [4, 16 + T])
        self.diff = new("diff", [4, T])
        self.inv_count = new("inv_count", [4, T])
        self.at_mask = new("at_mask", [384])
        self.ql_T = new("ql_T", [2, T])
        self.kv_T = new("kv_T", [T])
        self.q_tok = new("q_tok", [NB, MH * QK])
        self.k_tok = new("k_tok", [NB, MH, QK])
        self.v_tok = new("v_tok", [NB, MH, VD])
        self.q_T = new("q_T", [MH, T])
        self.k_T = new("k_T", [MH, T])
        self.score = new("score", [MH, 384])
        self.row_m = new("row_m", [MH, NB])
        self.row_l = new("row_l", [MH, NB])
        self.prob_T = new("prob_T", [MH, 384])
        self.y_pool = new("y_pool", [4, T])
        self.y_sq = new("y_sq", [4, T])
        self.pool_sum = new("pool_sum", [NB])
        self.y_att = new("y_att", [NB, 512])
        self.y_attn = new("y_attn", [NB, 512])
        self.ya_T = new("ya_T", [4, T])
        self.h_T = new("h_T", [KT, T])
        self.iota_i = new("iota_i", [P], I32)
        self.iota_f = new("iota_f", [JOBS])
        self.part32 = new("part32", [1])
        self.logits = new("logits", [NB, E])
        self.top = new("top", [8])
        self.top_i = new("top_i", [8], U32)
        self.top_f = new("top_f", [TOPK])
        self.top_e = new("top_e", [TOPK])
        self.top_s = new("top_s", [1])
        self.one_hot = new("one_hot", [TOPK, E])
        self.mask = new("mask", [NB, E])
        self.gate_e = new("gate_e", [NB, E])
        self.count = new("count", [E])
        self.pos_e = new("pos_e", [NB, E])
        self.over = new("over", [E])
        self.first_over = new("first_over", [E])
        self.end_over = new("end_over", [E])
        self.job_e = new("job_e", [JOBS])

    def experts(self, new):
        self.x_hi = new("x_hi", [NB, D], F32R)
        self.x_lo = new("x_lo", [NB, D], F32R)
        self.w_hi = new("w_hi", [SPLIT, CW], F32R)
        self.w_lo = new("w_lo", [SPLIT, CW], F32R)
        self.x_T = new("x_T", [KT, 2 * SLOTS], F32R)
        self.act_T = new("act_T", [KT, 2 * SLOTS], F32R)
        self.bias_hl = new("bias_hl", [2 * FE], F32R)
        self.picks = new("picks", [NB, SLOTS], F32R)
        self.bias_sel = new("bias_sel", [2 * SLOTS], F32R)
        self.mix_in = new("mix_in", [NB, 2 * SLOTS])
        self.mix_w = new("mix_w", [T])
        self.lo_rows = new("lo_rows", [2, 512])

    def scratch(self, new):
        self.gate = new("gate", [512])
        self.up = new("up", [512])
        self.sig = new("sig", [512])
        self.act = new("act", [2, 512])
        self.y_slot = new("y_slot", [2, 512])

    def before_loop(self, new):
        self.bias_raw = new("bias_raw", [2 * FE])
        self.b_down = new("b_down", [D])


VECTORS = dict(norm_mix="norm_mix_g", norm_ffn="norm_ffn_g", attn_norm="g_attn_norm_2", ffn_norm="g_ffn_norm_2",
               conv_w="conv_w", conv_b="conv_b", b_alpha="b_alpha", gla_g="gla_norm_g", b_pool="b_pool_2",
               pool_scale="pool_scale_2", g_q_a="g_q_a_2", g_kv_a="g_kv_a_2", g_out_pool="g_out_pool_2",
               g_out_attn="g_out_attn_2", b_gate="b_gate")
INPUTS = (
    "x norm_mix_g w_in b_gate w_alpha_up b_alpha gla_norm_g w_branch_sb w_branch_gla w_out norm_ffn_g w_ffn_in conv_w "
    "conv_b w_ffn_out norm_final_g positions_2 g_attn_norm_2 w_in_2 w_pool_2 b_pool_2 pool_scale_2 g_q_a_2 w_q_b_2 "
    "g_kv_a_2 w_kv_b_2 g_out_pool_2 g_out_attn_2 w_out_2 g_ffn_norm_2 w_router_2 b_router_2 w_gate_up_2 b_gate_up_2 "
    "w_down_2 b_down_2 g_final_2"
).split()


def views(aps):
    w = {name: ap if name in ("norm_final_g", "g_final_2") else ap.squeeze(0) for name, ap in aps.items()}
    w["positions"] = w["positions_2"]
    for name in ("norm_final_g", "g_final_2", "g_ffn_norm_2", "b_router_2"):
        w["row_" + name] = w[name].rearrange("(a n) -> a n", a=1)
    w["vectors"] = {key: w[name] if len(w[name].shape) == 2 else w[name].rearrange("(a n) -> a n", a=1)
                    for key, name in VECTORS.items()}
    return w


def kernel(**inputs):
    import concourse.bacc as bacc
    from concourse.bass_utils import run_bass_kernel_spmd

    nc = bacc.Bacc("TRN2", target_bir_lowering=False, num_devices=1)
    arrays, aps = {}, {}
    for name in INPUTS:
        a = np.ascontiguousarray(inputs[name])
        arrays[f"in_{name}"] = a
        aps[name] = nc.dram_tensor(f"in_{name}", a.shape, mybir.dt.from_np(a.dtype), kind="ExternalInput").ap()
    out = nc.dram_tensor("out", (1, T, D), F32, kind="ExternalOutput").ap()
    build(nc, views(aps), out.squeeze(0))
    result = run_bass_kernel_spmd(nc, [arrays], core_ids=[0])
    return result.results[0]["out"]
```

```python
from contextlib import ExitStack

import numpy as np

import concourse.bass as bass
from concourse import mybir
from concourse.alu_op_type import AluOpType as ALU

F32 = mybir.dt.float32
F32R = mybir.dt.float32r
I32 = mybir.dt.int32
U32 = mybir.dt.uint32
ACT = mybir.ActivationFunctionType
X = mybir.AxisListType.X

P = 128
T = 256
NB = T // P
D = 1024
KT = D // P
EPS = 1e-6

SB_H, SB_D = 8, 64
GLA_H, GLA_DK, GLA_DV, CH = 4, 64, 128, 64
KW, VW, RANK = 256, 512, 16
D_FF = 2816
FF_STEPS = D_FF // 256
OFF_Q, OFF_K, OFF_V, OFF_GQK, OFF_GV, OFF_GR, OFF_GA, OFF_GATE = 0, 512, 1024, 1536, 2048, 2560, 3072, 3088

POOL_W = (2, 4, 8, 16)
MH, NOPE, ROPE, QK, VD = 8, 64, 32, 96, 64
HALF = ROPE // 2
QL, KVL = 256, 128
E, TOPK, FE = 32, 4, 1024
SWIGLU_ALPHA, SWIGLU_LIMIT = 1.702, 7.0

SLOTS = 64
OVER = (T * TOPK) // (SLOTS + 1)
JOBS = E + OVER + 1

RING = 6
SPLIT = 6
CW = 2048
JC = 12
AHEAD = 2
POOL_LO = (0, 3, 6, 10)
DVE_LO = tuple(c for c in range(JC) if c not in POOL_LO)

VEC_A = dict(norm_mix=0, norm_ffn=8, attn_norm=16, ffn_norm=24, conv_w=32, conv_b=98)
VEC_B = dict(b_alpha=0, gla_g=2, b_pool=6, pool_scale=10, g_q_a=14, g_kv_a=16, g_out_pool=17, g_out_attn=21,
             b_gate=25)
ROWS_A, ROWS_B = 120, 41

RESULTS = (
    [("vec", "dve")] + [(f"xT{b}{h}", "dve") for b in range(2) for h in range(2)]
    + [("sbq0", "act"), ("sbq1", "act"), ("sbk0", "act"), ("sbk1", "act"), ("sbv0", "dve"), ("sbv1", "dve")]
    + [(f"z{h}", "act") for h in range(4)] + [("gq", "dve"), ("gk", "dve")]
    + [(f"z{h}", "act") for h in range(4, 8)] + [("gv0", "dve"), ("gv1", "dve"), ("ga", "dve")]
    + [("gr0", "act"), ("gr1", "act"), ("al", "dve")]
    + [(f"c{h}", "dve") for h in range(4)] + [(f"gate{n}", "act") for n in range(4)]
    + [(f"c{h}", "dve") for h in range(4, 8)] + [("kend", "act"), ("att0", "act"), ("att1", "act"), ("o0", "dve")]
    + [(f"gate{n}", "act") for n in range(4, 8)]
    + [("ds0", "dve"), ("ds1", "dve"), ("o1", "dve"), ("og0", "act"), ("og1", "act"), ("ogt0", "dve"), ("ogt1", "dve")]
    + [(f"y{n}", "dve") for n in range(8)] + [(f"wo{n}{b}", "dve") for n in range(2) for b in range(2)]
    + [(f"hT{b}{h}", "dve") for b in range(2) for h in range(2)]
)
RESULTS2 = (
    [(f"nT{b}{h}", "dve") for b in range(2) for h in range(2)]
    + [("lat0", "act"), ("lat1", "act"), ("u0", "act"), ("u1", "act")]
    + [("qlT", "dve"), ("kvT", "dve")]
    + [(f"qq{b}{n}", "act") for b in range(2) for n in range(2)]
    + [(f"kv{b}{n}", "act") for b in range(2) for n in range(2)]
    + [(f"qT{n}", "act") for n in range(4)] + [(f"kT{n}", "dve") for n in range(4)]
    + [(f"s{h}", "dve") for h in range(MH)]
    + [("pm0", "act"), ("pm1", "act"), ("pss", "dve")]
    + [(f"pt{h}", "act") for h in range(MH)] + [("av0", "dve"), ("av1", "dve")]
    + [("yt0", "dve"), ("yt1", "dve")]
    + [(f"{s}{n}{b}", "dve") for n in range(2) for b in range(2) for s in ("pa", "pp")]
    + [(f"rT{b}{h}", "act") for b in range(2) for h in range(2)] + [("lg", "dve"), ("rk", "dve"), ("gT", "act")]
)


class Results:

    def __init__(self, order, s, banks):
        self.at = {name: n for n, (name, _) in enumerate(order)}
        self.order, self.s, self.banks = order, s, banks

    def bank(self, name):
        return self.banks[self.at[name] % 8]

    def filled(self, name):
        return self.s.filled, self.at[name] + 1

    def drained(self, name):
        n = self.at[name]
        who = self.order[n][1]
        return drained_sem(self.s, who), sum(w == who for _, w in self.order[: n + 1])

    def room(self, name):
        n = self.at[name]
        return self.drained(self.order[n - 8][0]) if n >= 8 else None


def drained_sem(s, who):
    return s.drained_act if who == "act" else s.drained_dve


class Steps:

    def __init__(self, eng, sem, base=0):
        self.eng, self.sem, self.base, self.n = eng, sem, base, 0

    def settle(self):
        self.eng.wait_ge(self.sem, self.base + self.n)

    def __call__(self, ins):
        ins.then_inc(self.sem, 1)
        self.n += 1
        self.settle()


def spread(ap, n):
    shape = [int(x) for x in ap.shape]
    return ap.unsqueeze(len(shape)).to_broadcast(shape + [n])


def front_chunks(w):
    def cols(m, c0, n, k0=0, kt=4):
        return m[k0 * P:(k0 + kt) * P, c0:c0 + n].rearrange("(k p) n -> p k n", p=P)

    first = []
    for c, user in ((OFF_Q, "sbq1"), (OFF_K, "sbk1"), (OFF_V, "sbv1"), (OFF_GQK, "gk"), (OFF_GV, "gv1"),
                    (OFF_GR, "gr1"), *((OFF_GATE + 512 * n, f"gate{2 * n + 1}") for n in range(4))):
        first += [(cols(w["w_in"], c, 512, 4 * h), (4, 512), user) for h in range(2)]
    for n in range(2):
        first += [(cols(m, 512 * n, 512), (4, 512), f"y{4 * n + 3}") for m in (w["w_branch_sb"], w["w_branch_gla"])]
    for n in range(2):
        first += [(cols(w["w_out"], 512 * n, 512, 4 * h), (4, 512), f"wo{n}1") for h in range(2)]
    second = []
    for c, n, user in ((512, 416, "lat1"), (0, 512, "u1")):
        second += [(cols(w["w_in_2"], c, n, 4 * h), (4, n), user) for h in range(2)]
    second.append((cols(w["w_q_b_2"], 0, 768, 0, 2), (2, 768), "qq11"))
    second.append((w["w_kv_b_2"].rearrange("p (o n) -> p o n", o=1), (1, 1024), "kv11"))
    second.append((w["w_pool_2"].rearrange("g c d -> c g d"), (4, 128), "pm1"))
    for n in range(2):
        second += [(cols(w["w_out_2"], 512 * n, 512, 4 * h), (4, 512), f"pp{n}1") for h in (1, 0)]
    return first, second


def ffn_chunk(g, kind, i):
    if kind == "o":
        return g.n_ffn + (3 * i + 3 if i < FF_STEPS - 1 else 3 * i + 2)
    return g.n_ffn + ((0, 1)[kind == "g"] if i == 0 else 3 * i + (1 if kind == "g" else -1))


def h_part(m, b, h):
    return m[:, 4 * h:4 * h + 4, b * P:(b + 1) * P]


def ffn_made(kind, i):
    if kind == "g":
        return (2 if isinstance(i, int) and i == 0 else i * 3 + 2), i + 1
    if isinstance(i, int) and (kind, i) in (("a", 0), ("o", FF_STEPS - 1)):
        return (1, 1) if kind == "a" else (3 * FF_STEPS, 2 * FF_STEPS)
    return (i * 3, i * 2) if kind == "a" else (i * 3 + 4, i * 2 + 3)


class Program:

    def __init__(self, nc, w, s, t, out, banks):
        self.nc, self.w, self.s, self.t, self.out, self.banks = nc, w, s, t, out, banks
        self.r1, self.r2 = Results(RESULTS, s, banks), Results(RESULTS2, Filled2(s), banks)
        self.first, self.second = front_chunks(w)
        self.n_ffn = len(self.first)
        self.n_second = self.n_ffn + 3 * FF_STEPS
        self.n_moe = self.n_second + len(self.second)


def build(nc, w, out):
    with ExitStack() as ctx:
        s = Semaphores(lambda name: ctx.enter_context(nc.semaphore(name)))
        banks = [ctx.enter_context(nc.psum_tensor(f"bank{n}", [P, 512], F32)) for n in range(8)]

        def into(stack):
            def new(name, shape, dtype=F32):
                return stack.enter_context(nc.sbuf_tensor(name, [P, *shape], dtype))
            return new

        t = Buffers()
        t.persistent(into(ctx))
        for phase in (t.mixer, t.ffn, t.attention):
            with ExitStack() as stack:
                phase(into(stack))
        with ExitStack() as stack:
            for kept, early in ((t.experts_weights, t.bias_early), (t.experts_rows, t.down_early)):
                kept(into(stack))
                with ExitStack() as inner:
                    early(into(inner))
            t.scratch(into(stack))
        t.h_n = t.x_n
        t.y_T = t.x_n[:].rearrange("p b (k n) -> p (b k) n", n=T)
        flat = t.sb_s[:].rearrange("p h n -> p (h n)")
        t.o_gla = flat[:, 0:1024].rearrange("p (b n) -> p b n", b=NB)
        t.o_n = flat[:, 1024:2048].rearrange("p (b n) -> p b n", b=NB)
        t.o_glaT = flat[:, 2048:3072].rearrange("p (k n) -> p k n", k=4)
        flat = t.h_T[:].rearrange("p k n -> p (k n)")
        t.sel, t.sel_tmp = (flat[:, n * (OVER + 1) * E:(n + 1) * (OVER + 1) * E].rearrange("p (m e) -> p m e", e=E)
                            for n in range(2))

        g = Program(nc, w, s, t, out, banks)

        block = ctx.enter_context(nc.Block())

        @block.sync
        def _(sp):
            sync_program(g, sp)

        @block.gpsimd
        def _(pool):
            gpsimd_program(g, pool)

        @block.scalar
        def _(act):
            scalar_program(g, act)

        @block.vector
        def _(dve):
            vector_program(g, dve)

        @block.tensor
        def _(pe):
            tensor_program(g, pe)


def slot_use(n):
    return n % RING, 16 * (n // RING + 1)


def lo_count(lo_of, j, c):
    return j * len(lo_of) + (c // JC * len(lo_of) + sum(x <= c % JC for x in lo_of))


def lo_maker(s, c):
    return (s.lo_pool, POOL_LO) if c % JC in POOL_LO else (s.lo_dve, DVE_LO)


def chunk(g, n, shape):
    k, m = shape
    return g.t.ring[:, n % RING, 0:k * m].rearrange("p (k m) -> p k m", k=k)


def sync_program(g, sp):
    s, w, t = g.s, g.w, g.t

    def load(n, src, shape):
        sp.dma_start(chunk(g, n, shape), src).then_inc(s.landed[n % RING], 16)

    for n, (src, shape, _) in enumerate(g.first):
        if n == 1:
            sp.wait_ge(s.x_in, 16 * NB)
        if n == 3:
            sp.wait_ge(s.vec_in, 16 * (len(VEC_A) + len(VEC_B)))
        if n >= RING:
            sp.wait_ge(*g.r1.filled(g.first[n - RING][2]))
        load(n, src, shape)

    ffn_in = w["w_ffn_in"].rearrange("(k p) n -> p k n", p=P)
    ffn_out = w["w_ffn_out"].rearrange("(k p) n -> p k n", p=P)

    def load_ffn(i, kind, turns=0, i0=0):
        n = ffn_chunk(g, kind, i0)
        dst = t.ring[:, n % RING, :].rearrange("p (k m) -> p k m", k=2 if kind == "o" else KT)
        if kind == "o":
            src = ffn_out[:, bass.ds(i * 2, 2), :]
        else:
            src = ffn_in[:, :, bass.ds(i * 256 + (D_FF if kind == "g" else 0), 256)]
        sp.dma_start(dst, src).then_inc(s.landed[n % RING], 16)

    for i, kind in ((0, "a"), (0, "g"), (1, "a"), (0, "o"), (1, "g"), (2, "a")):
        n = ffn_chunk(g, kind, i)
        sp.wait_ge(*g.r1.filled(g.first[n - RING][2]))
        load_ffn(i, kind, 0, i)
    sp.wait_ge(s.ff_a, 1)
    load_ffn(1, "o", 0, 1)
    with sp.Fori(0, (FF_STEPS - 3) // 2) as m:
        for q in range(2):
            sp.wait_ge(s.ff_g, m * 2 + (q + 1))
            load_ffn(m * 2 + (q + 2), "g", m, q + 2)
            sp.wait_ge(s.ff_a, m * 2 + (q + 2))
            load_ffn(m * 2 + (q + 3), "a", m, q + 3)
            sp.wait_ge(s.ff_o, m * 2 + (q + 1))
            load_ffn(m * 2 + (q + 2), "o", m, q + 2)
    sp.wait_ge(s.ff_g, FF_STEPS - 2)
    load_ffn(FF_STEPS - 1, "g", 0, FF_STEPS - 1)
    sp.wait_ge(s.ff_o, FF_STEPS - 2)
    load_ffn(FF_STEPS - 1, "o", 0, FF_STEPS - 1)

    former = [("o", 3), ("g", 2), ("a", 1), ("o", 2), ("g", 1), ("o", 1)]
    for n, (src, shape, _) in enumerate(g.second):
        if n < RING:
            kind, back = former[n]
            sp.wait_ge({"a": s.ff_a, "g": s.ff_g, "o": s.ff_o}[kind], FF_STEPS + 1 - back)
        else:
            sp.wait_ge(*g.r2.filled(g.second[n - RING][2]))
        load(g.n_second + n, src, shape)

    gate_up = w["w_gate_up_2"].rearrange("e (h k p) n -> e h p k n", p=P, k=4)
    down = w["w_down_2"].rearrange("e (h k p) n -> e h p k n", p=P, k=4)

    def load_expert(e, q, h, c):
        if q < 4:
            col = 512 * (q // 2) + FE * (q % 2)
            src = gate_up[e, h, :, :, col:col + 512]
        else:
            src = down[e, h, :, :, 512 * (q - 4):512 * (q - 4) + 512]
        n = g.n_moe + c
        sp.dma_start(chunk(g, n, (4, 512)), src).then_inc(s.landed[n % RING], 16)

    def wait_split(j, c):
        sem, lo_of = lo_maker(s, c)
        sp.wait_ge(sem, lo_count(lo_of, j, c))

    for c in range(RING):
        sp.wait_ge(*g.r2.filled(g.second[len(g.second) - RING + c][2]))
        load_expert(0, c // 2, c % 2, c)
    def expert(job):
        if isinstance(job, int):
            return job
        return sp.value_load(t.job_expert[0:1, bass.ds(job, 1)], min_val=0, max_val=E - 1)

    def rest_of_turn(j):
        e = expert(j)
        e_next = expert(j + 1)
        for c, q, h, who in ((6, 3, 0, e), (7, 3, 1, e), (8, 0, 0, e_next), (9, 0, 1, e_next),
                             (10, 4, 0, e), (11, 4, 1, e), (12, 5, 0, e), (13, 5, 1, e)):
            wait_split(j, c - RING)
            load_expert(who, q, h, c)

    def start_of_next(j):
        e = expert(j + 1)
        for c, q, h in ((14, 1, 0), (15, 1, 1), (16, 2, 0), (17, 2, 1)):
            wait_split(j, c - RING)
            load_expert(e, q, h, c)

    rest_of_turn(0)
    start_of_next(0)
    sp.wait_ge(s.jobs_ready, 1)
    last = sp.value_load(t.job_count[0:1, 0:1], min_val=E - 1, max_val=E + OVER - 1)
    with sp.Fori(0, last - 1) as m:
        rest_of_turn(m + 1)
        start_of_next(m + 1)
    e = expert(last)
    for c, q, h in ((6, 3, 0), (7, 3, 1), (8, 4, 0), (9, 4, 1), (10, 5, 0), (11, 5, 1)):
        wait_split(last, c - RING)
        load_expert(e, q, h, c)

    sp.wait_ge(s.out_ready, 2)
    for b in range(NB):
        sp.dma_start(g.out[b * P:(b + 1) * P, :], t.h[:, b, :]).then_inc(s.stored, 16)
    sp.wait_ge(s.stored, 16 * NB)


NORMS = (("mix", NB), ("gla", NB * GLA_H), ("ffn", NB), ("end1", NB), ("attn", NB), ("lat", 2 * NB), ("mla", NB),
         ("pool", NB), ("moe", NB), ("end2", NB))
WITH_ACT = ("ffn", "end1", "attn", "moe", "end2")
NORM_AT = {name: n for n, (name, _) in enumerate(NORMS)}
NORM_N = dict(NORMS)


def gpsimd_program(g, pool):
    s, t = g.s, g.t
    step = Steps(pool, s.pool_step)

    def triangle(ap, op, sign, fill, n=P):
        step(pool.affine_select(out=ap, in_=ap, compare_op=op, fill=fill, base=0, pattern=[[sign, n]],
                                channel_multiplier=-sign))

    step(pool.memset(t.ident[:], 0.0))
    triangle(t.ident[:], ALU.not_equal, 1, 1.0)
    step(pool.memset(t.neg_half[:], -0.5))
    for i in range(HALF):
        freq = np.float32(10000.0) ** np.float32(-i / HALF)
        step(pool.memset(t.inv_freq[:, i:i + 1], float(freq)))
    pool.memset(t.ones[:], 1.0).then_inc(s.early_consts, 1)
    step(pool.memset(t.zrow[0:1, :], 0.0))
    step(pool.memset(t.tri[:], 1.0))
    triangle(t.tri[:], ALU.is_ge, -1, 0.0)
    step(pool.memset(t.before[:], 1.0))
    triangle(t.before[:], ALU.is_gt, 1, 0.0)
    step(pool.memset(t.sb_keep[:], 1.0))
    step(pool.memset(t.sb_cap[:], 0.0))
    for c in (0, 2 * P):
        triangle(t.sb_keep[:, c:c + P], ALU.is_gt, 1, 0.0)
        triangle(t.sb_cap[:, c:c + P], ALU.is_gt, 1, -1e30)
    step(pool.memset(t.chunk_start[:], 1.0))
    step(pool.memset(t.att[:], 0.0))
    step(pool.memset(t.state[:], 0.0))
    pool.memset(t.chunk_start[:, 0:T:CH], 0.0).then_inc(s.consts, 1)

    def rsqrt(name):
        k, n = NORM_AT[name], NORM_N[name]
        pool.wait_ge(s.msq_ready, k + 1)
        pool.tensor_tensor(t.rstd[:, k, 0:n], t.msq[:, k, 0:n], t.neg_half[:, 0:n], ALU.pow).then_inc(s.rstd_ready, 1)

    rsqrt("mix")
    pool.wait_ge(*g.r1.drained("att1"))
    for q in range(2):
        rows = slice(CH * q, CH * q + CH)
        pool.affine_select(out=t.att[rows, :, rows], in_=t.att[rows, :, rows], compare_op=ALU.is_ge, fill=0.0, base=0,
                           pattern=[[0, 2 * GLA_H], [1, CH]], channel_multiplier=-1).then_inc(s.att_masked, 1)
    rsqrt("gla")
    rsqrt("ffn")

    def ffn_lo(i, i0):
        slot = ffn_chunk(g, "g", i0) % RING
        pool.wait_ge(s.ff_hi_done, ffn_made("g", i)[0])
        if i0 > 0:
            pool.wait_ge(s.ff_g, i)
        pool.tensor_tensor(t.ff_lo[:, 1, :], t.ring[:, slot, :], t.ff_hi[:, slot, :].bitcast(F32),
                           ALU.subtract).then_inc(s.ff_lo_pool, 1)

    ffn_lo(0, 0)
    with pool.Fori(0, (FF_STEPS - 1) // 2) as m:
        ffn_lo(m * 2 + 1, 1)
        ffn_lo(m * 2 + 2, 2)
    rsqrt("end1")
    rsqrt("attn")
    step(pool.memset(t.at_mask[:], 0.0))
    for c in (0, 2 * P):
        triangle(t.at_mask[:, c:c + P], ALU.is_ge, -1, -1e30)
    for n, win in enumerate(POOL_W):
        step(pool.memset(t.inv_count[:, n, :], 1.0 / win))
    for i in range(POOL_W[-1] - 1):
        n = next(n for n, win in enumerate(POOL_W) if win > i + 1)
        step(pool.memset(t.inv_count[:, n:, i:i + 1], 1.0 / (i + 1)))
    for q in range(2):
        step(pool.iota(t.iota_i[32 * q:32 * q + 32, 0:1], pattern=[[0, 1]], base=0, channel_multiplier=1))
    step(pool.tensor_copy(t.part32[0:64, :], t.iota_i[0:64, 0:1]))
    step(pool.iota(t.iota_i[:, 0:JOBS], pattern=[[1, JOBS]], base=0, channel_multiplier=0))
    step(pool.tensor_copy(t.iota_f[:, 0:JOBS], t.iota_i[:, 0:JOBS]))
    step(pool.iota(t.iota_i[:, 0:2 * SLOTS], pattern=[[0, 2], [1, SLOTS]], base=0, channel_multiplier=0))
    step(pool.tensor_copy(t.iota_s[:], t.iota_i[:, 0:2 * SLOTS]))
    step(pool.memset(t.bias_col[0:64, 0:SLOTS], 1.0))
    step(pool.memset(t.bias_col[0:64, SLOTS:], 0.0))
    pool.memset(t.u_pad[:, :, 0:16], 0.0).then_inc(s.consts2, 1)
    rsqrt("lat")
    pool.wait_ge(*g.r2.drained("u1"))
    pool.wait_ge(s.consts2, 1)
    src, dst = t.u_pad, t.win_a
    for n in range(4):
        sh = 1 << n
        step(pool.tensor_tensor(dst[:, n:, sh:], src[:, n:, sh:], src[:, n:, :16 + T - sh], ALU.add))
        step(pool.tensor_tensor(t.diff[:, n, :], dst[:, n, 16:], t.inv_count[:, n, :], ALU.mult))
        if n < 3:
            step(pool.tensor_copy(dst[:, n:, 0:sh], src[:, n:, 0:sh]))
        src, dst = dst, (t.win_b if dst is t.win_a else t.win_a)
    pool.tensor_tensor(t.diff[:], t.diff[:], t.u_pad[:, :, 16:], ALU.subtract).then_inc(s.diff_ready, 1)
    rsqrt("mla")
    rsqrt("pool")
    rsqrt("moe")

    def lo(j, c, done=None):
        pool.wait_ge(s.hi_done, j * JC + (c + 1))
        pool.tensor_tensor(t.w_lo[:, c % SPLIT, :], t.ring[:, (g.n_moe + c) % RING, :],
                           t.w_hi[:, c % SPLIT, :].bitcast(F32), ALU.subtract).then_inc(done or s.lo_pool, 1)

    for c in range(SPLIT):
        lo(0, c, s.lo_pool if c in POOL_LO else s.lo_dve)
    pool.wait_ge(s.jobs_ready, 1)
    last = pool.value_load(t.job_count[0:1, 0:1], min_val=E - 1, max_val=E + OVER - 1)

    def turn(j, chunks):
        for c in chunks:
            if c % JC in POOL_LO:
                lo(j, c)

    turn(0, range(SPLIT, AHEAD + JC))
    with pool.Fori(0, last - 1) as m:
        turn(m + 1, range(AHEAD, AHEAD + JC))
    turn(last, range(AHEAD, JC))
    rsqrt("end2")


def scalar_program(g, act):
    s, t, w, r1, r2 = g.s, g.t, g.w, g.r1, g.r2
    step = Steps(act, s.act_step)

    for b in range(NB):
        act.dma_start(t.h[:, b, :], w["x"][b * P:(b + 1) * P, :]).then_inc(s.x_in, 16)

    def rows(table, r0, m):
        n = int(np.prod(m.shape)) // P
        flat = m.rearrange("a (k p) -> (a k) p", p=P)
        act.dma_start(table[r0:r0 + n, :], flat).then_inc(s.vec_in, 16)

    for name, r0 in VEC_A.items():
        rows(t.vec_a, r0, w["vectors"][name])
    for name, r0 in VEC_B.items():
        rows(t.vec_b, r0, w["vectors"][name])
    act.dma_start(t.pos_i[:], w["positions"].rearrange("(b p) -> p b", p=P),
                  allow_slow_non_contiguous=True).then_inc(s.pos_in, 16)
    act.dma_start(t.w_ga[:], w["w_in"][:, OFF_GA:OFF_GA + RANK].rearrange("(k p) n -> p k n", p=P)).then_inc(
        s.small_in, 16)
    act.dma_start(t.w_alpha[0:RANK, :], w["w_alpha_up"]).then_inc(s.small_in, 16)
    act.dma_start(t.w_router[:], w["w_router_2"].rearrange("(k p) n -> p k n", p=P)).then_inc(s.small_in, 16)
    act.dma_start(t.b_router[:], w["row_b_router_2"].to_broadcast([P, E])).then_inc(s.small_in, 16)
    act.dma_start(t.g_rows[:], w["row_norm_final_g"].to_broadcast([P, D])).then_inc(s.small_in, 16)

    act.wait_ge(s.angles, 1)
    act.activation(t.sin_cos[:], t.ang[:], ACT.Sin).then_inc(s.rope_ready, 1)
    act.preload_act_table_set("natural_log_exp_and_others")

    def take(r, name, dst, src, scale=1.0, fn=ACT.Copy):
        act.wait_ge(*r.filled(name))
        act.activation(dst, src, fn, scale=scale).then_inc(r.drained(name)[0], 1)

    def square(name, sem, value):
        k = NORM_AT[name]
        act.wait_ge(sem, value)
        act.activation(t.x_n[:, 0, :], t.h[:, 0, :], ACT.Square, accum_out=t.msq[:, k, 0:1]).then_inc(s.act_msq, 1)

    def pair(r, name):
        return r.bank(name)[:].rearrange("p (k n) -> p k n", k=2)

    for n in range(2):
        take(r1, f"sbq{n}", t.sb_q[:, 2 * n:2 * n + 2, :], pair(r1, f"sbq{n}"), scale=SB_D ** -0.5)
    for n in range(2):
        take(r1, f"sbk{n}", t.sb_k[:, 2 * n:2 * n + 2, :], pair(r1, f"sbk{n}"))

    def log_term(dst, src, done):
        step(act.activation(dst, src, ACT.Abs))
        step(act.activation(dst, dst, ACT.Exp, scale=-1.0))
        act.activation(dst, dst, ACT.Ln, bias=1.0).then_inc(done, 1)

    for half in range(2):
        for h in range(4 * half, 4 * half + 4):
            take(r1, f"z{h}", t.z[:, h, :], r1.bank(f"z{h}")[:, 0:384])
        act.wait_ge(*r1.drained(f"z{4 * half + 3}"))
        hs = slice(4 * half, 4 * half + 4)
        log_term(t.sb_l[:, hs, :], t.z[:, hs, :], s.sb_log)
    for n in range(2):
        src = pair(r1, f"gr{n}")
        act.wait_ge(*r1.filled(f"gr{n}"))
        step(act.activation(t.gr[:, 2 * n:2 * n + 2, :], src, ACT.Copy))
        act.activation(t.gr_e[:, 2 * n:2 * n + 2, :], src, ACT.Exp, scale=-1.0).then_inc(s.drained_act, 1)
    act.wait_ge(*r1.drained("al"))
    log_term(t.al_l[:], t.a_pre[:], s.al_log)

    def weights_of_half(half):
        hs = slice(4 * half, 4 * half + 4)
        act.wait_ge(s.sb_arg, half + 1)
        act.activation(t.sb_l[:, hs, :], t.z[:, hs, :], ACT.Exp).then_inc(s.sb_w, 1)

    def gate(n):
        act.wait_ge(*r1.filled(f"gate{n}"))
        if n >= 4:
            for i in range(2):
                ins = act.activation(t.gates[:, 2 * n + i, :], pair(r1, f"gate{n}")[:, i, :], ACT.Sigmoid,
                                     bias=vec(t, "b_gate", 2 * n + i))
                if i == 0:
                    step(ins)
            ins.then_inc(s.drained_act, 1)
            return
        for i in range(2):
            ins = act.activation(t.gates[:, 2 * n + i, :], pair(r1, f"gate{n}")[:, i, :], ACT.Exp, scale=-1.0,
                                 bias=t.neg_b_gate[:, 2 * n + i:2 * n + i + 1])
            if i == 0:
                step(ins)
        ins.then_inc(s.drained_act, 1)

    weights_of_half(0)
    act.wait_ge(s.gla_cum, 1)
    act.activation(t.dec_q[:], t.cum[:], ACT.Exp, scale=-1.0 / 16).then_inc(s.gla_exp, 1)
    act.activation(t.dec_k[:], t.cum[:], ACT.Exp, scale=1.0 / 16).then_inc(s.gla_exp, 1)
    act.activation(t.dec_e[:], t.cum_end[:], ACT.Exp, scale=1.0 / 16).then_inc(s.gla_exp, 1)
    for n in range(4):
        gate(n)
    weights_of_half(1)
    take(r1, "kend", t.k_end[:], r1.bank("kend")[:].rearrange("p (b n) -> p b n", b=NB))
    for n in range(2):
        act.wait_ge(*r1.filled(f"att{n}"))
        for q in range(2):
            rows = slice(CH * q, CH * q + CH)
            ins = act.activation(t.att[rows, 4 * n:4 * n + 4, rows],
                                 r1.bank(f"att{n}")[rows].rearrange("p (k n) -> p k n", k=4)[:, :, rows], ACT.Copy)
            if q == 0:
                step(ins)
        ins.then_inc(s.drained_act, 1)
    act.preload_act_table(ACT.Sigmoid)
    for n in range(4, 8):
        gate(n)
    for b in range(NB):
        take(r1, f"og{b}", t.o_gla[:, b, :], r1.bank(f"og{b}")[:])

    act.wait_ge(*r1.filled("wo11"))
    square("ffn", *r1.drained("wo10"))
    act.preload_act_table(ACT.Gelu_apprx_tanh)

    def pad(i, q, i0):
        act.wait_ge(s.ff_a, i + 1)
        if i0 > 1:
            act.wait_ge(s.ff_conv, i - 1)
        act.activation(t.a_pad[:, q, :, 2:], g.banks[4 + q][:].rearrange("p (k n) -> p k n", k=2),
                       ACT.Copy).then_inc(s.ff_pad, 1)

    def gelu(i, q):
        act.wait_ge(s.ff_conv, i + 1)
        act.activation(t.ff_ge[:, q], t.ff_c[:, q], ACT.Gelu_apprx_tanh).then_inc(s.ff_gelu, 1)

    def ffn_hi(kind, turns, i0):
        n = ffn_chunk(g, kind, i0)
        act.wait_ge(s.landed[n % RING], turns * 16 + 16 * (n // RING + 1))
        act.activation(t.ff_hi[:, n % RING, :], t.ring[:, n % RING, :], ACT.Copy).then_inc(s.ff_hi_done, 1)

    def ffn_step(i, q, turns, i0):
        pad(i, q, i0)
        if i0 + 1 < FF_STEPS:
            ffn_hi("a", turns, i0 + 1)
        gelu(i, q)
        ffn_hi("o", turns, i0)
        if i0 + 1 < FF_STEPS:
            ffn_hi("g", turns, i0 + 1)
        act.wait_ge(s.ff_prod, i + 1)
        if i0 > 1:
            act.wait_ge(s.ff_o, i - 1)
        act.activation(t.u_hi[:, q], t.ff_u[:, q], ACT.Copy).then_inc(s.u_hi_done, 1)

    ffn_hi("a", 0, 0)
    ffn_hi("g", 0, 0)
    for b in range(NB):
        for h in range(2):
            act.wait_ge(*r1.drained(f"hT{b}{h}"))
            act.activation(h_part(t.h_hi, b, h), h_part(t.h_nT, b, h), ACT.Copy).then_inc(s.h_rounded, 1)
    act.wait_ge(s.ff_zero, 1)
    ffn_step(0, 0, 0, 0)
    ffn_step(1, 1, 0, 1)
    with act.Fori(0, (FF_STEPS - 3) // 2) as m:
        ffn_step(m * 2 + 2, 0, m, 2)
        ffn_step(m * 2 + 3, 1, m, 3)
    ffn_step(FF_STEPS - 1, 0, 0, FF_STEPS - 1)
    act.preload_act_table_set("natural_log_exp_and_others")

    square("end1", s.rows_ready, 1)

    square("attn", s.rows_ready, 2)
    act.wait_ge(s.msq_ready, NORM_AT["attn"] + 1)
    act.dma_start(t.g_rows[:], w["row_g_ffn_norm_2"].to_broadcast([P, D])).then_inc(s.late_in, 16)
    for b in range(NB):
        take(r2, f"lat{b}", t.lat[:, b, :], r2.bank(f"lat{b}")[:, 0:416])
    act.wait_ge(s.consts2, 1)
    for n in range(2):
        take(r2, f"u{n}", t.u_pad[:, 2 * n:2 * n + 2, 16:], pair(r2, f"u{n}"))
    for b in range(NB):
        for n in range(2):
            take(r2, f"qq{b}{n}", t.q_tok[:, b, 384 * n:384 * n + 384], r2.bank(f"qq{b}{n}")[:, 0:384])
    for b in range(NB):
        for n in range(2):
            src = r2.bank(f"kv{b}{n}")[:].rearrange("p (h x) -> p h x", h=4)
            hs = slice(4 * n, 4 * n + 4)
            act.wait_ge(*r2.filled(f"kv{b}{n}"))
            step(act.activation(t.k_tok[:, b, hs, 0:NOPE], src[:, :, 0:NOPE], ACT.Copy))
            act.activation(t.v_tok[:, b, hs, :], src[:, :, NOPE:], ACT.Copy).then_inc(r2.drained("kv00")[0], 1)
    for n in range(4):
        take(r2, f"qT{n}", t.q_T[0:QK, 2 * n:2 * n + 2, :], pair(r2, f"qT{n}")[0:QK])

    def soft(h):
        for b in range(NB):
            cs = slice(0, P) if b == 0 else slice(P, 3 * P)
            act.wait_ge(s.row_max, h // 4 + 1)
            act.activation(t.score[:, h, cs], t.score[:, h, cs], ACT.Exp, bias=t.row_m[:, h, b:b + 1],
                           accum_out=t.row_l[:, h, b:b + 1]).then_inc(s.prob_ready, 1)

    for h in range(MH):
        soft(h)
        if h == 3:
            for n in range(2):
                act.wait_ge(*r2.filled(f"pm{n}"))
                for i in range(2):
                    f = 2 * n + i
                    ins = act.activation(t.y_pool[:, f, :], pair(r2, f"pm{n}")[:, i, :], ACT.Identity,
                                         bias=vec(t, "b_pool", f))
                    if i == 0:
                        step(ins)
                ins.then_inc(r2.drained(f"pm{n}")[0], 1)
    for h in range(MH):
        take(r2, f"pt{h}", t.prob_T[:, h, :], r2.bank(f"pt{h}")[:, 0:384])
    square("moe", *r2.drained("pp10"))
    for b in range(NB):
        for h in range(2):
            take(r2, f"rT{b}{h}", t.h_T[:, 4 * h:4 * h + 4, b * P:(b + 1) * P],
                 r2.bank(f"rT{b}{h}")[:].rearrange("p (k n) -> p k n", k=4))
    def hi(j, c, first=False):
        n = g.n_moe + c
        act.wait_ge(s.landed[n % RING], j * (16 * JC // RING) + 16 * (n // RING + 1))
        if not first:
            act.wait_ge(s.group_done if c % 2 else s.half_done, j * 6 + ((c - SPLIT) // 2 + 1 + 2))
        act.activation(t.w_hi[:, c % SPLIT, :], t.ring[:, n % RING, :], ACT.Copy).then_inc(s.hi_done, 1)

    for q in range(2):
        act.dma_start(t.bias_raw[32 * q:32 * q + 32, :], w["b_gate_up_2"]).then_inc(s.bias_in, 16)
    act.dma_start(t.b_down[0:E, :], w["b_down_2"]).then_inc(s.b_down_in, 16)
    hi(0, 0, first=True)
    hi(0, 1, first=True)
    act.wait_ge(s.top_ready, 1)
    act.activation(t.top_e[:], t.top_e[:], ACT.Exp).then_inc(s.top_exp, 1)
    act.preload_act_table(ACT.Sigmoid)
    act.wait_ge(s.bias_in, 32)
    act.activation(t.bias_hl[0:64, :], t.bias_raw[0:64, :], ACT.Copy).then_inc(s.bias_hi, 1)
    hi(0, 2, first=True)
    hi(0, 3, first=True)
    take(r2, "gT", t.gate_T[0:E, :], r2.bank("gT")[0:E, 0:T])
    hi(0, 4, first=True)
    hi(0, 5, first=True)
    act.wait_ge(s.h_ready, NB)
    act.dma_start(t.g_rows[:], w["row_g_final_2"].to_broadcast([P, D])).then_inc(s.end_in, 16)

    def low_rows(j, r):
        act.wait_ge(s.group_done, j * 6 + r + 1 + 2)
        act.wait_ge(s.summed, j * 4 + r + 1)
        act.activation(t.lo_rows[0:SLOTS, r % 2, :], g.banks[4 + r % 2][SLOTS:, :],
                       ACT.Copy).then_inc(s.lo_rows_ready, 1)

    def take_x():
        act.activation(t.x_T[:, :, 0:SLOTS], g.banks[6][:].rearrange("p (k n) -> p k n", k=KT),
                       ACT.Copy).then_inc(s.x_copied, 1)

    def copy_x(j):
        act.wait_ge(s.gathered, j + 2)
        act.wait_ge(s.group_done, j * 6 + 3 + 1 + 2)
        take_x()

    act.wait_ge(s.bias_ready, 1)
    act.wait_ge(s.gathered, 1)
    take_x()
    act.wait_ge(s.jobs_ready, 1)
    last = act.value_load(t.job_count[0:1, 0:1], min_val=E - 1, max_val=E + OVER - 1)
    low_rows(0, 0)
    def turn(j, first=False, final=False):
        def sigmoid(half):
            act.wait_ge(s.gate_ready, j * 2 + half + 1)
            act.wait_ge(s.act_ready, j * 2 + half + 2)
            act.activation(t.sig[0:SLOTS, :], t.gate[0:SLOTS, :], ACT.Sigmoid,
                           scale=SWIGLU_ALPHA).then_inc(s.sig_ready, 1)

        def act_hi(half):
            act.wait_ge(s.act_turned, j * 2 + half + 1 + 2)
            act.activation(t.act_T[:, 4 * half:4 * half + 4, 0:SLOTS],
                           g.banks[7][:, 256 * half:256 * half + 256].rearrange("p (k n) -> p k n", k=4),
                           ACT.Copy).then_inc(s.act_hi, 1)

        def copy_y(n):
            r = (4 if final else 5) + n
            act.wait_ge(s.group_done, j * 6 + (r + 1 + 2))
            act.wait_ge(s.combined, j * 2 + n + 1)
            act.activation(t.y_slot[:, n, :], g.banks[4 + r % 2][:], ACT.Copy).then_inc(s.y_copied, 1)

        def mix():
            act.wait_ge(s.weights_turned, j + 1 + 1)
            act.wait_ge(s.combined, j * 2 + 2)
            act.activation(t.mix_w[:], g.banks[6][:, 0:T], ACT.Copy).then_inc(s.mix_ready, 1)

        if not first:
            hi(j, 4)
            hi(j, 5)
        hi(j, 6)
        low_rows(j, 1)
        sigmoid(0)
        hi(j, 7)
        hi(j, 8)
        low_rows(j, 2)
        act_hi(0)
        hi(j, 9)
        if not final:
            hi(j, 10)
            copy_x(j)
            hi(j, 11)
        low_rows(j, 3)
        sigmoid(1)
        if final:
            hi(j, 10)
            hi(j, 11)
            act_hi(1)
        else:
            hi(j, 12)
            hi(j, 13)
            hi(j, 14)
            act_hi(1)
            hi(j, 15)
            low_rows(j, 4)
        copy_y(0)
        mix()
        copy_y(1)

    turn(0, first=True)
    with act.Fori(0, last - 1) as m:
        turn(m + 1)
    turn(last, final=True)
    square("end2", s.rows_ready, 3)


def vec(t, name, n=0, count=1):
    c = (VEC_A[name] if name in VEC_A else ROWS_A + VEC_B[name]) + n
    return t.vec_T[:, c:c + count]


def vector_program(g, dve):
    s, t, w, r1, r2 = g.s, g.t, g.w, g.r1, g.r2
    step = Steps(dve, s.dve_step)

    def mean_squares(name, parts):
        k = NORM_AT[name]
        for i, (src, scratch, n) in enumerate(parts):
            step(dve.tensor_tensor_reduce(scratch, src, src, 1.0, 0.0, ALU.mult, ALU.add, t.msq[:, k, i:i + 1]))
        finish_mean(name, [n for _, _, n in parts])

    def mean_squares_with_act(name):
        k = NORM_AT[name]
        step(dve.tensor_tensor_reduce(t.x_n[:, 1, :], t.h[:, 1, :], t.h[:, 1, :], 1.0, 0.0, ALU.mult, ALU.add,
                                      t.msq[:, k, 1:2]))
        dve.wait_ge(s.act_msq, WITH_ACT.index(name) + 1)
        finish_mean(name, [D] * NB)

    def finish_mean(name, widths):
        k, m = NORM_AT[name], len(widths)
        for n in sorted(set(widths)):
            cols = [i for i, x in enumerate(widths) if x == n]
            a, b = cols[0], cols[-1] + 1
            ins = dve.tensor_scalar(t.msq[:, k, a:b], t.msq[:, k, a:b], 1.0 / n, EPS, ALU.mult, ALU.add)
            if n != max(widths):
                step(ins)
        ins.then_inc(s.msq_ready, 1)

    def rstd(name, i):
        return t.rstd[:, NORM_AT[name], i:i + 1]

    def have_rstd(name):
        dve.wait_ge(s.rstd_ready, NORM_AT[name] + 1)

    def out_of(r, name):
        dve.wait_ge(*r.filled(name))
        return r.bank(name), r.drained(name)[0]

    def turned(r, prefix, dst, gain):
        for b in range(NB):
            for h in range(2):
                bank, done = out_of(r, f"{prefix}{b}{h}")
                dve.tensor_tensor(dst[:, 4 * h:4 * h + 4, b * P:(b + 1) * P],
                                  bank[:].rearrange("p (k n) -> p k n", k=4),
                                  spread(vec(t, gain, 4 * h, 4), P), ALU.mult).then_inc(done, 1)

    bank, done = None, None
    dve.wait_ge(s.x_in, 16 * NB)
    mean_squares("mix", [(t.h[:, b, :], t.x_n[:, b, :], D) for b in range(NB)])
    bank, done = out_of(r1, "vec")
    step(dve.tensor_copy(t.vec_T[:, 0:ROWS_A], bank[:, 0:ROWS_A]))
    dve.tensor_copy(t.vec_T[:, ROWS_A:], bank[:, P:P + ROWS_B]).then_inc(done, 1)
    dve.wait_ge(*r1.drained("vec"))
    step(dve.tensor_scalar(t.neg_b_gate[:], vec(t, "b_gate", 0, 16), -1.0, None, ALU.mult))
    have_rstd("mix")
    for b in range(NB):
        dve.tensor_scalar(t.x_n[:, b, :], t.h[:, b, :], rstd("mix", b), None, ALU.mult).then_inc(s.x_n_ready, 1)
    turned(r1, "xT", t.x_nT, "norm_mix")

    dve.wait_ge(s.early_consts, 1)
    dve.wait_ge(s.pos_in, 16)
    step(dve.tensor_copy(t.pos_f[:], t.pos_i[:]))
    sin_arg, cos_arg = t.ang[:, 0], t.ang[:, 1]
    for b in range(NB):
        step(dve.tensor_scalar(sin_arg[:, b, :], t.inv_freq[:], t.pos_f[:, b:b + 1], None, ALU.mult))
    step(dve.tensor_scalar(t.turns[:], sin_arg, float(1 / (2 * np.pi)), None, ALU.mult))
    step(dve.tensor_copy(t.turns_i[:], t.turns[:]))
    step(dve.tensor_copy(t.turns[:], t.turns_i[:]))
    two_pi, parts = 2 * np.pi, []
    for bits in (6, 9, 30):
        part = float(np.float32(two_pi if bits == 30 else np.floor(two_pi * 2.0 ** bits) / 2.0 ** bits))
        parts.append(part)
        two_pi -= part
    for part in parts:
        step(dve.scalar_tensor_tensor(out=sin_arg, in0=t.turns[:], scalar=-part, in1=sin_arg, op0=ALU.mult,
                                      op1=ALU.add))
    step(dve.tensor_scalar(cos_arg, sin_arg, float(np.pi / 2), None, ALU.add))
    pi = 3.141592
    for arg in (sin_arg, cos_arg):
        for op, turn in ((ALU.is_gt, -2 * np.pi), (ALU.is_lt, 2 * np.pi)):
            bound = pi if op == ALU.is_gt else -pi
            step(dve.tensor_scalar(t.turns[:], arg, bound, float(turn), op, ALU.mult))
            step(dve.tensor_tensor(arg, arg, t.turns[:], ALU.add))
    dve.tensor_scalar(t.ang[:], t.ang[:], -pi, pi, ALU.max, ALU.min).then_inc(s.angles, 1)

    for b in range(NB):
        bank, done = out_of(r1, f"sbv{b}")
        dve.tensor_copy(t.sb_v[:, b, :], bank[:]).then_inc(done, 1)

    def two(r, name):
        bank, done = out_of(r, name)
        return bank[:].rearrange("p (k n) -> p k n", k=2), done

    bank, done = two(r1, "gq")
    dve.tensor_scalar(t.g_q[:], bank, GLA_DK ** -0.5, None, ALU.mult).then_inc(done, 1)
    bank, done = two(r1, "gk")
    dve.tensor_copy(t.g_k[:], bank).then_inc(done, 1)

    def softplus_of(half):
        hs = slice(4 * half, 4 * half + 4)
        dve.wait_ge(s.sb_log, half + 1)
        step(dve.scalar_tensor_tensor(out=t.sb_s[:, hs, :], in0=t.z[:, hs, :], scalar=0.0, in1=t.sb_l[:, hs, :],
                                      op0=ALU.max, op1=ALU.add))
        for h in range(4 * half, 4 * half + 4):
            dve.tensor_tensor(t.sb_s[:, h, :], t.sb_s[:, h, :], t.sb_keep[:], ALU.mult).then_inc(s.sb_soft, 1)

    def arguments_of(half):
        for h in range(4 * half, 4 * half + 4):
            bank, done = out_of(r1, f"c{h}")
            dve.tensor_tensor(t.z[:, h, :], t.z[:, h, :], bank[:, 0:384], ALU.subtract).then_inc(done, 1)
        dve.wait_ge(*r1.drained(f"c{4 * half + 3}"))
        for h in range(4 * half, 4 * half + 4):
            ins = dve.tensor_tensor(t.z[:, h, :], t.z[:, h, :], t.sb_cap[:], ALU.min)
            if h % 4 < 3:
                step(ins)
        ins.then_inc(s.sb_arg, 1)

    dve.wait_ge(s.consts, 1)
    softplus_of(0)
    for b in range(NB):
        bank, done = out_of(r1, f"gv{b}")
        dve.tensor_copy(t.g_v[:, b, :], bank[:]).then_inc(done, 1)
    bank, done = out_of(r1, "ga")
    dve.tensor_copy(t.ga_T[0:RANK, :], bank[0:RANK, 0:T]).then_inc(done, 1)
    softplus_of(1)
    bank, done = two(r1, "al")
    step(dve.tensor_scalar(t.a_pre[:, 0, :], bank[:, 0, :], vec(t, "b_alpha", 0), None, ALU.add))
    dve.tensor_scalar(t.a_pre[:, 1, :], bank[:, 1, :], vec(t, "b_alpha", 1), None, ALU.add).then_inc(done, 1)
    arguments_of(0)

    dve.wait_ge(s.al_log, 1)
    dve.wait_ge(*r1.drained("al"))
    step(dve.tensor_scalar(t.a_pre[:], t.a_pre[:], -1.0, 0.0, ALU.mult, ALU.max))
    step(dve.tensor_tensor(t.a_pre[:], t.a_pre[:], t.al_l[:], ALU.add))
    for k in range(2):
        step(dve.tensor_tensor_scan(t.cum[:, k, :], t.chunk_start[:], t.a_pre[:, k, :], 0.0, ALU.mult, ALU.add))
    for k in range(2):
        by_chunk = t.cum[:, k, :].rearrange("p (c n) -> p c n", n=CH)
        ends = t.cum[:, k, CH - 1:T:CH]
        ins = dve.tensor_tensor(t.cum_end[:, k, :].rearrange("p (c n) -> p c n", n=CH), by_chunk, spread(ends, CH),
                                ALU.subtract)
        if k == 0:
            step(ins)
    ins.then_inc(s.gla_cum, 1)
    dve.wait_ge(s.gla_exp, 3)
    for k in range(2):
        step(dve.tensor_copy(t.chunk_decay[:, k, :], t.dec_q[:, k, CH - 1:T:CH]))
    dve.tensor_tensor(t.dec_q[:], t.g_q[:], t.dec_q[:], ALU.mult).then_inc(s.gla_dec, 1)
    dve.tensor_tensor(t.dec_k[:], t.g_k[:], t.dec_k[:], ALU.mult).then_inc(s.gla_dec, 1)
    dve.tensor_tensor(t.dec_e[:], t.g_k[:], t.dec_e[:], ALU.mult).then_inc(s.gla_dec, 1)
    arguments_of(1)

    def sigmoids(ap):
        step(dve.tensor_scalar(ap, ap, 1.0, None, ALU.add))
        step(dve.reciprocal(ap, ap))

    dve.wait_ge(*r1.drained("gr1"))
    sigmoids(t.gr_e[:])
    for f in range(4):
        step(dve.scalar_tensor_tensor(out=t.gr[:, f, :], in0=t.gr[:, f, :], scalar=vec(t, "gla_g", f),
                                      in1=t.gr_e[:, f, :], op0=ALU.mult, op1=ALU.mult))

    def sb_out(n):
        bank, done = two(r1, f"o{n}")
        dve.tensor_copy(t.o_sb[:, 2 * n:2 * n + 2, :], bank).then_inc(done, 1)

    sb_out(0)
    dve.wait_ge(*r1.drained("gate3"))
    sigmoids(t.gates[:, 0:KT])
    for c in range(3):
        if c < 2:
            bank, done = out_of(r1, f"ds{c}")
        else:
            bank = r1.bank("ds0")
        for h in range(GLA_H):
            rows, k = slice(GLA_DK * (h % 2), GLA_DK * (h % 2) + GLA_DK), h // 2
            c0 = (k * 2 + c // 2) * GLA_DV
            part, dst = bank[rows, c0:c0 + GLA_DV], t.state[rows, k, c, h % 2, :]
            if c == 0:
                ins = dve.tensor_copy(dst, part)
            else:
                ins = dve.scalar_tensor_tensor(out=dst, in0=t.state[rows, k, c - 1, h % 2, :],
                                               scalar=t.chunk_decay[rows, k, c:c + 1], in1=part, op0=ALU.mult,
                                               op1=ALU.add)
            if (c, h) in ((1, 3), (2, 3)):
                ins.then_inc(s.drained_dve, 1)
                dve.wait_ge(s.drained_dve, r1.drained(f"ds{c - 1}")[1])
            else:
                step(ins)
    sb_out(1)
    dve.wait_ge(*r1.drained("og1"))
    o_heads = t.o_gla.rearrange("p b (h n) -> p (b h) n", h=GLA_H)
    on_heads = t.o_n.rearrange("p b (h n) -> p (b h) n", h=GLA_H)
    step(dve.tensor_tensor(t.o_n, t.o_gla, t.o_gla, ALU.mult))
    step(dve.tensor_reduce(t.msq[:, NORM_AT["gla"], 0:8], on_heads, X, ALU.add))
    finish_mean("gla", [GLA_DV] * 8)
    dve.wait_ge(*r1.drained("gate7"))
    have_rstd("gla")
    dve.tensor_tensor(on_heads, o_heads, spread(t.rstd[:, NORM_AT["gla"], 0:8], GLA_DV),
                      ALU.mult).then_inc(s.o_n_ready, 1)
    for n in range(2):
        bank, done = two(r1, f"ogt{n}")
        pair = slice(2 * n, 2 * n + 2)
        dve.tensor_tensor(t.o_glaT[:, pair, :], bank, t.gr[:, pair, :], ALU.mult).then_inc(done, 1)
    for f in range(KT):
        bank, done = two(r1, f"y{f}")
        y_a, y_b = t.gr_e[:, 2 * (f % 2), :], t.gr_e[:, 2 * (f % 2) + 1, :]
        if f >= 2:
            dve.wait_ge(s.y_ready, f - 1)
        step(dve.tensor_tensor(y_a, bank[:, 0, :], t.gates[:, f, :], ALU.mult))
        dve.tensor_tensor(y_b, bank[:, 1, :], t.gates[:, KT + f, :], ALU.mult).then_inc(done, 1)
        dve.wait_ge(*r1.drained(f"y{f}"))
        dve.tensor_tensor(t.y_T[:, f, :], y_a, y_b, ALU.add).then_inc(s.y_ready, 1)
    for n in range(2):
        for b in range(NB):
            bank, done = out_of(r1, f"wo{n}{b}")
            cols = slice(512 * n, 512 * n + 512)
            dve.tensor_tensor(t.h[:, b, cols], t.h[:, b, cols], bank[:], ALU.add).then_inc(done, 1)
    dve.wait_ge(*r1.drained("wo11"))
    mean_squares_with_act("ffn")
    have_rstd("ffn")
    for b in range(NB):
        dve.tensor_scalar(t.x_n[:, b, :], t.h[:, b, :], rstd("ffn", b), None, ALU.mult).then_inc(s.x_n_ready, 1)
    for b in range(NB):
        for h in range(2):
            bank, done = out_of(r1, f"hT{b}{h}")
            dve.tensor_tensor(h_part(t.h_nT, b, h), bank[:].rearrange("p (k n) -> p k n", k=4),
                              spread(vec(t, "norm_ffn", 4 * h, 4), P), ALU.mult).then_inc(done, 1)
    for b in range(NB):
        for h in range(2):
            dve.wait_ge(s.h_rounded, 2 * b + h + 1)
            dve.tensor_tensor(h_part(t.h_lo, b, h), h_part(t.h_nT, b, h), h_part(t.h_hi, b, h).bitcast(F32),
                              ALU.subtract).then_inc(s.h_split, 1)
    step(dve.memset(t.a_pad[:, 0], 0.0))
    dve.memset(t.a_pad[:, 1], 0.0).then_inc(s.ff_zero, 1)

    conv_b = VEC_A["conv_b"]

    def ffn_lo(kind, i, i0):
        slot = ffn_chunk(g, kind, i0) % RING
        dve.wait_ge(s.ff_hi_done, ffn_made(kind, i)[0])
        if i0 > 0:
            dve.wait_ge(s.ff_a if kind == "a" else s.ff_o, i)
        dve.tensor_tensor(t.ff_lo[:, "ago".index(kind), :], t.ring[:, slot, :], t.ff_hi[:, slot, :].bitcast(F32),
                          ALU.subtract).then_inc(s.ff_lo_dve, 1)

    def ffn(i, q, i0):
        per = 6
        local = Steps(dve, s.ff_dve_step, i * per)
        dve.wait_ge(s.ff_pad, i + 1)
        for k in range(2):
            src, dst = t.a_pad[:, q, k, :], t.ff_c[:, q, k, :]
            tap = [t.vec_T[:, bass.ds(i * 2 + (VEC_A["conv_w"] + x * (D_FF // P) + k), 1)] for x in range(3)]
            bias = t.vec_T[:, bass.ds(i * 2 + (conv_b + k), 1)]
            local(dve.tensor_scalar(dst, src[:, 0:T], tap[0], bias, ALU.mult, ALU.add))
            for x in (1, 2):
                local(dve.scalar_tensor_tensor(out=dst, in0=src[:, x:T + x], scalar=tap[x], in1=dst, op0=ALU.mult,
                                               op1=ALU.add))
        dve.sem_inc(s.ff_conv, 1)
        if i0 + 1 < FF_STEPS:
            ffn_lo("a", i + 1, i0 + 1)
        ffn_lo("o", i, i0)
        dve.wait_ge(s.ff_gelu, i + 1)
        dve.wait_ge(s.ff_g, i + 1)
        if i0 > 1:
            dve.wait_ge(s.ff_o, i - 1)
        dve.tensor_tensor(t.ff_u[:, q], t.ff_ge[:, q], g.banks[6 + q][:].rearrange("p (k n) -> p k n", k=2),
                          ALU.mult).then_inc(s.ff_prod, 1)
        dve.wait_ge(s.u_hi_done, i + 1)
        dve.tensor_tensor(t.u_lo[:, q], t.ff_u[:, q], t.u_hi[:, q].bitcast(F32), ALU.subtract).then_inc(s.ff_u, 1)
        assert local.n == per

    ffn_lo("a", 0, 0)
    ffn(0, 0, 0)
    ffn(1, 1, 1)
    with dve.Fori(0, (FF_STEPS - 3) // 2) as m:
        ffn(m * 2 + 2, 0, 2)
        ffn(m * 2 + 3, 1, 3)
    ffn(FF_STEPS - 1, 0, FF_STEPS - 1)

    dve.wait_ge(s.ff_o, FF_STEPS)
    for b in range(NB):
        for n in range(2):
            cols = slice(512 * n, 512 * n + 512)
            step(dve.tensor_tensor(t.h[:, b, cols], t.h[:, b, cols], g.banks[2 * b + n][:], ALU.add))
        if b == 0:
            dve.sem_inc(s.rows_ready, 1)
    mean_squares_with_act("end1")
    have_rstd("end1")
    dve.wait_ge(s.small_in, 16 * 5)
    for b in range(NB):
        step(dve.scalar_tensor_tensor(out=t.h[:, b, :], in0=t.h[:, b, :], scalar=rstd("end1", b), in1=t.g_rows[:],
                                      op0=ALU.mult, op1=ALU.mult))
        if b == 0:
            dve.sem_inc(s.rows_ready, 1)

    mean_squares_with_act("attn")
    have_rstd("attn")
    for b in range(NB):
        dve.tensor_scalar(t.x_n[:, b, :], t.h[:, b, :], rstd("attn", b), None, ALU.mult).then_inc(s.x_n_ready, 1)
    turned(r2, "nT", t.h_nT2, "attn_norm")

    dve.wait_ge(*r2.drained("lat1"))
    mean_squares("lat", [(t.lat[:, b, 0:QL], t.lat_n[:, b, 0:QL], QL) for b in range(NB)]
                 + [(t.lat[:, b, QL:QL + KVL], t.lat_n[:, b, QL:QL + KVL], KVL) for b in range(NB)])

    def rope(dst, src, heads, b):
        def table(n):
            ap = t.sin_cos[:, n, b, :]
            return ap if heads is None else ap.unsqueeze(1).to_broadcast([P, heads, HALF])
        sin, cos = table(0), table(1)
        x1, x2 = (src[..., 0:HALF], src[..., HALF:]) if heads is None else (src[:, :, 0:HALF], src[:, :, HALF:])
        d1, d2 = (dst[..., 0:HALF], dst[..., HALF:]) if heads is None else (dst[:, :, 0:HALF], dst[:, :, HALF:])
        tmp = [t.rope_tmp[:, i, 0:1, :].squeeze(1) if heads is None else t.rope_tmp[:, i] for i in range(4)]
        for i, (a, c) in enumerate(((x1, cos), (x2, sin), (x2, cos), (x1, sin))):
            step(dve.tensor_tensor(tmp[i], a, c, ALU.mult))
        step(dve.tensor_tensor(d1, tmp[0], tmp[1], ALU.subtract))
        step(dve.tensor_tensor(d2, tmp[2], tmp[3], ALU.add))

    dve.wait_ge(s.rope_ready, 1)
    for b in range(NB):
        rope(t.k_rope[:, b, :], t.lat[:, b, QL + KVL:], None, b)
    have_rstd("lat")
    for b in range(NB):
        dve.tensor_scalar(t.lat_n[:, b, 0:QL], t.lat[:, b, 0:QL], rstd("lat", b), None,
                          ALU.mult).then_inc(s.lat_ready, 1)
        dve.tensor_scalar(t.lat_n[:, b, QL:], t.lat[:, b, QL:QL + KVL], rstd("lat", NB + b), None,
                          ALU.mult).then_inc(s.lat_ready, 1)
    bank, done = two(r2, "qlT")
    dve.tensor_tensor(t.ql_T[:], bank, spread(vec(t, "g_q_a", 0, 2), T), ALU.mult).then_inc(done, 1)
    bank, done = out_of(r2, "kvT")
    dve.tensor_scalar(t.kv_T[:], bank[:, 0:T], vec(t, "g_kv_a"), None, ALU.mult).then_inc(done, 1)
    for b in range(NB):
        step(dve.tensor_copy(t.k_tok[:, b, :, NOPE:], t.k_rope[:, b, :].unsqueeze(1).to_broadcast([P, MH, ROPE])))
    dve.wait_ge(*r2.drained("qq11"))
    for b in range(NB):
        q = t.q_tok[:, b, :].rearrange("p (h x) -> p h x", h=MH)[:, :, NOPE:]
        rope(q, q, MH, b)
    dve.sem_inc(s.q_roped, 1)
    for n in range(4):
        bank, done = two(r2, f"kT{n}")
        dve.tensor_copy(t.k_T[0:QK, 2 * n:2 * n + 2, :], bank[0:QK]).then_inc(done, 1)
    dve.wait_ge(s.consts2, 1)
    for h in range(MH):
        bank, done = out_of(r2, f"s{h}")
        dve.scalar_tensor_tensor(out=t.score[:, h, :], in0=bank[:, 0:384], scalar=QK ** -0.5, in1=t.at_mask[:],
                                 op0=ALU.mult, op1=ALU.add).then_inc(done, 1)
        if h % 4 == 3:
            dve.wait_ge(*r2.drained(f"s{h}"))
            hs = slice(h - 3, h + 1)
            step(dve.tensor_reduce(t.row_m[:, hs, 0], t.score[:, hs, 0:P], X, ALU.max))
            step(dve.tensor_reduce(t.row_m[:, hs, 1], t.score[:, hs, P:], X, ALU.max))
            dve.tensor_scalar(t.row_m[:, hs, :], t.row_m[:, hs, :], -1.0, None, ALU.mult).then_inc(s.row_max, 1)
    dve.wait_ge(*r2.drained("pm1"))
    step(dve.tensor_tensor(t.y_pool[:], t.y_pool[:], spread(vec(t, "pool_scale", 0, 4), T), ALU.mult))
    dve.tensor_tensor(t.y_sq[:], t.y_pool[:], t.y_pool[:], ALU.mult).then_inc(s.pool_sq, 1)
    dve.wait_ge(s.pool_sq, 1)
    dve.tensor_tensor(t.y_pool[:], t.y_pool[:], spread(vec(t, "g_out_pool", 0, 4), T), ALU.mult).then_inc(s.pool_y, 1)
    dve.wait_ge(s.prob_ready, NB * MH)
    step(dve.reciprocal(t.row_l[:], t.row_l[:]))
    bank, done = out_of(r2, "pss")
    dve.tensor_copy(t.pool_sum[:], bank[:, 0:NB]).then_inc(done, 1)
    dve.wait_ge(*r2.drained("pss"))
    for b in range(NB):
        bank, done = out_of(r2, f"av{b}")
        dve.tensor_tensor(t.y_att[:, b, :].rearrange("p (h n) -> p h n", h=MH),
                          bank[:].rearrange("p (h n) -> p h n", h=MH), spread(t.row_l[:, :, b], VD),
                          ALU.mult).then_inc(done, 1)
    dve.wait_ge(*r2.drained("av1"))
    mean_squares("mla", [(t.y_att[:, b, :], t.y_attn[:, b, :], 512) for b in range(NB)])
    k = NORM_AT["pool"]
    dve.tensor_scalar(t.msq[:, k, 0:NB], t.pool_sum[:], 1.0 / 512, EPS, ALU.mult, ALU.add).then_inc(s.msq_ready, 1)
    have_rstd("mla")
    for b in range(NB):
        dve.tensor_scalar(t.y_attn[:, b, :], t.y_att[:, b, :], rstd("mla", b), None,
                          ALU.mult).then_inc(s.y_attn_ready, 1)
    for b in range(NB):
        bank, done = out_of(r2, f"yt{b}")
        dve.tensor_tensor(t.ya_T[:, :, b * P:(b + 1) * P], bank[:].rearrange("p (k n) -> p k n", k=4),
                          spread(vec(t, "g_out_attn", 0, 4), P), ALU.mult).then_inc(done, 1)
    have_rstd("pool")
    for n in range(2):
        for b in range(NB):
            cols = slice(512 * n, 512 * n + 512)
            bank, done = out_of(r2, f"pa{n}{b}")
            dve.tensor_tensor(t.h[:, b, cols], t.h[:, b, cols], bank[:], ALU.add).then_inc(done, 1)
            dve.wait_ge(*r2.drained(f"pa{n}{b}"))
            bank, done = out_of(r2, f"pp{n}{b}")
            dve.scalar_tensor_tensor(out=t.h[:, b, cols], in0=bank[:], scalar=rstd("pool", b), in1=t.h[:, b, cols],
                                     op0=ALU.mult, op1=ALU.add).then_inc(done, 1)
    dve.wait_ge(*r2.drained("pp11"))
    mean_squares_with_act("moe")
    have_rstd("moe")
    dve.wait_ge(s.late_in, 16)
    for b in range(NB):
        dve.scalar_tensor_tensor(out=t.h_n[:, b, :], in0=t.h[:, b, :], scalar=rstd("moe", b), in1=t.g_rows[:],
                                 op0=ALU.mult, op1=ALU.mult).then_inc(s.h_ready, 1)

    bank, done = out_of(r2, "lg")
    dve.tensor_tensor(t.logits[:], bank[:, 0:NB * E].rearrange("p (b e) -> p b e", b=NB),
                      t.b_router[:].unsqueeze(1).to_broadcast([P, NB, E]), ALU.add).then_inc(done, 1)
    dve.wait_ge(*r2.drained("lg"))
    iota_e = t.iota_f[:, 0:E]
    for b in range(NB):
        step(dve.max(t.top[:, b, :], t.logits[:, b, :]))
        step(dve.max_index(t.top_i[:, b, :], t.top[:, b, :], t.logits[:, b, :]))
    dve.tensor_tensor(t.top_e[:], t.top[:, :, 0:TOPK], spread(t.top[:, :, 0], TOPK),
                      ALU.subtract).then_inc(s.top_ready, 1)
    step(dve.tensor_copy(t.top_f[:], t.top_i[:, :, 0:TOPK]))
    hot_shape = [P, NB, TOPK, E]
    step(dve.tensor_tensor(t.one_hot[:], iota_e.unsqueeze(1).unsqueeze(1).to_broadcast(hot_shape),
                           spread(t.top_f[:], E), ALU.is_equal))
    dve.tensor_reduce(t.mask[:], t.one_hot[:].rearrange("p b k e -> p b e k"), X, ALU.add).then_inc(s.mask_ready, 1)
    dve.wait_ge(s.top_exp, 1)
    step(dve.tensor_reduce(t.top_s[:], t.top_e[:], X, ALU.add))
    step(dve.reciprocal(t.top_s[:], t.top_s[:]))
    step(dve.tensor_tensor(t.top_e[:], t.top_e[:], spread(t.top_s[:], TOPK), ALU.mult))
    dve.wait_ge(s.mask_ready, 1)
    step(dve.tensor_tensor(t.one_hot[:], t.one_hot[:], spread(t.top_e[:], E), ALU.mult))
    dve.tensor_reduce(t.gate_e[:], t.one_hot[:].rearrange("p b k e -> p b e k"), X, ALU.add).then_inc(s.gates_ready, 1)
    dve.wait_ge(s.gates_ready, 1)
    bank, done = out_of(r2, "rk")
    rank = bank[:, 0:NB * E].rearrange("p (b e) -> p b e", b=NB)
    step(dve.tensor_scalar(t.count[:], bank[:, NB * E:NB * E + E], 1.0, None, ALU.mult))
    dve.scalar_tensor_tensor(out=t.pos_e[:], in0=rank, scalar=1000.0, in1=t.mask[:], op0=ALU.add,
                             op1=ALU.mult).then_inc(done, 1)
    dve.wait_ge(*r2.drained("rk"))
    step(dve.tensor_scalar(t.pos_e[:], t.pos_e[:], -1000.0, None, ALU.add))
    def pick(j):
        for b in range(NB):
            dve.tensor_scalar(t.picks[:, b, :], t.iota_s[:, 0:SLOTS], t.job_pos[:, b, bass.ds(j, 1)], None,
                              ALU.is_equal).then_inc(s.picked, 1)

    def pick_bias(j):
        dve.tensor_scalar(t.bias_sel[0:64, :], t.bias_col[0:64, :], t.job_sel[0:64, bass.ds(j, 1)], None,
                          ALU.mult).then_inc(s.bias_picked, 1)

    def x_lo(j):
        dve.wait_ge(s.x_copied, j + 1)
        dve.tensor_tensor(t.x_T[:, :, SLOTS:], g.banks[6][:].rearrange("p (k n) -> p k n", k=KT),
                          t.x_T[:, :, 0:SLOTS].bitcast(F32), ALU.subtract).then_inc(s.x_ready, 1)

    step(dve.tensor_copy(t.job_e[:, 0:E], iota_e))
    for b in range(NB):
        step(dve.tensor_copy(t.job_pos[:, b, 0:E], t.pos_e[:, b, :]))
        step(dve.tensor_copy(t.job_gate[:, b, 0:E], t.gate_e[:, b, :]))
    step(dve.tensor_scalar(t.job_sel[0:64, 0:E], t.job_e[0:64, 0:E], t.part32[0:64, :], None, ALU.is_equal))
    pick(0)
    pick_bias(0)
    dve.wait_ge(s.bias_hi, 1)
    dve.tensor_tensor(t.bias_hl[32:64, :], t.bias_raw[32:64, :], t.bias_hl[32:64, :].bitcast(F32),
                      ALU.subtract).then_inc(s.bias_ready, 1)
    dve.sem_inc(s.summed, 2)
    dve.sem_inc(s.act_ready, 2)
    step(dve.tensor_scalar(t.over[:], t.count[:], float(SLOTS), None, ALU.is_gt))
    for n in (2, 3):
        step(dve.scalar_tensor_tensor(out=t.over[:], in0=t.count[:], scalar=float(n * SLOTS), in1=t.over[:],
                                      op0=ALU.is_gt, op1=ALU.add))
    step(dve.memset(t.first_over[:], 1.0))
    step(dve.tensor_tensor_scan(t.end_over[:], t.first_over[:], t.over[:], 0.0, ALU.mult, ALU.add))
    step(dve.tensor_tensor(t.first_over[:], t.end_over[:], t.over[:], ALU.subtract))
    m_shape = [P, OVER + 1, E]
    m_iota = spread(t.iota_f[:, 0:OVER + 1], E)

    def per_job(ap):
        return ap.unsqueeze(1).to_broadcast(m_shape)

    step(dve.tensor_tensor(t.sel, m_iota, per_job(t.first_over[:]), ALU.is_ge))
    step(dve.tensor_tensor(t.sel_tmp, m_iota, per_job(t.end_over[:]), ALU.is_lt))
    step(dve.tensor_tensor(t.sel, t.sel, t.sel_tmp, ALU.mult))

    def choose(dst, values):
        step(dve.tensor_tensor(t.sel_tmp, t.sel, per_job(values), ALU.mult))
        step(dve.tensor_reduce(dst, t.sel_tmp, X, ALU.add))

    choose(t.job_e[:, E:], iota_e)
    for b in range(NB):
        if b == 1:
            x_lo(0)
        choose(t.job_gate[:, b, E:], t.gate_e[:, b, :])
        step(dve.scalar_tensor_tensor(out=t.pos_e[:, b, :], in0=t.first_over[:], scalar=float(SLOTS),
                                      in1=t.pos_e[:, b, :], op0=ALU.mult, op1=ALU.add))
        choose(t.job_pos[:, b, E:], t.pos_e[:, b, :])
        step(dve.scalar_tensor_tensor(out=t.job_pos[:, b, E:], in0=t.iota_f[:, 1:OVER + 2], scalar=-float(SLOTS),
                                      in1=t.job_pos[:, b, E:], op0=ALU.mult, op1=ALU.add))
    step(dve.tensor_scalar(t.job_sel[0:64, E:], t.job_e[0:64, E:], t.part32[0:64, :], None, ALU.is_equal))
    step(dve.tensor_copy(t.job_expert[0:1, :], t.job_e[0:1, :]))
    step(dve.tensor_scalar(t.count[0:1, 0:1], t.end_over[0:1, E - 1:E], float(E - 1), None, ALU.add))
    dve.tensor_copy(t.job_count[0:1, 0:1], t.count[0:1, 0:1]).then_inc(s.jobs_ready, 1)

    dve.wait_ge(s.jobs_ready, 1)
    last = dve.value_load(t.job_count[0:1, 0:1], min_val=E - 1, max_val=E + OVER - 1)

    def lo(j, c):
        dve.wait_ge(s.hi_done, j * JC + (c + 1))
        dve.tensor_tensor(t.w_lo[:, c % SPLIT, :], t.ring[:, (g.n_moe + c) % RING, :],
                          t.w_hi[:, c % SPLIT, :].bitcast(F32), ALU.subtract).then_inc(s.lo_dve, 1)

    def add_rows(j, r, dst):
        dve.wait_ge(s.lo_rows_ready, j * 4 + r + 1)
        dve.tensor_tensor(dst, g.banks[4 + r % 2][0:SLOTS, :], t.lo_rows[0:SLOTS, r % 2, :],
                          ALU.add).then_inc(s.summed, 1)
        dve.wait_ge(s.summed, j * 4 + r + 1 + 2)

    def swiglu_gate(j, half):
        dve.wait_ge(s.act_ready, j * 2 + half + 2)
        add_rows(j, 2 * half, t.gate[0:SLOTS, :])
        dve.tensor_scalar(t.gate[0:SLOTS, :], t.gate[0:SLOTS, :], SWIGLU_LIMIT, None,
                          ALU.min).then_inc(s.gate_ready, 1)

    dve.wait_ge(s.lo_dve, lo_count(DVE_LO, 0, SPLIT - 1))
    dve.wait_ge(s.half_done, 1 + 2)
    dve.memset(t.y_slot[:], 0.0).then_inc(s.y_copied, 2)
    dve.memset(t.mix_w[:], 0.0).then_inc(s.mix_ready, 1)
    swiglu_gate(0, 0)
    def turn(j, first=False, final=False):
        own = Steps(dve, s.job_dve_step, j * JOB_DVE_STEPS)

        def swiglu_up(half):
            up = t.act[0:SLOTS, half, :]
            dve.wait_ge(s.act_turned, j * 2 + half + 1)
            add_rows(j, 2 * half + 1, up)
            dve.wait_ge(s.gate_ready, j * 2 + half + 1)
            own(dve.tensor_scalar(up, up, SWIGLU_LIMIT, -SWIGLU_LIMIT, ALU.min, ALU.max))
            own(dve.scalar_tensor_tensor(out=up, in0=up, scalar=1.0, in1=t.gate[0:SLOTS, :], op0=ALU.add, op1=ALU.mult))
            dve.wait_ge(s.sig_ready, j * 2 + half + 1)
            dve.tensor_tensor(up, up, t.sig[0:SLOTS, :], ALU.mult).then_inc(s.act_ready, 1)

        def act_lo(half):
            dve.wait_ge(s.act_hi, j * 2 + half + 1)
            fs = slice(4 * half, 4 * half + 4)
            dve.tensor_tensor(t.act_T[:, fs, SLOTS:],
                              g.banks[7][:, 256 * half:256 * half + 256].rearrange("p (k n) -> p k n", k=4),
                              t.act_T[:, fs, 0:SLOTS].bitcast(F32), ALU.subtract).then_inc(s.act_lo, 1)

        def weights():
            dve.wait_ge(s.weights_turned, j + 1)
            for b in range(NB):
                dve.tensor_scalar(t.mix_in[:, b, :], t.iota_s[:], t.job_pos[:, b, bass.ds(j, 1)],
                                  t.job_gate[:, b, bass.ds(j, 1)], ALU.is_equal, ALU.mult).then_inc(s.mix_in_ready, 1)

        def next_tokens():
            dve.wait_ge(s.gathered, j + 1)
            pick(j + 1)

        def next_bias():
            dve.wait_ge(s.half_done, j * 6 + 3 + 1 + 2)
            pick_bias(j + 1)

        if not final:
            next_tokens()
        if not first:
            lo(j, 4)
            lo(j, 5)
        swiglu_up(0)
        lo(j, 7)
        swiglu_gate(j, 1)
        weights()
        act_lo(0)
        if final:
            swiglu_up(1)
            lo(j, 8)
            lo(j, 9)
            act_lo(1)
            lo(j, 11)
        else:
            next_bias()
            lo(j, 8)
            x_lo(j + 1)
            lo(j, 9)
            swiglu_up(1)
            lo(j, 11)
            act_lo(1)
            swiglu_gate(j + 1, 0)
            lo(j, 13)
            lo(j, 14)
        assert own.n == JOB_DVE_STEPS

    turn(0, first=True)
    with dve.Fori(0, last - 1) as m:
        turn(m + 1)
    turn(last, final=True)

    dve.wait_ge(s.closed, 1)
    for b in range(NB):
        for n in range(2):
            cols = slice(512 * n, 512 * n + 512)
            step(dve.tensor_tensor(t.h[:, b, cols], t.h[:, b, cols], g.banks[2 * b + n][:], ALU.add))
        if b == 0:
            dve.sem_inc(s.rows_ready, 1)
    mean_squares_with_act("end2")
    have_rstd("end2")
    dve.wait_ge(s.end_in, 16)
    for b in range(NB):
        dve.scalar_tensor_tensor(out=t.h[:, b, :], in0=t.h[:, b, :], scalar=rstd("end2", b), in1=t.g_rows[:],
                                 op0=ALU.mult, op1=ALU.mult).then_inc(s.out_ready, 1)


JOB_DVE_STEPS = 4


def tensor_program(g, pe):
    s, t, r1, r2, banks = g.s, g.t, g.r1, g.r2, g.banks

    def open_bank(r, name):
        room = r.room(name)
        if room is not None:
            pe.wait_ge(*room)
        return r.bank(name)

    def landed(n):
        slot, value = slot_use(n)
        pe.wait_ge(s.landed[slot], value)

    def halves(n, m):
        return [chunk(g, n + k // 4, (4, m))[:, k % 4, :] for k in range(KT)]

    def turn(r, prefix, src):
        for b in range(NB):
            for h in range(2):
                bank = open_bank(r, f"{prefix}{b}{h}")
                for k in range(4):
                    f = 4 * h + k
                    ins = pe.transpose(bank[:, k * P:(k + 1) * P], src[:, b, f * P:(f + 1) * P], t.ident[:])
                ins.then_inc(r.s.filled, 1)

    def project_T(r, names, weights, src, f0=0):
        for i, name in enumerate(names):
            bank = open_bank(r, name)
            for j in range(2):
                f = f0 + 2 * i + j
                for k, wk in enumerate(weights):
                    ins = pe.matmul(bank[:, j * T:(j + 1) * T], wk[:, f * P:(f + 1) * P], src[:, k, :],
                                    start=(k == 0), stop=(k == len(weights) - 1))
            ins.then_inc(r.s.filled, 1)

    def project(r, name, b, weights, src, c0, n):
        bank = open_bank(r, name)
        for k, wk in enumerate(weights):
            ins = pe.matmul(bank[:, 0:n], src[:, k, b * P:(b + 1) * P], wk[:, c0:c0 + n], start=(k == 0),
                            stop=(k == len(weights) - 1))
        ins.then_inc(r.s.filled, 1)

    pe.wait_ge(s.early_consts, 1)
    pe.wait_ge(s.vec_in, 16 * (len(VEC_A) + len(VEC_B)))
    bank = open_bank(r1, "vec")
    pe.transpose(bank[:, 0:ROWS_A], t.vec_a[0:ROWS_A, :], t.ident[0:ROWS_A, 0:ROWS_A])
    pe.transpose(bank[:, P:P + ROWS_B], t.vec_b[0:ROWS_B, :], t.ident[0:ROWS_B, 0:ROWS_B]).then_inc(s.filled, 1)
    pe.wait_ge(s.x_n_ready, NB)
    turn(r1, "xT", t.x_n)
    pe.wait_ge(*r1.drained("xT11"))

    def w_in(n):
        landed(n)
        landed(n + 1)
        return halves(n, 512)

    project_T(r1, ["sbq0", "sbq1"], w_in(0), t.x_nT)
    project_T(r1, ["sbk0", "sbk1"], w_in(2), t.x_nT)
    wv = w_in(4)
    for b in range(NB):
        project(r1, f"sbv{b}", b, wv, t.x_nT, 0, 512)

    def head_scores(h):
        bank = open_bank(r1, f"z{h}")
        rows = slice(SB_D * (h % 2), SB_D * (h % 2) + SB_D)
        k, q = t.sb_k[rows, h // 2, :], t.sb_q[rows, h // 2, :]
        pe.matmul(bank[:, 0:T], k[:, 0:P], q, start=True, stop=True)
        pe.matmul(bank[:, T:T + P], k[:, P:], q[:, P:], start=True, stop=True).then_inc(s.filled, 1)

    pe.wait_ge(*r1.drained("sbk1"))
    for h in range(4):
        head_scores(h)
    project_T(r1, ["gq", "gk"], w_in(6), t.x_nT)
    for h in range(4, 8):
        head_scores(h)
    wv = w_in(8)
    for b in range(NB):
        project(r1, f"gv{b}", b, wv, t.x_nT, 0, 512)
    pe.wait_ge(s.small_in, 16 * 5)
    bank = open_bank(r1, "ga")
    for k in range(KT):
        ins = pe.matmul(bank[0:RANK, 0:T], t.w_ga[:, k, :], t.x_nT[:, k, :], start=(k == 0), stop=(k == KT - 1))
    ins.then_inc(s.filled, 1)
    project_T(r1, ["gr0", "gr1"], w_in(10), t.x_nT)
    pe.wait_ge(*r1.drained("ga"))
    project_T(r1, ["al"], [t.w_alpha[0:RANK, :]], t.ga_T[0:RANK, :].unsqueeze(1))

    def key_sums(h):
        pe.wait_ge(s.sb_soft, h + 1)
        bank = open_bank(r1, f"c{h}")
        sp = t.sb_s[:, h, :]
        pe.matmul(bank[:, 0:T], t.tri[:], sp[:, 0:T], start=True, stop=False)
        pe.matmul(bank[:, P:T], t.ones[:], sp[:, T:], start=False, stop=True)
        pe.matmul(bank[:, T:T + P], t.tri[:], sp[:, T:], start=True, stop=True).then_inc(s.filled, 1)

    def sb_outputs(n):
        pe.wait_ge(s.sb_w, n + 1)
        bank = open_bank(r1, f"o{n}")
        for h in range(4 * n, 4 * n + 4):
            rows, c0 = slice(SB_D * (h % 2), SB_D * (h % 2) + SB_D), T * (h // 2 % 2)
            v, wt = t.sb_v[:, :, SB_D * h:SB_D * (h + 1)], t.sb_l[:, h, :]
            pe.matmul(bank[rows, c0:c0 + T], v[:, 0, :], wt[:, 0:T], start=True, stop=False)
            ins = pe.matmul(bank[rows, c0 + P:c0 + T], v[:, 1, :], wt[:, T:], start=False, stop=True)
        ins.then_inc(s.filled, 1)

    for h in range(4):
        key_sums(h)
    for q in range(2):
        project_T(r1, [f"gate{2 * q}", f"gate{2 * q + 1}"], w_in(12 + 2 * q), t.x_nT)
    for h in range(4, 8):
        key_sums(h)
    pe.wait_ge(s.gla_dec, 3)
    bank = open_bank(r1, "kend")
    for b in range(NB):
        for k in range(2):
            c0 = (2 * b + k) * P
            ins = pe.transpose(bank[:, c0:c0 + P], t.dec_e[:, k, b * P:(b + 1) * P], t.ident[:])
    ins.then_inc(s.filled, 1)

    def gla_rows(h):
        return slice(GLA_DK * (h % 2), GLA_DK * (h % 2) + GLA_DK)

    def chunk_rows(c):
        return slice(CH * (c % 2), CH * (c % 2) + CH)

    for n in range(2):
        bank = open_bank(r1, f"att{n}")
        for m, (h, b) in enumerate((h, b) for h in (n, n + 2) for b in range(NB)):
            toks = slice(b * P, (b + 1) * P)
            ins = pe.matmul(bank[:, m * P:(m + 1) * P], t.dec_k[gla_rows(h), h // 2, toks],
                            t.dec_q[gla_rows(h), h // 2, toks], start=True, stop=True)
        ins.then_inc(s.filled, 1)
    sb_outputs(0)
    for q in range(2, 4):
        project_T(r1, [f"gate{2 * q}", f"gate{2 * q + 1}"], w_in(12 + 2 * q), t.x_nT)
    pe.wait_ge(*r1.drained("kend"))
    for n, cs in enumerate(((0, 2), (1,))):
        bank = open_bank(r1, f"ds{n}")
        for h in range(GLA_H):
            for c in cs:
                c0 = (h // 2 * 2 + c // 2) * GLA_DV
                ins = pe.matmul(bank[gla_rows(h), c0:c0 + GLA_DV],
                                t.k_end[chunk_rows(c), c // 2, GLA_DK * h:GLA_DK * (h + 1)],
                                t.g_v[chunk_rows(c), c // 2, GLA_DV * h:GLA_DV * (h + 1)], start=True, stop=True)
        ins.then_inc(s.filled, 1)
    sb_outputs(1)
    pe.wait_ge(s.att_masked, 2)
    pe.wait_ge(*r1.drained("ds1"))
    for b in range(NB):
        bank = open_bank(r1, f"og{b}")
        for k in range(2):
            for h in (2 * k, 2 * k + 1):
                ins = pe.matmul(bank[:, GLA_DV * h:GLA_DV * (h + 1)], t.att[:, 4 * (h % 2) + 2 * k + b, :],
                                t.g_v[:, b, GLA_DV * h:GLA_DV * (h + 1)], start=(h == 0), stop=False,
                                skip_group_check=True)
            for c in (2 * b, 2 * b + 1):
                if c > 0:
                    ins = pe.matmul(bank[chunk_rows(c), 2 * GLA_DV * k:2 * GLA_DV * (k + 1)],
                                    t.dec_q[:, k, CH * c:CH * c + CH],
                                    t.state[:, k, c - 1].rearrange("p h n -> p (h n)"), start=False, stop=(c % 2 == 1),
                                    skip_group_check=True)
        ins.then_inc(s.filled, 1)
    pe.wait_ge(s.o_n_ready, 1)
    for n in range(2):
        bank = open_bank(r1, f"ogt{n}")
        for h in (2 * n, 2 * n + 1):
            for b in range(NB):
                c0 = (h % 2) * T + b * P
                ins = pe.transpose(bank[:, c0:c0 + P], t.o_n[:, b, GLA_DV * h:GLA_DV * (h + 1)], t.ident[:])
        ins.then_inc(s.filled, 1)
    pe.wait_ge(*r1.drained("ogt1"))
    for f in range(KT):
        n = 20 + 2 * (f // 4)
        landed(n)
        landed(n + 1)
        bank = open_bank(r1, f"y{f}")
        cols = slice(P * (f % 4), P * (f % 4) + P)
        for q, src in enumerate((t.o_sb, t.o_glaT)):
            for k in range(4):
                ins = pe.matmul(bank[:, q * T:(q + 1) * T], chunk(g, n + q, (4, 512))[:, k, cols], src[:, k, :],
                                start=(k == 0), stop=(k == 3))
        ins.then_inc(s.filled, 1)
    pe.wait_ge(s.y_ready, KT)
    for n in range(2):
        wo = w_in(24 + 2 * n)
        for b in range(NB):
            project(r1, f"wo{n}{b}", b, wo, t.y_T, 0, 512)
    pe.wait_ge(s.x_n_ready, 2 * NB)
    turn(r1, "hT", t.x_n)

    pe.wait_ge(*r1.drained("hT11"))
    pe.wait_ge(s.h_split, 2 * NB)
    for n in range(4):
        pe.matmul(banks[n][:], t.zrow[0:1, 0:P], t.zrow[0:1, P:], start=True, stop=False)

    def ffn_parts(kind, i, i0):
        slot = ffn_chunk(g, kind, i0) % RING
        pe.wait_ge(s.ff_lo_pool if kind == "g" else s.ff_lo_dve, ffn_made(kind, i)[1])
        kt = 2 if kind == "o" else KT
        return (t.ff_hi[:, slot, :].rearrange("p (k m) -> p k m", k=kt),
                t.ff_lo[:, "ago".index(kind), :].rearrange("p (k m) -> p k m", k=kt))

    def ffn_in(kind, i, i0, bank, done):
        w_hi, w_lo = ffn_parts(kind, i, i0)
        for f in range(2):
            for k in range(KT):
                for part, (wt, ht) in enumerate(((w_hi, t.h_hi), (w_hi, t.h_lo), (w_lo, t.h_hi))):
                    ins = pe.matmul(bank[:, f * T:(f + 1) * T], wt[:, k, f * P:(f + 1) * P], ht[:, k, :],
                                    start=(k == 0 and part == 0), stop=(k == KT - 1 and part == 2))
        ins.then_inc(done, 1)

    def ffn_out(i, i0, q, end=False):
        w_hi, w_lo = ffn_parts("o", i, i0)
        pe.wait_ge(s.ff_u, i + 1)
        for b in range(NB):
            for c in range(2):
                for k in range(2):
                    for part, (ut, wt) in enumerate(((t.u_hi, w_hi), (t.u_hi, w_lo), (t.u_lo, w_hi))):
                        last = end and k == 1 and part == 2
                        ins = pe.matmul(banks[2 * b + c][:], ut[:, q, k, b * P:(b + 1) * P],
                                        wt[:, k, 512 * c:512 * c + 512], start=False, stop=last,
                                        skip_group_check=not last)
        ins.then_inc(s.ff_o, 1)

    ffn_in("a", 0, 0, banks[4], s.ff_a)
    ffn_in("g", 0, 0, banks[6], s.ff_g)
    with pe.Fori(0, (FF_STEPS - 1) // 2) as m:
        for q in range(2):
            pe.wait_ge(s.ff_pad, m * 2 + (q + 1))
            ffn_in("a", m * 2 + (q + 1), q + 1, banks[5 - q], s.ff_a)
            ffn_out(m * 2 + q, q, q)
            ffn_in("g", m * 2 + (q + 1), q + 1, banks[7 - q], s.ff_g)
    ffn_out(FF_STEPS - 1, FF_STEPS - 1, 0, end=True)

    pe.wait_ge(s.x_n_ready, 3 * NB)
    turn(r2, "nT", t.x_n)
    pe.wait_ge(*r2.drained("nT11"))
    n = g.n_second
    landed(n)
    landed(n + 1)
    wl = halves(n, 416)
    for b in range(NB):
        project(r2, f"lat{b}", b, wl, t.h_nT2, 0, 416)
    landed(n + 2)
    landed(n + 3)
    project_T(r2, ["u0", "u1"], halves(n + 2, 512), t.h_nT2)
    pe.wait_ge(s.lat_ready, 2 * NB)
    bank = open_bank(r2, "qlT")
    for k in range(2):
        for b in range(NB):
            ins = pe.transpose(bank[:, k * T + b * P:k * T + (b + 1) * P], t.lat_n[:, b, k * P:(k + 1) * P], t.ident[:])
    ins.then_inc(s.filled2, 1)
    bank = open_bank(r2, "kvT")
    for b in range(NB):
        ins = pe.transpose(bank[:, b * P:(b + 1) * P], t.lat_n[:, b, QL:QL + KVL], t.ident[:])
    ins.then_inc(s.filled2, 1)
    landed(n + 4)
    pe.wait_ge(*r2.drained("qlT"))
    wq = chunk(g, n + 4, (2, 768))
    for b in range(NB):
        for c in range(2):
            project(r2, f"qq{b}{c}", b, [wq[:, k, :] for k in range(2)], t.ql_T, 384 * c, 384)
    landed(n + 5)
    pe.wait_ge(*r2.drained("kvT"))
    wkv = chunk(g, n + 5, (1, 1024))
    for b in range(NB):
        for c in range(2):
            project(r2, f"kv{b}{c}", b, [wkv[:, 0, :]], t.kv_T[:].unsqueeze(1), 512 * c, 512)
    pe.wait_ge(s.q_roped, 1)
    pe.wait_ge(*r2.drained("kv11"))
    for prefix, src in (("qT", [t.q_tok[:, b, :].rearrange("p (h x) -> p h x", h=MH) for b in range(NB)]),
                        ("kT", [t.k_tok[:, b] for b in range(NB)])):
        for m in range(4):
            bank = open_bank(r2, f"{prefix}{m}")
            for h in (2 * m, 2 * m + 1):
                for b in range(NB):
                    c0 = (h % 2) * T + b * P
                    ins = pe.transpose(bank[0:QK, c0:c0 + P], src[b][:, h, :], t.ident[:])
            ins.then_inc(s.filled2, 1)
    pe.wait_ge(*r2.drained("qT3"))
    pe.wait_ge(*r2.drained("kT3"))
    for h in range(MH):
        bank = open_bank(r2, f"s{h}")
        pe.matmul(bank[:, 0:P], t.q_T[0:QK, h, 0:P], t.k_T[0:QK, h, 0:P], start=True, stop=True)
        pe.matmul(bank[:, P:3 * P], t.q_T[0:QK, h, P:], t.k_T[0:QK, h, :], start=True, stop=True).then_inc(s.filled2, 1)
    landed(n + 6)
    pe.wait_ge(s.diff_ready, 1)
    w_pool = chunk(g, n + 6, (4, P))
    for m in range(2):
        bank = open_bank(r2, f"pm{m}")
        for i in range(2):
            ins = pe.matmul(bank[:, i * T:(i + 1) * T], w_pool[:, 2 * m + i, :], t.diff[:, 2 * m + i, :],
                            start=True, stop=True)
        ins.then_inc(s.filled2, 1)
    pe.wait_ge(s.pool_sq, 1)
    bank = open_bank(r2, "pss")
    for b in range(NB):
        for k in range(4):
            ins = pe.matmul(bank[:, b:b + 1], t.y_sq[:, k, b * P:(b + 1) * P], t.ones[:, 0:1], start=(k == 0),
                            stop=(k == 3))
    ins.then_inc(s.filled2, 1)
    for h in range(MH):
        pe.wait_ge(s.prob_ready, NB * (h + 1))
        bank = open_bank(r2, f"pt{h}")
        for k in range(3):
            ins = pe.transpose(bank[:, k * P:(k + 1) * P], t.score[:, h, k * P:(k + 1) * P], t.ident[:])
        ins.then_inc(s.filled2, 1)
    pe.wait_ge(*r2.drained("pt7"))
    for b in range(NB):
        bank = open_bank(r2, f"av{b}")
        for h in range(MH):
            dst = bank[:, VD * h:VD * (h + 1)]
            for k in range(b + 1):
                c0 = (b + k) * P
                ins = pe.matmul(dst, t.prob_T[:, h, c0:c0 + P], t.v_tok[:, k, h, :], start=(k == 0), stop=(k == b))
        ins.then_inc(s.filled2, 1)
    for b in range(NB):
        pe.wait_ge(s.y_attn_ready, b + 1)
        bank = open_bank(r2, f"yt{b}")
        for k in range(4):
            ins = pe.transpose(bank[:, k * P:(k + 1) * P], t.y_attn[:, b, k * P:(k + 1) * P], t.ident[:])
        ins.then_inc(s.filled2, 1)
    pe.wait_ge(*r2.drained("yt1"))
    pe.wait_ge(s.pool_y, 1)
    for c in range(2):
        landed(n + 7 + 2 * c)
        landed(n + 8 + 2 * c)
        for b in range(NB):
            for q, (prefix, src) in enumerate((("pa", t.ya_T), ("pp", t.y_pool))):
                wt = chunk(g, n + 7 + 2 * c + q, (4, 512))
                project(r2, f"{prefix}{c}{b}", b, [wt[:, k, :] for k in range(4)], src, 0, 512)
    pe.wait_ge(s.h_ready, NB)
    turn(r2, "rT", t.x_n)
    pe.wait_ge(*r2.drained("rT11"))
    pe.wait_ge(s.small_in, 16 * 5)
    bank = open_bank(r2, "lg")
    for b in range(NB):
        for k in range(KT):
            ins = pe.matmul(bank[:, b * E:(b + 1) * E], t.h_T[:, k, b * P:(b + 1) * P], t.w_router[:, k, :],
                            start=(k == 0), stop=(k == KT - 1))
    ins.then_inc(s.filled2, 1)
    pe.wait_ge(s.mask_ready, 1)
    bank = open_bank(r2, "rk")
    pe.matmul(bank[:, 0:E], t.before[:], t.mask[:, 0, :], start=True, stop=True)
    pe.matmul(bank[:, E:2 * E], t.ones[:], t.mask[:, 0, :], start=True, stop=False)
    pe.matmul(bank[:, E:2 * E], t.before[:], t.mask[:, 1, :], start=False, stop=True)
    for b in range(NB):
        ins = pe.matmul(bank[:, 2 * E:3 * E], t.ones[:], t.mask[:, b, :], start=(b == 0), stop=(b == 1))
    ins.then_inc(s.filled2, 1)
    bank = open_bank(r2, "gT")
    pe.wait_ge(s.gates_ready, 1)
    for b in range(NB):
        ins = pe.transpose(bank[0:E, b * P:(b + 1) * P], t.gate_e[:, b, :], t.ident[:])
    ins.then_inc(s.filled2, 1)

    def gather(j):
        pe.wait_ge(s.picked, j * NB + NB)
        for f in range(KT):
            for b in range(NB):
                ins = pe.matmul(banks[6][:, f * SLOTS:(f + 1) * SLOTS], t.h_n[:, b, f * P:(f + 1) * P],
                                t.picks[:, b, :], start=(b == 0), stop=(b == 1))
        ins.then_inc(s.gathered, 1)

    def turn(j, half):
        pe.wait_ge(s.act_ready, j * 2 + half + 1 + 2)
        pe.wait_ge(s.act_lo, j * 2 + half + 2)
        for k in range(4):
            c0 = 256 * half + k * SLOTS
            ins = pe.matmul(banks[7][:, c0:c0 + SLOTS], t.act[0:SLOTS, half, k * P:(k + 1) * P],
                            t.ident[0:SLOTS, 0:SLOTS], start=True, stop=True)
        ins.then_inc(s.act_turned, 1)

    def half_group(j, r, half, stationary, bias=None):
        bank = banks[4 + r % 2]
        c = 2 * r + half
        if bias is not None and half == 0:
            pe.matmul(bank[:], t.bias_sel[0:64, :], t.bias_hl[0:64, bias:bias + 512], start=True, stop=False)
        pe.wait_ge(s.hi_done, j * JC + (c + 1))
        sem, lo_of = lo_maker(s, c)
        pe.wait_ge(sem, lo_count(lo_of, j, c))
        for k in range(4):
            for part, wt in enumerate((t.w_hi, t.w_lo)):
                ins = pe.matmul(bank[:], stationary[:, 4 * half + k, :], wt[:, c % SPLIT, 512 * k:512 * k + 512],
                                start=(bias is None and half == 0 and k == 0 and part == 0),
                                stop=(half == 1 and k == 3 and part == 1))
        ins.then_inc(s.group_done if half else s.half_done, 1)

    def combine(j, c):
        pe.wait_ge(s.y_copied, j * 2 + c + 1)
        for b in range(NB):
            ins = pe.matmul(banks[2 * b + c][:], t.mix_w[:, b * P:(b + 1) * P], t.y_slot[:, c, :], start=False,
                            stop=False, skip_group_check=True)
        ins.then_inc(s.combined, 1)

    pe.wait_ge(*r2.drained("rk"))
    gather(0)
    pe.wait_ge(*r2.drained("gT"))
    pe.wait_ge(s.b_down_in, 16)
    for b in range(NB):
        for c in range(2):
            pe.matmul(banks[2 * b + c][:], t.gate_T[0:E, b * P:(b + 1) * P], t.b_down[0:E, 512 * c:512 * c + 512],
                      start=True, stop=False, skip_group_check=True)
    pe.wait_ge(s.bias_ready, 1)
    for sem in (s.half_done, s.group_done, s.act_lo, s.act_turned):
        pe.sem_inc(sem, 2)
    pe.sem_inc(s.weights_turned, 1)
    pe.wait_ge(s.bias_picked, 1)
    pe.wait_ge(s.x_ready, 1)
    for half in range(2):
        half_group(0, 0, half, t.x_T, bias=0)
    pe.wait_ge(s.jobs_ready, 1)
    last = pe.value_load(t.job_count[0:1, 0:1], min_val=E - 1, max_val=E + OVER - 1)
    def job_turn(j, final=False):
        pe.wait_ge(s.y_copied, j * 2 + 1)
        half_group(j, 1, 0, t.x_T, bias=FE)
        pe.wait_ge(s.mix_ready, j + 1)
        if not final:
            gather(j + 1)
        half_group(j, 1, 1, t.x_T)
        pe.wait_ge(s.y_copied, j * 2 + 2)
        pe.wait_ge(s.summed, j * 4 + 1 + 2)
        half_group(j, 2, 0, t.x_T, bias=512)
        half_group(j, 2, 1, t.x_T)
        turn(j, 0)
        pe.wait_ge(s.summed, j * 4 + 2 + 2)
        half_group(j, 3, 0, t.x_T, bias=FE + 512)
        half_group(j, 3, 1, t.x_T)
        combine(j, 0)
        combine(j, 1)
        r = 4
        if not final:
            pe.wait_ge(s.summed, j * 4 + 3 + 2)
            pe.wait_ge(s.bias_picked, j + 2)
            pe.wait_ge(s.x_ready, j + 2)
            half_group(j, r, 0, t.x_T, bias=0)
            half_group(j, r, 1, t.x_T)
            r = 5
        turn(j, 1)
        pe.wait_ge(s.summed, j * 4 + (r - 1 + 2))
        pe.wait_ge(s.act_lo, j * 2 + 1 + 2)
        half_group(j, r, 0, t.act_T)
        pe.wait_ge(s.mix_in_ready, j * 2 + 2)
        for b in range(NB):
            ins = pe.transpose(banks[6][:, b * P:(b + 1) * P], t.mix_in[:, b, :], t.ident[:])
        ins.then_inc(s.weights_turned, 1)
        pe.wait_ge(s.act_lo, j * 2 + 2 + 2)
        half_group(j, r, 1, t.act_T)
        pe.wait_ge(s.summed, j * 4 + (r + 2))
        half_group(j, r + 1, 0, t.act_T)
        half_group(j, r + 1, 1, t.act_T)

    with pe.Fori(0, last) as j:
        job_turn(j)
    job_turn(last, final=True)
    pe.wait_ge(s.mix_ready, last + 2)
    combine(last + 1, 0)
    combine(last + 1, 1)
    for n in range(4):
        ins = pe.matmul(banks[n][:], t.zrow[0:1, 0:P], t.zrow[0:1, P:], start=False, stop=True, skip_group_check=True)
    ins.then_inc(s.closed, 1)


class Semaphores:
    def __init__(self, new):
        self.filled = new("filled")
        self.drained_act = new("drained_act")
        self.drained_dve = new("drained_dve")
        self.filled2 = new("filled2")
        self.drained_act2 = new("drained_act2")
        self.drained_dve2 = new("drained_dve2")
        self.early_consts = new("early_consts")
        self.consts = new("consts")
        self.consts2 = new("consts2")
        self.pool_step = new("pool_step")
        self.act_step = new("act_step")
        self.dve_step = new("dve_step")
        self.x_in = new("x_in")
        self.vec_in = new("vec_in")
        self.pos_in = new("pos_in")
        self.small_in = new("small_in")
        self.late_in = new("late_in")
        self.end_in = new("end_in")
        self.bias_in = new("bias_in")
        self.b_down_in = new("b_down_in")
        self.angles = new("angles")
        self.rope_ready = new("rope_ready")
        self.msq_ready = new("msq_ready")
        self.rows_ready = new("rows_ready")
        self.act_msq = new("act_msq")
        self.rstd_ready = new("rstd_ready")
        self.x_n_ready = new("x_n_ready")
        self.sb_log = new("sb_log")
        self.sb_soft = new("sb_soft")
        self.sb_arg = new("sb_arg")
        self.sb_w = new("sb_w")
        self.al_log = new("al_log")
        self.gla_cum = new("gla_cum")
        self.gla_exp = new("gla_exp")
        self.gla_dec = new("gla_dec")
        self.att_masked = new("att_masked")
        self.o_n_ready = new("o_n_ready")
        self.y_ready = new("y_ready")
        self.ff_zero = new("ff_zero")
        self.ff_a = new("ff_a")
        self.ff_g = new("ff_g")
        self.ff_o = new("ff_o")
        self.h_rounded = new("h_rounded")
        self.h_split = new("h_split")
        self.ff_prod = new("ff_prod")
        self.ff_hi_done = new("ff_hi_done")
        self.ff_lo_dve = new("ff_lo_dve")
        self.ff_lo_pool = new("ff_lo_pool")
        self.u_hi_done = new("u_hi_done")
        self.ff_pad = new("ff_pad")
        self.ff_conv = new("ff_conv")
        self.ff_gelu = new("ff_gelu")
        self.ff_u = new("ff_u")
        self.ff_dve_step = new("ff_dve_step")
        self.lat_ready = new("lat_ready")
        self.diff_ready = new("diff_ready")
        self.q_roped = new("q_roped")
        self.row_max = new("row_max")
        self.prob_ready = new("prob_ready")
        self.pool_sq = new("pool_sq")
        self.pool_y = new("pool_y")
        self.y_attn_ready = new("y_attn_ready")
        self.h_ready = new("h_ready")
        self.top_ready = new("top_ready")
        self.top_exp = new("top_exp")
        self.mask_ready = new("mask_ready")
        self.gates_ready = new("gates_ready")
        self.jobs_ready = new("jobs_ready")
        self.bias_hi = new("bias_hi")
        self.bias_ready = new("bias_ready")
        self.picked = new("picked")
        self.bias_picked = new("bias_picked")
        self.gathered = new("gathered")
        self.x_copied = new("x_copied")
        self.x_ready = new("x_ready")
        self.hi_done = new("hi_done")
        self.lo_dve = new("lo_dve")
        self.lo_pool = new("lo_pool")
        self.half_done = new("half_done")
        self.group_done = new("group_done")
        self.lo_rows_ready = new("lo_rows_ready")
        self.summed = new("summed")
        self.gate_ready = new("gate_ready")
        self.sig_ready = new("sig_ready")
        self.act_ready = new("act_ready")
        self.act_turned = new("act_turned")
        self.act_hi = new("act_hi")
        self.act_lo = new("act_lo")
        self.mix_in_ready = new("mix_in_ready")
        self.weights_turned = new("weights_turned")
        self.mix_ready = new("mix_ready")
        self.y_copied = new("y_copied")
        self.combined = new("combined")
        self.job_dve_step = new("job_dve_step")
        self.closed = new("closed")
        self.out_ready = new("out_ready")
        self.stored = new("stored")
        self.landed = [new(f"landed{n}") for n in range(RING)]


class Filled2:

    def __init__(self, s):
        self.filled, self.drained_act, self.drained_dve = s.filled2, s.drained_act2, s.drained_dve2


class Buffers:

    def persistent(self, new):
        self.h = new("h", [NB, D])
        self.x_n = new("x_n", [NB, D])
        self.ring = new("ring", [RING, CW])
        self.ident = new("ident", [P])
        self.ones = new("ones", [P])
        self.before = new("before", [P])
        self.neg_half = new("neg_half", [8])
        self.inv_freq = new("inv_freq", [HALF])
        self.vec_T = new("vec_T", [ROWS_A + ROWS_B])
        self.zrow = new("zrow", [P + 512], mybir.dt.bfloat16)
        self.g_rows = new("g_rows", [D])
        self.w_router = new("w_router", [KT, E])
        self.b_router = new("b_router", [E])
        self.sin_cos = new("sin_cos", [2, NB, HALF])
        self.msq = new("msq", [len(NORMS), 8])
        self.rstd = new("rstd", [len(NORMS), 8])
        self.job_expert = new("job_expert", [JOBS], I32)
        self.job_count = new("job_count", [1], I32)
        self.job_pos = new("job_pos", [NB, JOBS])
        self.job_gate = new("job_gate", [NB, JOBS])
        self.job_sel = new("job_sel", [JOBS])
        self.iota_s = new("iota_s", [2 * SLOTS])
        self.bias_col = new("bias_col", [2 * SLOTS])
        self.gate_T = new("gate_T", [T])

    def mixer(self, new):
        self.vec_a = new("vec_a", [P])
        self.vec_b = new("vec_b", [P])
        self.tri = new("tri", [P])
        self.pos_i = new("pos_i", [NB], I32)
        self.pos_f = new("pos_f", [NB])
        self.turns = new("turns", [NB, HALF])
        self.turns_i = new("turns_i", [NB, HALF], I32)
        self.ang = new("ang", [2, NB, HALF])
        self.w_ga = new("w_ga", [KT, RANK])
        self.w_alpha = new("w_alpha", [KW])
        self.neg_b_gate = new("neg_b_gate", [16])
        self.x_nT = new("x_nT", [KT, T])
        self.sb_q = new("sb_q", [4, T])
        self.sb_k = new("sb_k", [4, T])
        self.sb_v = new("sb_v", [NB, 512])
        self.z = new("z", [SB_H, 384])
        self.sb_l = new("sb_l", [SB_H, 384])
        self.sb_s = new("sb_s", [SB_H, 384])
        self.sb_keep = new("sb_keep", [384])
        self.sb_cap = new("sb_cap", [384])
        self.g_q = new("g_q", [2, T])
        self.g_k = new("g_k", [2, T])
        self.g_v = new("g_v", [NB, VW])
        self.gr = new("gr", [4, T])
        self.gr_e = new("gr_e", [4, T])
        self.ga_T = new("ga_T", [T])
        self.a_pre = new("a_pre", [2, T])
        self.al_l = new("al_l", [2, T])
        self.chunk_start = new("chunk_start", [T])
        self.cum = new("cum", [2, T])
        self.cum_end = new("cum_end", [2, T])
        self.dec_q = new("dec_q", [2, T])
        self.dec_k = new("dec_k", [2, T])
        self.dec_e = new("dec_e", [2, T])
        self.chunk_decay = new("chunk_decay", [2, 4])
        self.k_end = new("k_end", [NB, KW])
        self.att = new("att", [8, P])
        self.state = new("state", [2, 3, 2, GLA_DV])
        self.gates = new("gates", [16, T])
        self.o_sb = new("o_sb", [4, T])

    def ffn(self, new):
        self.h_nT = new("h_nT", [KT, T])
        self.h_hi = new("h_hi", [KT, T], F32R)
        self.h_lo = new("h_lo", [KT, T], F32R)
        self.ff_hi = new("ff_hi", [RING, CW], F32R)
        self.ff_lo = new("ff_lo", [3, CW], F32R)
        self.u_hi = new("u_hi", [2, 2, T], F32R)
        self.u_lo = new("u_lo", [2, 2, T], F32R)
        self.a_pad = new("a_pad", [2, 2, 2 + T])
        self.ff_c = new("ff_c", [2, 2, T])
        self.ff_ge = new("ff_ge", [2, 2, T])
        self.ff_u = new("ff_u", [2, 2, T])

    def attention(self, new):
        self.h_nT2 = new("h_nT2", [KT, T])
        self.lat = new("lat", [NB, 416])
        self.lat_n = new("lat_n", [NB, 384])
        self.k_rope = new("k_rope", [NB, ROPE])
        self.rope_tmp = new("rope_tmp", [4, MH, HALF])
        self.u_pad = new("u_pad", [4, 16 + T])
        self.win_a = new("win_a", [4, 16 + T])
        self.win_b = new("win_b", [4, 16 + T])
        self.diff = new("diff", [4, T])
        self.inv_count = new("inv_count", [4, T])
        self.at_mask = new("at_mask", [384])
        self.ql_T = new("ql_T", [2, T])
        self.kv_T = new("kv_T", [T])
        self.q_tok = new("q_tok", [NB, MH * QK])
        self.k_tok = new("k_tok", [NB, MH, QK])
        self.v_tok = new("v_tok", [NB, MH, VD])
        self.q_T = new("q_T", [MH, T])
        self.k_T = new("k_T", [MH, T])
        self.score = new("score", [MH, 384])
        self.row_m = new("row_m", [MH, NB])
        self.row_l = new("row_l", [MH, NB])
        self.prob_T = new("prob_T", [MH, 384])
        self.y_pool = new("y_pool", [4, T])
        self.y_sq = new("y_sq", [4, T])
        self.pool_sum = new("pool_sum", [NB])
        self.y_att = new("y_att", [NB, 512])
        self.y_attn = new("y_attn", [NB, 512])
        self.ya_T = new("ya_T", [4, T])
        self.h_T = new("h_T", [KT, T])
        self.iota_i = new("iota_i", [P], I32)
        self.iota_f = new("iota_f", [JOBS])
        self.part32 = new("part32", [1])
        self.logits = new("logits", [NB, E])
        self.top = new("top", [NB, 8])
        self.top_i = new("top_i", [NB, 8], U32)
        self.top_f = new("top_f", [NB, TOPK])
        self.top_e = new("top_e", [NB, TOPK])
        self.top_s = new("top_s", [NB])
        self.one_hot = new("one_hot", [NB, TOPK, E])
        self.mask = new("mask", [NB, E])
        self.gate_e = new("gate_e", [NB, E])
        self.count = new("count", [E])
        self.pos_e = new("pos_e", [NB, E])
        self.over = new("over", [E])
        self.first_over = new("first_over", [E])
        self.end_over = new("end_over", [E])
        self.job_e = new("job_e", [JOBS])

    def experts_weights(self, new):
        self.w_hi = new("w_hi", [SPLIT, CW], F32R)
        self.w_lo = new("w_lo", [SPLIT, CW], F32R)

    def experts_rows(self, new):
        self.x_T = new("x_T", [KT, 2 * SLOTS], F32R)
        self.act_T = new("act_T", [KT, 2 * SLOTS], F32R)
        self.bias_hl = new("bias_hl", [2 * FE], F32R)
        self.picks = new("picks", [NB, SLOTS])
        self.bias_sel = new("bias_sel", [2 * SLOTS], F32R)

    def scratch(self, new):
        self.mix_in = new("mix_in", [NB, 2 * SLOTS])
        self.mix_w = new("mix_w", [T])
        self.lo_rows = new("lo_rows", [2, 512])
        self.gate = new("gate", [512])
        self.sig = new("sig", [512])
        self.act = new("act", [2, 512])
        self.y_slot = new("y_slot", [2, 512])

    def bias_early(self, new):
        self.bias_raw = new("bias_raw", [2 * FE])

    def down_early(self, new):
        self.b_down = new("b_down", [D])


VECTORS = dict(norm_mix="norm_mix_g", norm_ffn="norm_ffn_g", attn_norm="g_attn_norm_2", ffn_norm="g_ffn_norm_2",
               conv_w="conv_w", conv_b="conv_b", b_alpha="b_alpha", gla_g="gla_norm_g", b_pool="b_pool_2",
               pool_scale="pool_scale_2", g_q_a="g_q_a_2", g_kv_a="g_kv_a_2", g_out_pool="g_out_pool_2",
               g_out_attn="g_out_attn_2", b_gate="b_gate")
INPUTS = (
    "x norm_mix_g w_in b_gate w_alpha_up b_alpha gla_norm_g w_branch_sb w_branch_gla w_out norm_ffn_g w_ffn_in conv_w "
    "conv_b w_ffn_out norm_final_g positions_2 g_attn_norm_2 w_in_2 w_pool_2 b_pool_2 pool_scale_2 g_q_a_2 w_q_b_2 "
    "g_kv_a_2 w_kv_b_2 g_out_pool_2 g_out_attn_2 w_out_2 g_ffn_norm_2 w_router_2 b_router_2 w_gate_up_2 b_gate_up_2 "
    "w_down_2 b_down_2 g_final_2"
).split()


def views(aps):
    w = {name: ap if name in ("norm_final_g", "g_final_2") else ap.squeeze(0) for name, ap in aps.items()}
    w["positions"] = w["positions_2"]
    for name in ("norm_final_g", "g_final_2", "g_ffn_norm_2", "b_router_2"):
        w["row_" + name] = w[name].rearrange("(a n) -> a n", a=1)
    w["vectors"] = {key: w[name] if len(w[name].shape) == 2 else w[name].rearrange("(a n) -> a n", a=1)
                    for key, name in VECTORS.items()}
    return w


def kernel(**inputs):
    import concourse.bacc as bacc
    from concourse.bass_utils import run_bass_kernel_spmd

    nc = bacc.Bacc("TRN2", target_bir_lowering=False, num_devices=1)
    arrays, aps = {}, {}
    for name in INPUTS:
        a = np.ascontiguousarray(inputs[name])
        arrays[f"in_{name}"] = a
        aps[name] = nc.dram_tensor(f"in_{name}", a.shape, mybir.dt.from_np(a.dtype), kind="ExternalInput").ap()
    out = nc.dram_tensor("out", (1, T, D), F32, kind="ExternalOutput").ap()
    build(nc, views(aps), out.squeeze(0))
    result = run_bass_kernel_spmd(nc, [arrays], core_ids=[0])
    return result.results[0]["out"]
```
